# Optimizing a Trainium2 kernel written in Bass

```python
import numpy as np
import jax
import jax.numpy as jnp
from jax import lax

D_MODEL = 1024
BATCH = 1
SEQ = 256
DEPTH = 1
DEC_BATCH = 1
DEC_SEQ = 32
PAST_LEN = 512

CHUNK = 64
MIX_WIDTH = D_MODEL
GLA_HEADS = 4
GLA_VALUE_WIDTH = MIX_WIDTH // 2
GLA_KEY_WIDTH = GLA_VALUE_WIDTH // 2
GLA_HEAD_K = GLA_KEY_WIDTH // GLA_HEADS
GLA_HEAD_V = GLA_VALUE_WIDTH // GLA_HEADS
GLA_LOW_RANK = 16
GLA_GATE_NORMALIZER = 16.0
FOX_WIDTH = MIX_WIDTH - GLA_VALUE_WIDTH
FOX_HEAD_DIM = 64
FOX_HEADS = FOX_WIDTH // FOX_HEAD_DIM
FOX_Q_BLOCK = 128
IN_WIDTH = 2 * GLA_KEY_WIDTH + 2 * GLA_VALUE_WIDTH + GLA_LOW_RANK + 3 * FOX_WIDTH + FOX_HEADS
N_EXPERTS = 64
N_GROUPS = 8
TOPK_GROUPS = 4
TOP_K = 8
D_EXPERT = 256
D_SHARED = 256
ROUTED_SCALE = 2.5
EXPERT_BLOCK = 256
NORM_EPS = 1e-6

kernel_name = 'gla_fox_moe_adaln_stream_step'

def rms_norm(x, g):
    xf = x.astype(jnp.float32)
    y = xf * lax.rsqrt(jnp.mean(xf * xf, axis=-1, keepdims=True) + NORM_EPS)
    return (y * g.astype(jnp.float32)).astype(x.dtype)

def ada_modulation(c, w_ada, b_ada):
    m = (jax.nn.silu(c) @ w_ada + b_ada)[:, None, :]
    return jnp.split(m, 6, axis=-1)

def gla_chunked(q, k, v, log_a, s0, block):
    bsz, length, heads, dk = q.shape
    n_blocks = length // block

    def to_blocks(t):
        t = t.astype(jnp.float32).reshape(bsz, n_blocks, block, heads, t.shape[-1])
        return t.transpose(1, 0, 3, 2, 4)

    qb = to_blocks(q) * (dk ** -0.5)
    kb, vb, gb = to_blocks(k), to_blocks(v), to_blocks(log_a)
    causal = jnp.tril(jnp.ones((block, block), dtype=bool))
    mid = block // 2

    def step(s, xs):
        qc, kc, vc, gc = xs
        b = jnp.cumsum(gc, axis=-2)
        ref = b[..., mid:mid + 1, :]
        b_last = b[..., -1:, :]
        a = jnp.einsum('bhtk,bhsk->bhts', qc * jnp.exp(b - ref), kc * jnp.exp(ref - b))
        a = jnp.where(causal, a, 0.0)
        o = (jnp.einsum('bhtk,bhkv->bhtv', qc * jnp.exp(b), s)
             + jnp.einsum('bhts,bhsv->bhtv', a, vc))
        s_new = (s * jnp.swapaxes(jnp.exp(b_last), -1, -2)
                 + jnp.einsum('bhsk,bhsv->bhkv', kc * jnp.exp(b_last - b), vc))
        return s_new, o

    s_final, o = lax.scan(step, s0.astype(jnp.float32), (qb, kb, vb, gb))
    o = o.transpose(1, 0, 3, 2, 4).reshape(bsz, length, heads, v.shape[-1])
    return o, s_final

def fox_attention(q, cq, qpos, k, v, ck, kpos):
    bsz, lq, heads, d = q.shape
    qb = FOX_Q_BLOCK if lq % FOX_Q_BLOCK == 0 else lq
    n = lq // qb
    q_blocks = q.reshape(bsz, n, qb, heads, d).swapaxes(0, 1)
    c_blocks = cq.reshape(bsz, n, qb, heads).swapaxes(0, 1)
    p_blocks = qpos.reshape(n, qb)
    ck_t = ck.transpose(0, 2, 1)
    scale = d ** -0.5

    def one(args):
        qi, ci, pi = args
        s = jnp.einsum('bqhd,bkhd->bhqk', qi, k).astype(jnp.float32) * scale
        s = s + ci.transpose(0, 2, 1)[..., None] - ck_t[:, :, None, :]
        s = jnp.where(kpos[None, :] <= pi[:, None], s, -jnp.inf)
        p = jax.nn.softmax(s, axis=-1)
        return jnp.einsum('bhqk,bkhd->bqhd', p.astype(v.dtype), v)

    o = lax.map(one, (q_blocks, c_blocks, p_blocks))
    return o.swapaxes(0, 1).reshape(bsz, lq, heads, d)

def token_mixer(h, gla_s0, fox_past, pos0, gla_block, w_in, w_gla_gk2, b_gla_gk, g_gla_out,
                b_fox_f, g_fox_out, w_out):
    bsz, length, _ = h.shape
    z = h @ w_in
    sizes = [GLA_KEY_WIDTH, GLA_KEY_WIDTH, GLA_VALUE_WIDTH, GLA_VALUE_WIDTH, GLA_LOW_RANK,
             FOX_WIDTH, FOX_WIDTH, FOX_WIDTH, FOX_HEADS]
    splits = [int(i) for i in np.cumsum(sizes)[:-1]]
    gq, gk, gv, gg, glr, fq, fk, fv, ff = jnp.split(z, splits, axis=-1)

    def heads(t, nh):
        return t.reshape(bsz, length, nh, t.shape[-1] // nh)

    log_a = jax.nn.log_sigmoid((glr @ w_gla_gk2 + b_gla_gk).astype(jnp.float32)) / GLA_GATE_NORMALIZER
    o_gla, s_new = gla_chunked(heads(gq, GLA_HEADS), heads(gk, GLA_HEADS), heads(gv, GLA_HEADS),
                               heads(log_a, GLA_HEADS), gla_s0, gla_block)
    o_gla = rms_norm(o_gla.astype(h.dtype), g_gla_out) * jax.nn.silu(heads(gg, GLA_HEADS))

    q, k, v = heads(fq, FOX_HEADS), heads(fk, FOX_HEADS), heads(fv, FOX_HEADS)
    logf = jax.nn.log_sigmoid((ff + b_fox_f).astype(jnp.float32))
    c_new = jnp.cumsum(logf, axis=1)
    qpos = pos0 + jnp.arange(length)
    if fox_past is None:
        k_all, v_all, ck, kpos = k, v, c_new, qpos
    else:
        k_past, v_past, logf_past = fox_past
        logf_past = logf_past.astype(jnp.float32)
        suffix = lax.cumsum(logf_past, axis=1, reverse=True) - logf_past
        k_all = jnp.concatenate([k_past.astype(k.dtype), k], axis=1)
        v_all = jnp.concatenate([v_past.astype(v.dtype), v], axis=1)
        ck = jnp.concatenate([-suffix, c_new], axis=1)
        kpos = jnp.arange(k_all.shape[1])
    o_fox = fox_attention(q, c_new, qpos, k_all, v_all, ck, kpos)
    o_fox = rms_norm(o_fox.reshape(bsz, length, FOX_WIDTH), g_fox_out)

    merged = jnp.concatenate([o_gla.reshape(bsz, length, GLA_VALUE_WIDTH), o_fox], axis=-1)
    return merged @ w_out, s_new, k, v, logf

def route(t, w_router, b_router):
    n_tok = t.shape[0]
    scores = jax.nn.sigmoid((t @ w_router).astype(jnp.float32))
    choice = scores + b_router.astype(jnp.float32)
    grp = choice.reshape(n_tok, N_GROUPS, N_EXPERTS // N_GROUPS)
    grp_score = lax.top_k(grp, 2)[0].sum(-1)
    _, top_g = lax.top_k(grp_score, TOPK_GROUPS)
    gmask = jax.nn.one_hot(top_g, N_GROUPS, dtype=jnp.float32).sum(1) > 0
    emask = jnp.repeat(gmask, N_EXPERTS // N_GROUPS, axis=1)
    _, idx = lax.top_k(jnp.where(emask, choice, -jnp.inf), TOP_K)
    w = jnp.take_along_axis(scores, idx, axis=1)
    w = w / (w.sum(-1, keepdims=True) + 1e-20) * ROUTED_SCALE
    return idx, w

def routed_experts(t, idx, wts, w_gate, w_up, w_down):
    n_tok = t.shape[0]
    n = n_tok * TOP_K
    flat_e = idx.reshape(n)
    flat_t = jnp.repeat(jnp.arange(n_tok, dtype=jnp.int32), TOP_K)
    flat_w = wts.reshape(n)
    order = jnp.argsort(flat_e)
    e_sorted = flat_e[order]
    counts = jnp.bincount(flat_e, length=N_EXPERTS)
    padded = (counts + EXPERT_BLOCK - 1) // EXPERT_BLOCK * EXPERT_BLOCK
    pad_end = jnp.cumsum(padded)
    pad_start = pad_end - padded
    start = jnp.cumsum(counts) - counts
    dest = pad_start[e_sorted] + jnp.arange(n) - start[e_sorted]
    n_blocks = -(-n // EXPERT_BLOCK) + N_EXPERTS
    rows = n_blocks * EXPERT_BLOCK
    row_tok = jnp.zeros((rows,), jnp.int32).at[dest].set(flat_t[order])
    row_w = jnp.zeros((rows,), jnp.float32).at[dest].set(flat_w[order])
    blk_e = jnp.minimum(jnp.searchsorted(pad_end, jnp.arange(n_blocks) * EXPERT_BLOCK, side='right'),
                        N_EXPERTS - 1)

    def block(acc, xs):
        tok, w, e = xs
        xb = t[tok]
        yb = (jax.nn.silu(xb @ w_gate[e]) * (xb @ w_up[e])) @ w_down[e]
        return acc.at[tok].add((yb * w[:, None]).astype(acc.dtype)), None

    acc, _ = lax.scan(block, jnp.zeros_like(t),
                      (row_tok.reshape(n_blocks, EXPERT_BLOCK), row_w.reshape(n_blocks, EXPERT_BLOCK), blk_e))
    return acc

def moe(h, w_router, b_router, w_exp_gate, w_exp_up, w_exp_down, w_sh_gate, w_sh_up, w_sh_down):
    bsz, length, d = h.shape
    t = h.reshape(bsz * length, d)
    idx, wts = route(t, w_router, b_router)
    routed = routed_experts(t, idx, wts, w_exp_gate, w_exp_up, w_exp_down)
    shared = (jax.nn.silu(t @ w_sh_gate) * (t @ w_sh_up)) @ w_sh_down
    return (routed + shared).reshape(bsz, length, d)

def trunk_layer(x, c, gla_s0, fox_past, pos0, gla_block, lw):
    (w_ada, b_ada, g_mix, g_ffn, w_in, w_gk2, b_gk, g_gla, b_f, g_fox, w_out,
     w_r, b_r, w_eg, w_eu, w_ed, w_sg, w_su, w_sd) = lw
    sh1, sc1, gt1, sh2, sc2, gt2 = ada_modulation(c, w_ada, b_ada)
    h = rms_norm(x, g_mix) * (1.0 + sc1) + sh1
    mix, s_new, k, v, logf = token_mixer(h, gla_s0, fox_past, pos0, gla_block, w_in, w_gk2, b_gk,
                                         g_gla, b_f, g_fox, w_out)
    x = x + gt1 * mix
    h = rms_norm(x, g_ffn) * (1.0 + sc2) + sh2
    x = x + gt2 * moe(h, w_r, b_r, w_eg, w_eu, w_ed, w_sg, w_su, w_sd)
    return x, s_new, k, v, logf

def setup_inputs(seed: int = 0) -> dict:
    key = jax.random.key(seed)
    ks = jax.random.split(key, 32)

    def nrm(k, shape, s):
        return jax.random.normal(k, shape, jnp.float32) * s

    nl, d = DEPTH, D_MODEL
    return {
        'x_prompt': nrm(ks[0], (BATCH, SEQ, d), 1.0),
        'x_sample': nrm(ks[1], (DEC_BATCH, DEC_SEQ, d), 1.0),
        'state_gla': nrm(ks[2], (nl, DEC_BATCH, GLA_HEADS, GLA_HEAD_K, GLA_HEAD_V), 1.0),
        'cache_fox_k': nrm(ks[3], (nl, DEC_BATCH, PAST_LEN, FOX_HEADS, FOX_HEAD_DIM), 1.0),
        'cache_fox_v': nrm(ks[4], (nl, DEC_BATCH, PAST_LEN, FOX_HEADS, FOX_HEAD_DIM), 1.0),
        'cache_fox_logf': jax.nn.log_sigmoid(3.0 + nrm(ks[5], (nl, DEC_BATCH, PAST_LEN, FOX_HEADS), 1.0)),
        'c_prompt': nrm(ks[6], (BATCH, d), 1.0),
        'c_sample': nrm(ks[7], (DEC_BATCH, d), 1.0),
        'w_ada': nrm(ks[8], (nl, d, 6 * d), 0.5 * d ** -0.5),
        'b_ada': nrm(ks[9], (nl, 6 * d), 0.02),
        'g_norm_mix': 1.0 + nrm(ks[10], (nl, d), 0.05),
        'g_norm_ffn': 1.0 + nrm(ks[11], (nl, d), 0.05),
        'w_in': nrm(ks[12], (nl, d, IN_WIDTH), d ** -0.5),
        'w_gla_gk2': nrm(ks[13], (nl, GLA_LOW_RANK, GLA_KEY_WIDTH), GLA_LOW_RANK ** -0.5),
        'b_gla_gk': nrm(ks[14], (nl, GLA_KEY_WIDTH), 0.02),
        'g_gla_out': 1.0 + nrm(ks[15], (nl, GLA_HEAD_V), 0.05),
        'b_fox_f': jax.random.uniform(ks[16], (nl, FOX_HEADS), jnp.float32, 1.0, 5.0),
        'g_fox_out': 1.0 + nrm(ks[17], (nl, FOX_WIDTH), 0.05),
        'w_out': nrm(ks[18], (nl, MIX_WIDTH, d), MIX_WIDTH ** -0.5),
        'w_router': nrm(ks[19], (nl, d, N_EXPERTS), d ** -0.5),
        'b_router': nrm(ks[20], (nl, N_EXPERTS), 0.01),
        'w_exp_gate': nrm(ks[21], (nl, N_EXPERTS, d, D_EXPERT), d ** -0.5),
        'w_exp_up': nrm(ks[22], (nl, N_EXPERTS, d, D_EXPERT), d ** -0.5),
        'w_exp_down': nrm(ks[23], (nl, N_EXPERTS, D_EXPERT, d), D_EXPERT ** -0.5),
        'w_sh_gate': nrm(ks[24], (nl, d, D_SHARED), d ** -0.5),
        'w_sh_up': nrm(ks[25], (nl, d, D_SHARED), d ** -0.5),
        'w_sh_down': nrm(ks[26], (nl, D_SHARED, d), D_SHARED ** -0.5),
        'g_final': 1.0 + nrm(ks[27], (d,), 0.05),
    }

def reference(x_prompt, x_sample, state_gla, cache_fox_k, cache_fox_v, cache_fox_logf, c_prompt, c_sample,
              w_ada, b_ada, g_norm_mix, g_norm_ffn, w_in, w_gla_gk2, b_gla_gk, g_gla_out, b_fox_f, g_fox_out,
              w_out, w_router, b_router, w_exp_gate, w_exp_up, w_exp_down, w_sh_gate, w_sh_up, w_sh_down,
              g_final):
    xp, xs = x_prompt, x_sample
    gla_p, gla_s, kp_l, vp_l, fp_l, ks_l, vs_l, fs_l = [], [], [], [], [], [], [], []
    for l in range(DEPTH):
        lw = (w_ada[l], b_ada[l], g_norm_mix[l], g_norm_ffn[l], w_in[l], w_gla_gk2[l], b_gla_gk[l],
              g_gla_out[l], b_fox_f[l], g_fox_out[l], w_out[l], w_router[l], b_router[l],
              w_exp_gate[l], w_exp_up[l], w_exp_down[l], w_sh_gate[l], w_sh_up[l], w_sh_down[l])
        s0 = jnp.zeros((xp.shape[0], GLA_HEADS, GLA_HEAD_K, GLA_HEAD_V), jnp.float32)
        xp, sp, kp, vp, fp = trunk_layer(xp, c_prompt, s0, None, 0, CHUNK, lw)
        xs, ss, k_s, v_s, f_s = trunk_layer(xs, c_sample, state_gla[l],
                                            (cache_fox_k[l], cache_fox_v[l], cache_fox_logf[l]),
                                            cache_fox_k.shape[2], xs.shape[1], lw)
        gla_p.append(sp)
        gla_s.append(ss)
        kp_l.append(kp)
        vp_l.append(vp)
        fp_l.append(fp)
        ks_l.append(k_s)
        vs_l.append(v_s)
        fs_l.append(f_s)
    y_prompt = rms_norm(xp, g_final)
    y_sample = rms_norm(xs, g_final)
    return (y_prompt, y_sample, jnp.stack(gla_p), jnp.stack(gla_s), jnp.stack(kp_l), jnp.stack(vp_l),
            jnp.stack(fp_l), jnp.stack(ks_l), jnp.stack(vs_l), jnp.stack(fs_l))


_drawn_inputs = setup_inputs


def setup_inputs(seed=0):
    import zlib

    import numpy as np

    out = dict(_drawn_inputs(seed))
    spreads = {}
    factors = {'cache_fox_logf': 2.96, 'b_gla_gk': 4.904, 'g_gla_out': 2.952, 'g_fox_out': 3.51}
    for name, (base, spread) in spreads.items():
        noise = np.random.default_rng([zlib.crc32(name.encode()), seed]).standard_normal(out[name].shape)
        drawn = base * np.exp(spread * noise) if base else spread * noise
        out[name] = jnp.asarray(drawn.astype(out[name].dtype))
    for name, factor in factors.items():
        out[name] = (out[name] * factor).astype(out[name].dtype)
    return out
```

```python
from contextlib import ExitStack

import concourse.bass as bass
from concourse import mybir

ALU = mybir.AluOpType
ACT = mybir.ActivationFunctionType
AX = mybir.AxisListType.X
F32 = mybir.dt.float32
BF16 = mybir.dt.bfloat16
I32 = mybir.dt.int32

P = 128
D = 1024
KC = D // P
NP_, NS_ = 256, 32
N = NP_ + NS_
TN = [128, 128, 32]
T0 = [0, 128, 256]
PAST = 512
GH, GK, GV = 4, 64, 128
FH, FD = 8, 64
LR = 16
E, DE = 64, 256
NG, TOPG, TOPK = 8, 4, 8
RSCALE = 2.5
EPS = 1e-6
NEG = -1e30
BLK = 64
C_GQ, C_GK, C_GV, C_GG, C_LR, C_FQ, C_FK, C_FV, C_FF = 0, 256, 512, 1024, 1536, 1552, 2064, 2576, 3088
SLOT = 2048


def layer(nc, x_prompt, x_sample, state_gla, cache_fox_k, cache_fox_v, cache_fox_logf, c_prompt, c_sample,
          w_ada, b_ada, g_norm_mix, g_norm_ffn, w_in, w_gla_gk2, b_gla_gk, g_gla_out, b_fox_f, g_fox_out,
          w_out, w_router, b_router, w_exp_gate, w_exp_up, w_exp_down, w_sh_gate, w_sh_up, w_sh_down, g_final,
          y_prompt, y_sample, st_prompt, st_sample, k_prompt, v_prompt, f_prompt, k_sample, v_sample, f_sample):
    ctx = ExitStack()

    place = {"at": nc.sbuf_base + (-nc.sbuf_base) % 64}

    def sb_at(name, shape, dt, at):
        return nc.alloc_sbuf_tensor_at(name, shape, dt, offset=at)

    def sb(name, shape, dt=F32):
        size = 2 if dt == BF16 else 4
        for s in shape[1:]:
            size *= s
        at = place["at"]
        place["at"] = at + size + (-size) % 64
        return sb_at(name, shape, dt, at)

    ident = sb("ident", [P, P])
    ones = sb("ones", [P, P])
    upper = sb("upper", [P, P])
    lower = sb("lower", [P, P])
    glamask = sb("glamask", [P, BLK])
    identb = sb("identb", [P, P], BF16)
    causal = sb("causal", [P, P], BF16)
    epst = sb("epst", [P, 1])
    g_mix = sb("g_mix", [P, KC])
    g_ffn = sb("g_ffn", [P, KC])
    g_fin = sb("g_fin", [P, KC])
    b_adaT = sb("b_adaT", [P, 6, KC])
    adaT = sb("adaT", [P, 6, 2, KC])
    gain1 = sb("gain1", [P, 2, KC])
    gain2 = sb("gain2", [P, 2, KC])
    g_gla = sb("g_gla", [P, 1])
    g_fox = sb("g_fox", [P, 4])
    b_gk = sb("b_gk", [P, 2])
    b_ff = sb("b_ff", [P, FH])
    b_rt = sb("b_rt", [P, E])
    w_gk2 = sb("w_gk2", [LR, 256])
    w_rt = sb("w_rt", [P, KC, E])
    w_lf = sb("w_lf", [P, KC, LR + FH])
    cT = sb("cT", [P, 2, KC])
    scT = sb("scT", [P, KC, 2])
    xT = sb("xT", [P, KC, N])
    rstdB = sb("rstdB", [P, N])
    hT = sb("hT", [P, KC, N])
    base = place["at"]
    RING = base
    NSLOT = 12
    FRONT = 6
    ring = [sb_at(f"ring{i}", [P, SLOT], F32, RING + 8192 * i) for i in range(NSLOT)]
    pair = [sb_at(f"pair{i}", [P, 2 * SLOT], F32, RING + 16384 * i) for i in range(FRONT // 2)]
    place["at"] = RING + 8192 * FRONT
    gqk = sb("gqk", [P, 4, N])
    zt = sb("zt", [P, 16, N])
    o_tok = sb_at("o_tok", [P, 3, D], F32, place["at"] - 4 * 16 * N)
    prob = [sb_at(f"prob{i}", [P, PAST + NS_], F32, place["at"] - 4 * 16 * N + 12288 + 2176 * i) for i in range(2)]
    toks = sb("toks", [P, 4, 3, 512])
    qA = sb("qA", [FD + 2, FH, N])
    kA = sb("kA", [FD + 2, FH, N])
    x_tok = sb_at("x_tok", [P, 3, D], F32, place["at"])
    kS = sb("kS", [FD + 2, FH, PAST])
    cacheK = sb("cacheK", [P, 4, 512])
    probT = [sb_at(f"probT{i}", [P, 256], F32, place["at"] - 8192 + 1024 * i) for i in range(2)]
    cacheV = sb("cacheV", [P, 4, 512])
    sq = sb_at("sq", [P, KC, N], F32, place["at"])
    xn = sb_at("xn", [P, KC, N], F32, place["at"] + 9216)
    g_t = sb("g_t", [P, 2, N])
    kl_tok = sb_at("kl_tok", [P, 3, 256], F32, place["at"])
    g_a = sb("g_a", [P, 2, N])
    g_b = sb("g_b", [P, 2, N])
    g_c = sb("g_c", [P, 2, N])
    qe = sb("qe", [P, 2, N])
    ke = sb("ke", [P, 2, N])
    qb = sb("qb", [P, 2, N])
    kl = sb("kl", [P, 2, N])
    a_t = sb("a_t", [P, 2, 3, 2, BLK])
    states = sb("states", [P, 6, 2, GV])
    dec = sb("dec", [P, 2, 5])
    logf = sb("logf", [P, 3, FH])
    lf_t = sb("lf_t", [P, 3, FH])
    lf_m = sb("lf_m", [P, 3, FH])
    pastf = sb("pastf", [P, 4, FH])
    crow = sb("crow", [FH, 2, N])
    srow = sb("srow", [FH, PAST])
    glr = sb("glr", [LR, N])
    nmax = sb("nmax", [P, 24])
    rsum = sb("rsum", [P, 24])
    rinv = sb("rinv", [P, 24])
    ssq5 = sb("ssq5", [P, 3, 5])
    rs5 = sb("rs5", [P, 3, 5])
    mT = hT
    ada_row = sb("ada_row", [P, 512])
    junk = ada_row
    assert place["at"] <= nc.sbuf_usable_end, (place["at"], nc.sbuf_usable_end)

    place["at"] = RING + 8192 * NSLOT
    acc = sb("acc", [P, KC, N])
    h2T = sb("h2T", [P, KC, N])
    actT = sb("actT", [P, 2, N])
    sil = sb("sil", [P, 2, N])
    wT = sb("wT", [E, N])
    wm = sb("wm", [E, N])
    sc = sb("sc", [P, 3, E])
    ch = sb("ch", [P, 3, E])
    top = sb("top", [P, NG, 8])
    gs = sb("gs", [P, NG])
    t8 = sb("t8", [P, 8])
    r_a = sb("r_a", [P, E])
    r_b = sb("r_b", [P, E])
    r_c = sb("r_c", [P, E])
    r_n = sb("r_n", [P, 1])
    wrt = sb("wrt", [P, 3, E])
    yout = sb("yout", [P, 3, D])
    sq2 = sb("sq2", [P, KC, N])
    assert place["at"] <= nc.sbuf_usable_end, (place["at"], nc.sbuf_usable_end)

    psum = nc.alloc_psum_tensor("psum", [P, 8 * 512], F32)
    bank = [psum[:, 512 * i:512 * i + 512] for i in range(8)]

    ada_d = nc.dram_tensor("ada_d", [2, 6, D], F32, kind="Internal").ap()
    crow_d = nc.dram_tensor("crow_d", [2, FH, N], F32, kind="Internal").ap()
    srow_d = nc.dram_tensor("srow_d", [FH, PAST], F32, kind="Internal").ap()

    def sem(name):
        return ctx.enter_context(nc.semaphore(name))

    s = {n: sem(n) for n in (
        "x_in c_in small_in cache_in state_in consts zeros xT_ps xT_ok sq_ok ssq_ps rstd_ok rinv_ok xn_ok sc_ok ada_ps ada_row ada_out adaT_in "
        "gain_ok hT_ok z_ps z_act z_dve narrow_ps glr_ok ff_ok lf_abs lf_ln logf_ok f_out crow_ps crow_ok crow_out rows_in ones_ok "
        "tok_ps tok_act tok_dve kv_out cK_ps cK_act cK_dve gate_ps gate_x gate_abs gate_ln cum_ok gexp_ok gprod_ok klT_ps klT_ok aT_ps aT_ok "
        "upd_ps state_ok st_out go_ps go_ok sc_ps max_ok exp_ok pT_ps pT_ok po_ps po_ok ssq_act rs_act on_ok mT_ps mT_act mT_dve "
        "mix_ps x1_ok d_chain a_chain w_used x2_sq h2n_ok h2_ok rt_ps rt_sc wrt_ok wT_ps wT_ok wm_ok gu_ps sil_ok su_ok act_ok "
        "dn_ps dn_ok fin_ok y_ps y_ok out_done").split()}
    ring_in = [sem(f"ring_in{i}") for i in range(NSLOT)]

    wa = w_ada[0].rearrange("(p k) n -> p k n", k=KC)
    wi = w_in[0].rearrange("(p k) n -> p k n", k=KC)
    wo = w_out[0].rearrange("(j p) n -> p j n", p=P)
    GROUPS = [C_GQ, C_GV, C_GG, C_FQ, C_FK, C_FV]
    pieces = []
    for k in range(KC):
        pieces.append((wa[:, k, 0:2048], 1))
    for c in GROUPS:
        pieces.append((wi[:, :, c:c + 512], 2))
    for r in (1, 2):
        for k in range(KC):
            pieces.append((wa[:, k, 2048 * r:2048 * r + 2048], 1))
    for j in range(0, 8, 4):
        pieces.append((wo[:, j:j + 4, :], 2))
    at, slots_of, loads, owner, waits_of, turn = 0, [], [0] * NSLOT, {}, [], []
    for n, (_, w) in enumerate(pieces):
        assert w == 1 or at % 2 == 0
        sl = [(at + i) % FRONT for i in range(w)]
        at += w
        waits_of.append(max([owner[q] for q in sl if q in owner], default=-1))
        for q in sl:
            owner[q] = n
        slots_of.append(sl)
        loads[sl[0]] += 1
        turn.append(loads[sl[0]])
    FIRST_WIN, FIRST_R1, FIRST_WO = KC, KC + 6, KC + 6 + 2 * KC
    NPIECE = len(pieces)

    def piece_in(eng, n):
        eng.wait_ge(ring_in[slots_of[n][0]], 16 * turn[n])

    def piece(n):
        return ring[slots_of[n][0]] if pieces[n][1] == 1 else pair[slots_of[n][0] // 2]

    SHARED = 6
    loads[SHARED] += 1
    loads[SHARED + 1] += 1
    loads[SHARED + 2] += 1
    PER = 4

    block = ctx.enter_context(nc.Block())
    small = [
        (g_mix[:, :], g_norm_mix[0].rearrange("(p k) -> p k", k=KC)),
        (g_ffn[:, :], g_norm_ffn[0].rearrange("(p k) -> p k", k=KC)),
        (g_fin[:, :], g_final.rearrange("(p k) -> p k", k=KC)),
        (b_adaT[:, :, :], b_ada[0].rearrange("(m p k) -> p m k", m=6, k=KC)),
        (g_gla[:, :], g_gla_out[0].rearrange("(p o) -> p o", o=1)),
        (g_fox[:, :], g_fox_out[0].rearrange("(j p) -> p j", p=P)),
        (b_gk[:, :], b_gla_gk[0].rearrange("(j p) -> p j", p=P)),
        (b_ff[:, :], b_fox_f[0].partition_broadcast(P)),
        (b_rt[:, :], b_router[0].partition_broadcast(P)),
        (w_gk2[:, :], w_gla_gk2[0]),
        (w_rt[:, :, :], w_router[0].rearrange("(p k) n -> p k n", k=KC)),
        (w_lf[:, :, 0:LR], wi[:, :, C_LR:C_LR + LR]),
        (w_lf[:, :, LR:], wi[:, :, C_FF:C_FF + FH]),
    ]
    SMALL = 16 * len(small)
    NKEY = (128, 256, PAST + NS_)

    def score(u):
        b = 4 + 2 * (u % 2)
        return psum[:, 512 * b:512 * b + 1024]

    def divide(dve, i, link):
        n = TN[i]
        dve.wait_ge(s["po_ps"], 8 * i + 8)
        link(dve.reciprocal(rinv[0:n, 8 * i:8 * i + 8], rsum[0:n, 8 * i:8 * i + 8]))
        dve.tensor_tensor(o_tok[0:n, i, 512:1024].rearrange("t (h d) -> t h d", h=FH),
                          bank[2 + i % 2][0:n, :].rearrange("t (h d) -> t h d", h=FH),
                          rinv[0:n, 8 * i:8 * i + 8].unsqueeze(2).broadcast_to([n, FH, FD]), ALU.mult).then_inc(s["po_ok"], 1)

    def update(b, c):
        w = 2 * (b // 2) % 4 + c
        return bank[2 if b == 4 else b % 2][:, GV * w:GV * w + GV]

    def inter(i, q):
        if i == 2:
            return bank[q][:, 0:256]
        return bank[6 + q][:, 256 * i:256 * i + 256]

    def silu_gate(i):
        return toks[0:TN[i], 1, i, :]

    @block.sync
    def _(sp):
        for i, (src, tn) in enumerate(((x_prompt[0, 0:128], 128), (x_prompt[0, 128:256], 128), (x_sample[0], 32))):
            sp.dma_start(x_tok[0:tn, i, :], src).then_inc(s["x_in"], 16)
        for n, (src, w) in enumerate(pieces):
            if waits_of[n] >= 0:
                sp.wait_ge(s["w_used"], waits_of[n] + 1)
            dst = piece(n)[:, :]
            if w == 2:
                dst = dst.rearrange("p (k n) -> p k n", n=src.shape[2])
            sp.dma_start(dst, src).then_inc(ring_in[slots_of[n][0]], 16)
        sp.wait_ge(s["x1_ok"], KC)
        sp.wait_ge(s["kv_out"], 96)
        sp.wait_ge(s["st_out"], 64)
        sp.wait_ge(s["f_out"], 32)
        for q, w, k in ((0, w_sh_gate, KC), (1, w_sh_up, KC), (2, w_sh_down, 2)):
            sp.dma_start(ring[SHARED + q][:, :], w[0].rearrange("(p k) n -> p (k n)", k=k)).then_inc(ring_in[SHARED + q], 16)

        def expert(u, e):
            for q, w, k in ((0, w_exp_gate, KC), (1, w_exp_up, KC), (2, w_exp_down, 2)):
                src = w[0].rearrange("e (p k) n -> e p (k n)", k=k)[bass.ds(e, 1)].rearrange("e p n -> (e p) n")
                sp.dma_start(ring[3 * u + q][:, :], src).then_inc(ring_in[3 * u + q], 16)

        for u in range(PER):
            sp.wait_ge(s["w_used"], NPIECE + (1 if u == 2 else 0))
            expert(u, u)
        with sp.Fori(1, E // PER) as it:
            for u in range(PER):
                sp.wait_ge(s["w_used"], sp.snap(it * PER + (NPIECE + 1 + u + 1 - PER)))
                expert(u, sp.snap(it * PER + u))

    @block.scalar
    def _(act):
        act.dma_start(cT[:, 0, :], c_prompt[0].rearrange("(p k) -> p k", k=KC)).then_inc(s["c_in"], 16)
        act.dma_start(cT[:, 1, :], c_sample[0].rearrange("(p k) -> p k", k=KC)).then_inc(s["c_in"], 16)
        with nc.allow_non_contiguous_dma(reason="vectors of a few hundred elements"):
            for dst, src in small:
                act.dma_start(dst, src).then_inc(s["small_in"], 16)
        act.dma_start(cacheK[:, :, :], cache_fox_k[0, 0].rearrange("(j p) h d -> p j (h d)", p=P)).then_inc(s["cache_in"], 16)
        act.dma_start(cacheV[:, :, :], cache_fox_v[0, 0].rearrange("(j p) h d -> p j (h d)", p=P)).then_inc(s["cache_in"], 16)
        act.dma_start(pastf[:, :, :], cache_fox_logf[0, 0].rearrange("(j p) h -> p j h", p=P)).then_inc(s["cache_in"], 16)
        for c in range(2):
            act.dma_start(states[:, 4, c, :], state_gla[0, 0, 2 * c:2 * c + 2].rearrange("h k v -> (h k) v")).then_inc(s["state_in"], 16)
        act.wait_ge(s["c_in"], 32)
        act.activation(scT[:, :, :].rearrange("p k g -> p g k"), cT[:, :, :], ACT.Silu).then_inc(s["sc_ok"], 1)
        for k in range(KC):
            act.wait_ge(s["xT_ok"], k + 1)
            act.activation(sq[:, k, :], xT[:, k, :], ACT.Square).then_inc(s["sq_ok"], 1)
        act.wait_ge(s["consts"], 1)
        act.wait_ge(s["ssq_ps"], 1)
        act.activation(rstdB[:, :], bank[6][:, 0:N], ACT.Sqrt, bias=epst[:, 0:1], scale=1.0 / D).then_inc(s["rstd_ok"], 1)

        def ada_rows(r):
            act.wait_ge(s["ada_ps"], r + 1)
            if r:
                act.wait_ge(s["ada_out"], 64 * r)
            for j in range(4):
                act.copy(ada_row[32 * j:32 * j + 2, :], bank[5][32 * j:32 * j + 2, :]).then_inc(s["ada_row"], 1)
            act.wait_ge(s["ada_row"], 4 * r + 4)
            for j in range(4):
                g = 4 * r + j
                act.dma_start(ada_d[:, g // 2, 512 * (g % 2):512 * (g % 2) + 512],
                              ada_row[32 * j:32 * j + 2, :]).then_inc(s["ada_out"], 16)
            act.wait_ge(s["ada_out"], 64 * (r + 1))
            for m in (2 * r, 2 * r + 1):
                act.dma_start(adaT[:, m, :, :], ada_d[:, m].rearrange("g (p k) -> p g k", k=KC)).then_inc(s["adaT_in"], 16)

        ada_rows(0)
        act.wait_ge(s["gain_ok"], 2)
        act.wait_ge(s["xn_ok"], 1)
        for k in range(KC):
            act.activation(hT[:, k, 0:NP_], xn[:, k, 0:NP_], ACT.Identity, bias=adaT[:, 0, 0, k:k + 1],
                           scale=gain1[:, 0, k:k + 1]).then_inc(s["hT_ok"], 1)
        for c in range(1, 24, 2):
            act.wait_ge(s["z_ps"], c + 1)
            b = bank[c % 4]
            if c < 2:
                last = act.mul(gqk[:, c, :], b[:, 0:N], GK ** -0.5)
            elif c < 4:
                last = act.copy(gqk[:, c, :], b[:, 0:N])
            elif 12 <= c < 16:
                act.mul(qA[0:FD, 2 * (c - 12), :], b[0:FD, 0:N], FD ** -0.5)
                last = act.mul(qA[0:FD, 2 * (c - 12) + 1, :], b[FD:P, 0:N], FD ** -0.5)
            elif 16 <= c < 20:
                act.copy(kA[0:FD, 2 * (c - 16), :], b[0:FD, 0:N])
                act.copy(kA[0:FD, 2 * (c - 16) + 1, :], b[FD:P, 0:N])
                last = act.copy(zt[:, 8 + c - 16, :], b[:, 0:N])
            else:
                last = act.copy(zt[:, c - 4 if c < 12 else c - 8, :], b[:, 0:N])
            last.then_inc(s["z_act"], 1)
        act.wait_ge(s["narrow_ps"], 1)
        act.copy(glr[:, :], bank[4][0:LR, 0:N]).then_inc(s["glr_ok"], 1)
        act.wait_ge(s["lf_abs"], 1)
        act.activation(logf[:, :, :], lf_t[:, :, :], ACT.Exp, scale=-1.0).then_inc(s["a_chain"], 1)
        act.wait_ge(s["a_chain"], 1)
        act.activation(lf_t[:, :, :], logf[:, :, :], ACT.Ln, bias=1.0).then_inc(s["lf_ln"], 1)
        act.wait_ge(s["gate_abs"], 1)
        act.activation(g_c[:, :, :], g_a[:, :, :], ACT.Exp, scale=-1.0).then_inc(s["a_chain"], 1)
        act.wait_ge(s["a_chain"], 2)
        act.activation(g_a[:, :, :], g_c[:, :, :], ACT.Ln, bias=1.0).then_inc(s["gate_ln"], 1)
        act.wait_ge(s["cum_ok"], 4)
        act.activation(qe[:, :, :], g_a[:, :, :], ACT.Exp).then_inc(s["gexp_ok"], 1)
        act.activation(ke[:, :, :], g_a[:, :, :], ACT.Exp, scale=-1.0).then_inc(s["gexp_ok"], 1)
        act.activation(qb[:, :, :], g_t[:, :, :], ACT.Exp).then_inc(s["gexp_ok"], 1)
        act.activation(kl[:, :, :], g_b[:, :, :], ACT.Exp).then_inc(s["gexp_ok"], 1)
        act.activation(dec[:, :, 0:4], g_t[:, :, BLK - 1:NP_:BLK], ACT.Exp).then_inc(s["gexp_ok"], 1)
        act.activation(dec[:, :, 4:5], g_t[:, :, N - 1:N], ACT.Exp).then_inc(s["gexp_ok"], 1)
        for c in range(4):
            act.wait_ge(s["cK_ps"], c + 1)
            act.copy(kS[0:FD, 2 * c + 1, :], bank[c][FD:P, :]).then_inc(s["cK_act"], 1)
        for i in range(3):
            act.wait_ge(s["tok_ps"], 3 + i + 1)
            act.activation(silu_gate(i), bank[4 + (3 + i) % 4][0:TN[i], :], ACT.Silu).then_inc(s["tok_act"], 1)
        for u in range(24):
            i = u // 8
            act.wait_ge(s["max_ok"], u + 1)
            if u >= 2:
                act.wait_ge(s["pT_ps"], u - 1)
            act.activation(prob[u % 2][0:TN[i], 0:NKEY[i]], score(u)[0:TN[i], 0:NKEY[i]], ACT.Exp, bias=nmax[0:TN[i], u:u + 1],
                           accum_out=rsum[0:TN[i], u:u + 1]).then_inc(s["exp_ok"], 1)
        ada_rows(1)
        ada_rows(2)
        for i in range(3):
            act.wait_ge(s["go_ok"], i + 1)
            act.wait_ge(s["po_ok"], i + 1)
            if i == 0:
                act.wait_ge(s["ada_out"], 64 * 3)
                act.wait_ge(s["zeros"], 2)
            for j in range(5):
                lo, hi = (GV * j, GV * j + GV) if j < 4 else (512, 1024)
                if i or j:
                    act.wait_ge(s["ssq_act"], 5 * i + j)
                act.activation(junk[0:TN[i], 0:hi - lo], o_tok[0:TN[i], i, lo:hi], ACT.Square,
                               accum_out=ssq5[0:TN[i], i, j:j + 1]).then_inc(s["ssq_act"], 1)
        act.wait_ge(s["ssq_act"], 15)
        act.activation(rs5[:, :, 0:4], ssq5[:, :, 0:4], ACT.Sqrt, bias=epst[:, 0:1], scale=1.0 / GV).then_inc(s["rs_act"], 1)
        act.activation(rs5[:, :, 4:5], ssq5[:, :, 4:5], ACT.Sqrt, bias=epst[:, 0:1], scale=1.0 / 512).then_inc(s["rs_act"], 1)
        for j in range(0, 8, 2):
            act.wait_ge(s["mT_ps"], j + 1)
            act.mul(mT[:, j, :], bank[j % 4][:, 0:N], g_gla[:, 0:1] if j < 4 else g_fox[:, j - 4:j - 3]).then_inc(s["mT_act"], 1)
        for k in range(KC):
            act.wait_ge(s["x1_ok"], k + 1 if k < KC - 1 else KC)
            if k == 0:
                act.wait_ge(s["x1_ok"], KC)
            act.activation(sq2[:, k, :], xT[:, k, :], ACT.Square).then_inc(s["x2_sq"], 1)
        act.wait_ge(s["ssq_ps"], 2)
        act.activation(rstdB[:, :], bank[6][:, 0:N], ACT.Sqrt, bias=epst[:, 0:1], scale=1.0 / D).then_inc(s["rstd_ok"], 1)
        act.wait_ge(s["h2n_ok"], 1)
        for k in range(KC):
            act.activation(h2T[:, k, 0:NP_], h2T[:, k, 0:NP_], ACT.Identity, bias=adaT[:, 3, 0, k:k + 1],
                           scale=gain2[:, 0, k:k + 1]).then_inc(s["h2_ok"], 1)
        act.wait_ge(s["rt_ps"], 1)
        for i in range(3):
            act.activation(sc[0:TN[i], i, :], bank[5][0:TN[i], E * i:E * i + E], ACT.Sigmoid).then_inc(s["rt_sc"], 1)
        act.wait_ge(s["gu_ps"], 1)
        for j in range(2):
            act.activation(sil[:, j, :], bank[j][:, 0:N], ACT.Silu).then_inc(s["sil_ok"], 1)
        with act.Fori(0, E) as e:
            act.wait_ge(s["gu_ps"], act.snap(e + 2))
            act.wait_ge(s["act_ok"], act.snap(2 * e + 2))
            for j in range(2):
                act.activation(sil[:, j, :], bank[j][:, 0:N], ACT.Silu).then_inc(s["sil_ok"], 1)
        for k in range(KC):
            act.wait_ge(s["fin_ok"], k + 1)
            act.activation(sq2[:, k, :], acc[:, k, :], ACT.Square).then_inc(s["x2_sq"], 1)
        act.wait_ge(s["ssq_ps"], 3)
        act.activation(rstdB[:, :], bank[6][:, 0:N], ACT.Sqrt, bias=epst[:, 0:1], scale=1.0 / D).then_inc(s["rstd_ok"], 1)
        for i in range(3):
            dst = y_sample[0] if i == 2 else y_prompt[0, 128 * i:128 * i + 128]
            act.wait_ge(s["y_ok"], 2 * i + 2)
            act.dma_start(dst, yout[0:TN[i], i, :]).then_inc(s["out_done"], 16)
        act.wait_ge(s["out_done"], 48)

    @block.gpsimd
    def _(pool):
        z = s["zeros"]
        pool.memset(ident[:, :], 0.0).then_inc(z, 1)
        pool.memset(ssq5[:, :, :], 1.0).then_inc(z, 1)
        pool.memset(identb[:, :], 0.0).then_inc(z, 1)
        pool.memset(ones[:, :], 1.0).then_inc(z, 1)
        pool.memset(causal[:, :], 0.0).then_inc(z, 1)
        pool.memset(epst[:, :], EPS).then_inc(z, 1)
        pool.wait_ge(z, 6)
        for t in (ident, identb):
            pool.affine_select(out=t[:, :], in_=t[:, :], compare_op=ALU.not_equal, fill=1.0, base=0,
                               pattern=[[-1, P]], channel_multiplier=1).then_inc(z, 1)
        pool.affine_select(out=upper[:, :], in_=ones[:, :], compare_op=ALU.is_ge, fill=0.0, base=0,
                           pattern=[[1, P]], channel_multiplier=-1).then_inc(z, 1)
        pool.affine_select(out=lower[:, :], in_=ones[:, :], compare_op=ALU.is_gt, fill=0.0, base=0,
                           pattern=[[-1, P]], channel_multiplier=1).then_inc(z, 1)
        pool.wait_ge(z, 10)
        pool.affine_select(out=glamask[0:BLK, :], in_=ones[0:BLK, 0:BLK], compare_op=ALU.is_ge, fill=0.0, base=0,
                           pattern=[[1, BLK]], channel_multiplier=-1).then_inc(z, 1)
        pool.wait_ge(z, 11)
        pool.affine_select(out=glamask[BLK:P, :], in_=ones[BLK:P, 0:BLK], compare_op=ALU.is_ge, fill=0.0, base=0,
                           pattern=[[1, BLK]], channel_multiplier=-1).then_inc(z, 1)
        pool.wait_ge(z, 12)
        pool.affine_select(out=causal[:, :], in_=causal[:, :], compare_op=ALU.is_ge, fill=NEG, base=0,
                           pattern=[[-1, P]], channel_multiplier=1).then_inc(s["consts"], 1)
        pool.wait_ge(s["consts"], 1)
        pool.memset(qA[FD:FD + 2, :, :], 1.0).then_inc(s["ones_ok"], 1)
        pool.wait_ge(s["ones_ok"], 1)
        pool.memset(kA[FD:FD + 2, :, :], 1.0).then_inc(s["ones_ok"], 1)
        pool.wait_ge(s["ones_ok"], 2)
        pool.wait_ge(s["xT_ps"], 8)
        pool.memset(kS[FD:FD + 2, :, :], 1.0).then_inc(s["ones_ok"], 1)
        pool.wait_ge(s["ones_ok"], 3)
        pool.memset(a_t[:, :, :, :, :], 0.0).then_inc(z, 1)
        pool.wait_ge(s["logf_ok"], 1)
        pool.dma_start(f_prompt[0, 0].rearrange("(i p) h -> p i h", p=P), logf[:, 0:2, :]).then_inc(s["f_out"], 16)
        pool.dma_start(f_sample[0, 0], logf[0:NS_, 2, :]).then_inc(s["f_out"], 16)
        pool.wait_ge(s["crow_ok"], 3)
        pool.dma_start(crow_d.rearrange("a h n -> h a n"), crow[:, :, :]).then_inc(s["crow_out"], 16)
        pool.dma_start(srow_d, srow[:, :]).then_inc(s["crow_out"], 16)
        pool.wait_ge(s["crow_out"], 32)
        pool.wait_ge(s["ones_ok"], 3)
        pool.dma_start(qA[FD + 1:FD + 2, :, :], crow_d[0:1]).then_inc(s["rows_in"], 16)
        pool.dma_start(kA[FD:FD + 1, :, :], crow_d[1:2]).then_inc(s["rows_in"], 16)
        pool.dma_start(kS[FD:FD + 1, :, :], srow_d.rearrange("(o h) n -> o h n", o=1)).then_inc(s["rows_in"], 16)
        pool.wait_ge(s["state_ok"], 10)
        for c in range(2):
            pool.dma_start(st_prompt[0, 0, 2 * c:2 * c + 2].rearrange("h k v -> (h k) v"), states[:, 3, c, :]).then_inc(s["st_out"], 16)
            pool.dma_start(st_sample[0, 0, 2 * c:2 * c + 2].rearrange("h k v -> (h k) v"), states[:, 5, c, :]).then_inc(s["st_out"], 16)
        pool.wait_ge(s["tok_dve"], 9)
        for q, (kp, ks_) in enumerate(((k_prompt, k_sample), (v_prompt, v_sample))):
            for i in range(2):
                pool.dma_start(kp[0, 0, 128 * i:128 * i + 128].rearrange("t h d -> t (h d)"), toks[:, 2 + q, i, :]).then_inc(s["kv_out"], 16)
            pool.dma_start(ks_[0, 0].rearrange("t h d -> t (h d)"), toks[0:NS_, 2 + q, 2, :]).then_inc(s["kv_out"], 16)
        pool.wait_ge(s["kv_out"], 96)
        pool.wait_ge(s["st_out"], 64)
        pool.wait_ge(s["f_out"], 32)

    @block.tensor
    def _(pe):
        mm, tr = nc.tensor.matmul, nc.tensor.transpose
        pe.wait_ge(s["consts"], 1)
        pe.wait_ge(s["x_in"], 48)
        for k in range(KC):
            if k >= 4:
                pe.wait_ge(s["xT_ok"], k - 3)
            for i in range(3):
                last = tr(bank[k % 4][:, T0[i]:T0[i] + TN[i]], x_tok[0:TN[i], i, k::KC], ident[0:TN[i], 0:TN[i]])
            last.then_inc(s["xT_ps"], 1)

        def sumsq(src, sem_, n0):
            for k in range(KC):
                pe.wait_ge(sem_, n0 + k + 1)
                last = mm(bank[6][:, 0:N], ones[:, :], src[:, k, :], start=k == 0, stop=k == KC - 1)
            last.then_inc(s["ssq_ps"], 1)

        sumsq(sq, s["sq_ok"], 0)

        def ada(r):
            for k in range(KC):
                n = k if r == 0 else FIRST_R1 + KC * (r - 1) + k
                piece_in(pe, n)
                for j in range(4):
                    last = mm(bank[5][32 * j:32 * j + 2, :], scT[:, k, :], piece(n)[:, 512 * j:512 * j + 512],
                              start=k == 0, stop=k == KC - 1, tile_position=(0, 32 * j))
                last.then_inc(s["w_used"], 1)
            pe.wait_ge(s["w_used"], FIRST_WIN if r == 0 else FIRST_R1 + KC * r)
            mm(bank[7][0:2, 0:2], ident[:, 0:2], ident[:, 0:2], start=True, stop=True).then_inc(s["ada_ps"], 1)

        pe.wait_ge(s["sc_ok"], 1)
        ada(0)

        pe.wait_ge(s["hT_ok"], 24)
        for g in range(6):
            piece_in(pe, FIRST_WIN + g)
            w = piece(FIRST_WIN + g)[:, :].rearrange("p (k n) -> p k n", k=KC)
            for q in range(4):
                c = 4 * g + q
                if c >= 4:
                    pe.wait_ge(s["z_act" if c % 2 else "z_dve"], (c - 4) // 2 + 1)
                for k in range(KC):
                    last = mm(bank[c % 4][:, 0:N], w[:, k, P * q:P * q + P], hT[:, k, :], start=k == 0, stop=k == KC - 1)
                last.then_inc(s["z_ps"], 1)
            pe.wait_ge(s["z_ps"], 4 * g + 4)
            mm(bank[7][0:2, 0:2], ident[:, 0:2], ident[:, 0:2], start=True, stop=True).then_inc(s["w_used"], 1)
        pe.wait_ge(s["small_in"], SMALL)
        for k in range(KC):
            mm(bank[4][0:LR, 0:N], w_lf[:, k, 0:LR], hT[:, k, :], start=k == 0, stop=k == KC - 1)
        for i in range(3):
            for k in range(KC):
                last = mm(bank[5][0:TN[i], FH * i:FH * i + FH], hT[:, k, T0[i]:T0[i] + TN[i]], w_lf[:, k, LR:],
                          start=k == 0, stop=k == KC - 1)
        last.then_inc(s["narrow_ps"], 1)
        pe.wait_ge(s["z_act"], 12)
        pe.wait_ge(s["z_dve"], 12)
        pe.wait_ge(s["cache_in"], 48)
        for c in range(4):
            for j in range(4):
                last = tr(bank[c][:, P * j:P * j + P], cacheK[:, j, P * c:P * c + P], ident[:, :])
            last.then_inc(s["cK_ps"], 1)
        pe.wait_ge(s["glr_ok"], 1)
        pe.wait_ge(s["ff_ok"], 1)
        for c in range(2):
            last = mm(bank[4 + c][:, 0:N], w_gk2[:, P * c:P * c + P], glr[:, :], start=True, stop=True)
        last.then_inc(s["gate_ps"], 1)
        pe.wait_ge(s["logf_ok"], 1)
        cb = bank[6]
        mm(cb[0:FH, 0:128], logf[:, 0, :], upper[:, :], start=True, stop=True)
        mm(cb[0:FH, 128:256], logf[:, 0, :], ones[:, :], start=True, stop=False)
        mm(cb[0:FH, 128:256], logf[:, 1, :], upper[:, :], start=False, stop=True)
        mm(cb[0:FH, 256:N], logf[0:NS_, 2, :], upper[0:NS_, 0:NS_], start=True, stop=True).then_inc(s["crow_ps"], 1)
        for j in range(4):
            for t in range(j, 4):
                last = mm(bank[7][0:FH, P * j:P * j + P], pastf[:, t, :], (lower if t == j else ones)[:, :],
                          start=t == j, stop=t == 3)
        last.then_inc(s["crow_ps"], 1)
        pe.wait_ge(s["gate_x"], 1)
        pe.wait_ge(s["crow_ok"], 3)
        for q in range(12):
            kind, i = q // 3, q % 3
            if q >= 4:
                kb, ib = (q - 4) // 3, (q - 4) % 3
                pe.wait_ge(s["tok_act" if kb == 1 else "tok_dve"], ib + 1 + (0 if kb < 2 else 3 * (kb - 1)))
            for j in range(4):
                last = tr(bank[4 + q % 4][0:TN[i], P * j:P * j + P], zt[:, 4 * kind + j, T0[i]:T0[i] + TN[i]], ident[:, :])
            last.then_inc(s["tok_ps"], 1)
        pe.wait_ge(s["tok_dve"], 9)
        pe.wait_ge(s["tok_act"], 3)
        pe.wait_ge(s["gprod_ok"], 4)
        for i in range(3):
            for c in range(2):
                o = 256 * (i % 2) + P * c
                last = tr(bank[4 + i // 2][0:TN[i], o:o + P], kl[:, c, T0[i]:T0[i] + TN[i]], ident[:, :])
        last.then_inc(s["klT_ps"], 1)
        def blocks():
            for b in range(5):
                i, pb, n = b // 2, 64 * (b % 2), BLK if b < 4 else NS_
                yield b, i, pb, n
        for b, i, pb, n in blocks():
            for h in range(GH):
                r, c = 64 * (h % 2), h // 2
                t0 = T0[i] + pb
                o = P * i + BLK * c
                last = mm(bank[6 + h % 2][pb:pb + n, o:o + n], ke[r:r + GK, c, t0:t0 + n], qe[r:r + GK, c, t0:t0 + n],
                          start=True, stop=True)
        last.then_inc(s["aT_ps"], 1)
        pe.wait_ge(s["cK_act"], 4)
        pe.wait_ge(s["cK_dve"], 4)
        pe.wait_ge(s["klT_ok"], 1)
        for b, i, pb, n in blocks():
            for h in range(GH):
                r, c = 64 * (h % 2), h // 2
                last = mm(update(b, c)[r:r + GK, :], kl_tok[pb:pb + n, i, GK * h:GK * h + GK],
                          toks[pb:pb + n, 0, i, GV * h:GV * h + GV], start=True, stop=True)
        last.then_inc(s["upd_ps"], 1)
        pe.wait_ge(s["aT_ok"], 4)
        pe.wait_ge(s["state_ok"], 10)
        for b, i, pb, n in blocks():
            for h in range(GH):
                r, c = 64 * (h % 2), h // 2
                t0 = T0[i] + pb
                mm(bank[3 + i][pb:pb + n, GV * h:GV * h + GV], a_t[pb:pb + n, h % 2, i, c, 0:n],
                   toks[pb:pb + n, 0, i, GV * h:GV * h + GV], start=True, stop=True)
                if b:
                    last = mm(inter(i, h % 2)[pb:pb + n, GV * c:GV * c + GV], qb[r:r + GK, c, t0:t0 + n],
                              states[r:r + GK, b - 1 if b < 4 else 4, c, :], start=True, stop=True)
            if b % 2 or b == 4:
                last.then_inc(s["go_ps"], 1)
        pe.wait_ge(s["rows_in"], 48)

        def scores(u):
            i, h = u // 8, u % 8
            if u < 2:
                pe.wait_ge(s["go_ok"], 3)
            else:
                pe.wait_ge(s["exp_ok"], u - 1)
            q = qA[:, h, T0[i]:T0[i] + TN[i]]
            out = score(u)[0:TN[i]]
            if i < 2:
                d = P * i
                if i:
                    mm(out[:, 0:P], q, kA[:, h, 0:P], start=True, stop=True)
                mm(out[:, d:d + P], q, kA[:, h, d:d + P], start=True, stop=False)
                last = mm(out[:, d:d + P], identb[:, :], causal[:, :], start=False, stop=True)
            else:
                mm(out[:, 0:PAST], q, kS[:, h, :], start=True, stop=True)
                mm(out[:, PAST:PAST + NS_], q, kA[:, h, NP_:N], start=True, stop=False)
                last = mm(out[:, PAST:PAST + NS_], identb[0:NS_, 0:NS_], causal[0:NS_, 0:NS_], start=False, stop=True)
            last.then_inc(s["sc_ps"], 1)

        def transposed(u):
            i, n = u // 8, TN[u // 8]
            pe.wait_ge(s["exp_ok"], u + 1)
            if u >= 2:
                pe.wait_ge(s["pT_ok"], u - 1)
            for t in range((NKEY[i] + P - 1) // P):
                w = min(P, NKEY[i] - P * t)
                last = tr(bank[u % 2][0:w, n * t:n * t + n], prob[u % 2][0:n, P * t:P * t + w], ident[0:n, 0:n])
            last.then_inc(s["pT_ps"], 1)

        def values(u):
            i, h, n = u // 8, u % 8, TN[u // 8]
            pe.wait_ge(s["pT_ok"], u + 1)
            if h == 0 and i == 2:
                pe.wait_ge(s["po_ok"], 1)
            nt = (NKEY[i] + P - 1) // P
            for t in range(nt):
                w = min(P, NKEY[i] - P * t)
                v = cacheV[:, t, FD * h:FD * h + FD] if i == 2 and t < 4 else toks[0:w, 3, 2 if i == 2 else t, FD * h:FD * h + FD]
                last = mm(bank[2 + i % 2][0:n, FD * h:FD * h + FD], probT[u % 2][0:w, n * t:n * t + n], v, start=t == 0, stop=t == nt - 1)
            last.then_inc(s["po_ps"], 1)

        scores(0)
        for u in range(24):
            if u + 1 < 24:
                scores(u + 1)
            transposed(u)
            if u:
                values(u - 1)
        values(23)
        pe.wait_ge(s["exp_ok"], 24)
        ada(1)
        pe.wait_ge(s["ada_row"], 8)
        ada(2)
        pe.wait_ge(s["po_ok"], 3)
        for j in range(8):
            if j >= 4:
                pe.wait_ge(s["mT_dve" if j % 2 else "mT_act"], (j - 4) // 2 + 1)
            for i in range(3):
                pe.wait_ge(s["on_ok"], 3)
                last = tr(bank[j % 4][:, T0[i]:T0[i] + TN[i]], o_tok[0:TN[i], i, P * j:P * j + P], ident[0:TN[i], 0:TN[i]])
            last.then_inc(s["mT_ps"], 1)
        pe.wait_ge(s["mT_act"], 4)
        pe.wait_ge(s["mT_dve"], 4)
        piece_in(pe, FIRST_WO)
        piece_in(pe, FIRST_WO + 1)
        for k in range(KC):
            if k >= 4:
                pe.wait_ge(s["x1_ok"], k - 3)
            for j in range(8):
                w = piece(FIRST_WO + j // 4)[:, :].rearrange("p (j n) -> p j n", j=4)[:, j % 4, k::KC]
                last = mm(bank[k % 4][:, 0:N], w, mT[:, j, :], start=j == 0, stop=j == 7)
            last.then_inc(s["mix_ps"], 1)
        pe.wait_ge(s["mix_ps"], KC)
        for _ in range(2):
            mm(bank[7][0:2, 0:2], ident[:, 0:2], ident[:, 0:2], start=True, stop=True).then_inc(s["w_used"], 1)
        sumsq(sq2, s["x2_sq"], 0)
        pe.wait_ge(s["h2_ok"], 16)
        for i in range(3):
            for k in range(KC):
                last = mm(bank[5][0:TN[i], E * i:E * i + E], h2T[:, k, T0[i]:T0[i] + TN[i]], w_rt[:, k, :],
                          start=k == 0, stop=k == KC - 1)
        last.then_inc(s["rt_ps"], 1)

        def gate_up(q0):
            for j in range(2):
                for w in range(2):
                    wt = ring[q0 + w][:, :].rearrange("p (k n) -> p k n", k=KC)
                    for k in range(KC):
                        last = mm(bank[j + 2 * w][:, 0:N], wt[:, k, j::2], h2T[:, k, :], start=k == 0, stop=k == KC - 1)
            last.then_inc(s["gu_ps"], 1)

        def down(q0, wait_dn):
            wt = ring[q0 + 2][:, :].rearrange("p (j n) -> p j n", j=2)
            for k in range(KC):
                wait_dn(k)
                for j in range(2):
                    last = mm(bank[5 + k % 2][:, 0:N], wt[:, j, k::KC], actT[:, j, :], start=j == 0, stop=j == 1)
                last.then_inc(s["dn_ps"], 1)

        def used(n):
            pe.wait_ge(s["dn_ps"], n)
            mm(bank[7][0:2, 0:2], ident[:, 0:2], ident[:, 0:2], start=True, stop=True).then_inc(s["w_used"], 1)

        for q in range(3):
            pe.wait_ge(ring_in[SHARED + q], 16)
        gate_up(SHARED)
        pe.wait_ge(s["act_ok"], 2)
        pe.wait_ge(s["rt_sc"], 3)
        pe.wait_ge(s["rstd_ok"], 2)
        down(SHARED, lambda k: pe.wait_ge(s["dn_ok"], k - 1) if k >= 2 else None)
        used(KC)
        pe.wait_ge(s["wrt_ok"], 3)
        for i in range(3):
            last = tr(bank[4][0:E, T0[i]:T0[i] + TN[i]], wrt[0:TN[i], i, :], ident[0:TN[i], 0:TN[i]])
        last.then_inc(s["wT_ps"], 1)
        with pe.Fori(0, E // PER) as it:
            for u in range(PER):
                e = it * PER + u
                q0 = PER and 3 * u
                for q in range(3):
                    pe.wait_ge(ring_in[q0 + q], pe.snap(16 * it + 16 * (loads[q0 + q] + 1)))
                pe.wait_ge(s["act_ok"], pe.snap(2 * e + 2))
                gate_up(q0)
                pe.wait_ge(s["wm_ok"], pe.snap(e + 1))
                mm(bank[4][:, 0:N], ones[0:E, :], wm[:, :], start=True, stop=True).then_inc(s["su_ok"], 1)
                pe.wait_ge(s["act_ok"], pe.snap(2 * e + 4))
                down(q0, lambda k: pe.wait_ge(s["dn_ok"], pe.snap(KC * e + (KC + k - 1))))
                used(pe.snap(KC * e + 2 * KC))
        sumsq(sq2, s["x2_sq"], KC)
        for i in range(3):
            for k in range(KC):
                if i == 0 and k == 0:
                    pe.wait_ge(s["h2n_ok"], 2)
                if k % 4 == 0 and i >= 1:
                    n = 2 * (i - 1) + k // 4
                    pe.wait_ge(s["y_ok"], n + 1)
                last = tr(bank[k // 4][0:TN[i], P * (k % 4):P * (k % 4) + P], acc[:, k, T0[i]:T0[i] + TN[i]], ident[:, :])
                if k % 4 == 3:
                    last.then_inc(s["y_ps"], 1)

    @block.vector
    def _(dve):
        chain = [0]

        def link(ins):
            chain[0] += 1
            ins.then_inc(s["d_chain"], 1)
            dve.wait_ge(s["d_chain"], chain[0])

        def over_k(ap):
            return ap.unsqueeze(1).broadcast_to([P, KC, N])

        for k in range(KC):
            dve.wait_ge(s["xT_ps"], k + 1)
            dve.tensor_copy(xT[:, k, :], bank[k % 4][:, 0:N]).then_inc(s["xT_ok"], 1)
        dve.wait_ge(s["rstd_ok"], 1)
        link(dve.reciprocal(rstdB[:, :], rstdB[:, :]))
        dve.wait_ge(s["xT_ok"], KC)
        dve.tensor_tensor(xn[:, :, :], xT[:, :, :], over_k(rstdB[:, :]), ALU.mult).then_inc(s["xn_ok"], 1)

        def modulation(r):
            dve.wait_ge(s["small_in"], SMALL)
            dve.wait_ge(s["adaT_in"], 96 if r else 32)
            m = adaT[:, 2 * r:2 * r + 2, :, :]
            link(dve.tensor_tensor(m, m, b_adaT[:, 2 * r:2 * r + 2, :].unsqueeze(2).broadcast_to([P, 2, 2, KC]), ALU.add))

        modulation(0)
        for g in range(2):
            dve.scalar_tensor_tensor(out=gain1[:, g, :], in0=adaT[:, 1, g, :], scalar=1.0, in1=g_mix[:, :],
                                     op0=ALU.add, op1=ALU.mult).then_inc(s["gain_ok"], 1)
        dve.wait_ge(s["gain_ok"], 2)
        dve.wait_ge(s["xn_ok"], 1)
        for k in range(KC):
            dve.tensor_scalar(hT[:, k, NP_:N], xn[:, k, NP_:N], gain1[:, 1, k:k + 1], adaT[:, 0, 1, k:k + 1],
                              ALU.mult, ALU.add).then_inc(s["hT_ok"], 1)
        dve.wait_ge(s["hT_ok"], 16)
        dve.memset(lf_t[:, :, :], 0.0).then_inc(s["hT_ok"], 8)
        for c in range(0, 24, 2):
            dve.wait_ge(s["z_ps"], c + 1)
            b = bank[c % 4]
            if c < 2:
                last = dve.tensor_scalar(gqk[:, c, :], b[:, 0:N], GK ** -0.5, None, ALU.mult)
            elif c < 4:
                last = dve.tensor_copy(gqk[:, c, :], b[:, 0:N])
            elif 12 <= c < 16:
                dve.tensor_scalar(qA[0:FD, 2 * (c - 12), :], b[0:FD, 0:N], FD ** -0.5, None, ALU.mult)
                last = dve.tensor_scalar(qA[0:FD, 2 * (c - 12) + 1, :], b[FD:P, 0:N], FD ** -0.5, None, ALU.mult)
            elif 16 <= c < 20:
                dve.tensor_copy(kA[0:FD, 2 * (c - 16), :], b[0:FD, 0:N])
                dve.tensor_copy(kA[0:FD, 2 * (c - 16) + 1, :], b[FD:P, 0:N])
                last = dve.tensor_copy(zt[:, 8 + c - 16, :], b[:, 0:N])
            else:
                last = dve.tensor_copy(zt[:, c - 4 if c < 12 else c - 8, :], b[:, 0:N])
            last.then_inc(s["z_dve"], 1)
        dve.wait_ge(s["narrow_ps"], 1)
        for i in range(3):
            last = dve.tensor_tensor(lf_t[0:TN[i], i, :], bank[5][0:TN[i], FH * i:FH * i + FH], b_ff[0:TN[i], :], ALU.add)
            if i == 2:
                last.then_inc(s["ff_ok"], 1)
            else:
                link(last)
        dve.wait_ge(s["ff_ok"], 1)
        link(dve.tensor_scalar(lf_m[:, :, :], lf_t[:, :, :], 0.0, None, ALU.min))
        dve.scalar_tensor_tensor(out=lf_t[:, :, :], in0=lf_m[:, :, :], scalar=-2.0, in1=lf_t[:, :, :], op0=ALU.mult,
                                 op1=ALU.add).then_inc(s["lf_abs"], 1)
        dve.wait_ge(s["lf_ln"], 1)
        dve.tensor_tensor(logf[:, :, :], lf_m[:, :, :], lf_t[:, :, :], ALU.subtract).then_inc(s["logf_ok"], 1)
        for c in range(4):
            dve.wait_ge(s["cK_ps"], c + 1)
            dve.tensor_copy(kS[0:FD, 2 * c, :], bank[c][0:FD, :]).then_inc(s["cK_dve"], 1)
        dve.wait_ge(s["gate_ps"], 1)
        for c in range(2):
            last = dve.tensor_scalar(g_t[:, c, :], bank[4 + c][:, 0:N], b_gk[:, c:c + 1], None, ALU.add)
            if c:
                last.then_inc(s["gate_x"], 1)
            else:
                link(last)
        dve.wait_ge(s["gate_x"], 1)
        link(dve.tensor_scalar(g_b[:, :, :], g_t[:, :, :], 0.0, None, ALU.min))
        dve.scalar_tensor_tensor(out=g_a[:, :, :], in0=g_b[:, :, :], scalar=-2.0, in1=g_t[:, :, :], op0=ALU.mult,
                                 op1=ALU.add).then_inc(s["gate_abs"], 1)
        dve.wait_ge(s["crow_ps"], 1)
        dve.tensor_copy(crow[:, 0, :], bank[6][0:FH, 0:N]).then_inc(s["crow_ok"], 1)
        dve.tensor_scalar(crow[:, 1, :], bank[6][0:FH, 0:N], -1.0, None, ALU.mult).then_inc(s["crow_ok"], 1)
        dve.wait_ge(s["crow_ps"], 2)
        dve.tensor_copy(srow[:, :], bank[7][0:FH, :]).then_inc(s["crow_ok"], 1)
        dve.wait_ge(s["gate_ln"], 1)
        link(dve.tensor_tensor(g_t[:, :, :], g_b[:, :, :], g_a[:, :, :], ALU.subtract))
        link(dve.tensor_scalar(g_b[:, :, :], g_t[:, :, :], 1.0 / 16.0, None, ALU.mult))
        for c in range(2):
            for b in range(5):
                t0, n = BLK * b, BLK if b < 4 else NS_
                last = dve.tensor_tensor_scan(g_t[:, c, t0:t0 + n], ones[:, 0:n], g_b[:, c, t0:t0 + n], 0.0, ALU.mult, ALU.add)
        link(last)

        def by_block(t, c):
            return t[:, c, 0:NP_].rearrange("p (b n) -> p b n", n=BLK)

        for c in range(2):
            def col(at):
                return g_t[:, c, at:NP_:BLK].unsqueeze(2).broadcast_to([P, 4, BLK])

            def scol(at):
                return g_t[:, c, at:at + 1].broadcast_to([P, NS_])
            dve.tensor_tensor(by_block(g_a, c), by_block(g_t, c), col(BLK // 2), ALU.subtract)
            dve.tensor_tensor(g_a[:, c, NP_:N], g_t[:, c, NP_:N], scol(NP_ + NS_ // 2), ALU.subtract).then_inc(s["cum_ok"], 1)
            dve.tensor_tensor(by_block(g_b, c), col(BLK - 1), by_block(g_t, c), ALU.subtract)
            dve.tensor_tensor(g_b[:, c, NP_:N], scol(N - 1), g_t[:, c, NP_:N], ALU.subtract).then_inc(s["cum_ok"], 1)
        for n, (t, z0) in enumerate(((qe, 0), (ke, 2), (qb, 0), (kl, 2))):
            dve.wait_ge(s["gexp_ok"], n + 1)
            dve.tensor_tensor(t[:, :, :], t[:, :, :], gqk[:, z0:z0 + 2, :], ALU.mult).then_inc(s["gprod_ok"], 1)
        for q in range(12):
            kind, i = q // 3, q % 3
            if kind != 1:
                dve.wait_ge(s["tok_ps"], q + 1)
                dve.tensor_copy(toks[0:TN[i], kind, i, :], bank[4 + q % 4][0:TN[i], :]).then_inc(s["tok_dve"], 1)
        dve.wait_ge(s["klT_ps"], 1)
        link(dve.tensor_copy(kl_tok[:, 0:2, :], bank[4][:, :].rearrange("p (i n) -> p i n", i=2)))
        dve.tensor_copy(kl_tok[0:NS_, 2, :], bank[5][0:NS_, 0:256]).then_inc(s["klT_ok"], 1)
        dve.wait_ge(s["aT_ps"], 1)
        dve.wait_ge(s["zeros"], 13)
        mask = glamask[:, :].bitcast(I32)
        for q in range(2):
            dve.copy_predicated(a_t[:, q, 0:2, :, :].rearrange("p i c n -> p (i c) n"), mask.unsqueeze(1).broadcast_to([P, 4, BLK]),
                                bank[6 + q][:, 0:256].rearrange("p (g n) -> p g n", n=BLK)).then_inc(s["aT_ok"], 1)
            dve.copy_predicated(a_t[0:NS_, q, 2, :, 0:NS_], mask[0:NS_, 0:NS_].unsqueeze(1).broadcast_to([NS_, 2, NS_]),
                                bank[6 + q][0:NS_, 256:384].rearrange("p (g n) -> p g n", n=BLK)[:, :, 0:NS_]).then_inc(s["aT_ok"], 1)
        dve.wait_ge(s["upd_ps"], 1)
        dve.wait_ge(s["gexp_ok"], 6)
        dve.wait_ge(s["state_in"], 32)

        for c in range(2):
            dve.tensor_copy(states[:, 0, c, :], update(0, c)).then_inc(s["state_ok"], 1)
            dve.scalar_tensor_tensor(out=states[:, 5, c, :], in0=states[:, 4, c, :], scalar=dec[:, c, 4:5], in1=update(4, c),
                                     op0=ALU.mult, op1=ALU.add).then_inc(s["state_ok"], 1)
        for b in range(1, 4):
            dve.wait_ge(s["state_ok"], 2 + 2 * b)
            for c in range(2):
                dve.scalar_tensor_tensor(out=states[:, b, c, :], in0=states[:, b - 1, c, :], scalar=dec[:, c, b:b + 1],
                                         in1=update(b, c), op0=ALU.mult, op1=ALU.add).then_inc(s["state_ok"], 1)
        for i in range(3):
            dve.wait_ge(s["go_ps"], max(i + 1, 2))
            link(dve.tensor_copy(o_tok[0:TN[i], i, 0:512], bank[3 + i][0:TN[i], :]))
            lo = BLK if i == 0 else 0
            for q in range(2):
                o = o_tok[lo:TN[i], i, 0:512].rearrange("t (c q v) -> t c q v", c=2, q=2)[:, :, q, :]
                last = dve.tensor_tensor(o, inter(i, q)[lo:TN[i], :].rearrange("t (c v) -> t c v", c=2), o, ALU.add)
            last.then_inc(s["go_ok"], 1)
        def maxima(u):
            i, n = u // 8, TN[u // 8]
            dve.wait_ge(s["sc_ps"], u + 1)
            dve.tensor_reduce(nmax[0:n, u:u + 1], score(u)[0:n, 0:NKEY[i]], AX, ALU.max, negate=True).then_inc(s["max_ok"], 1)

        maxima(0)
        for u in range(24):
            i, n = u // 8, TN[u // 8]
            if u + 1 < 24:
                maxima(u + 1)
            dve.wait_ge(s["pT_ps"], u + 1)
            if u >= 2:
                dve.wait_ge(s["po_ps"], u - 1)
            if i < 2:
                dve.tensor_copy(probT[u % 2][:, 0:n * (i + 1)], bank[u % 2][:, 0:n * (i + 1)]).then_inc(s["pT_ok"], 1)
            else:
                link(dve.tensor_copy(probT[u % 2][:, 0:4 * n], bank[u % 2][:, 0:4 * n]))
                dve.tensor_copy(probT[u % 2][0:NS_, 4 * n:5 * n], bank[u % 2][0:NS_, 4 * n:5 * n]).then_inc(s["pT_ok"], 1)
            if u % 8 == 0 and u:
                divide(dve, i - 1, link)
        divide(dve, 2, link)
        modulation(1)
        modulation(2)
        for g in range(2):
            dve.scalar_tensor_tensor(out=gain2[:, g, :], in0=adaT[:, 4, g, :], scalar=1.0, in1=g_ffn[:, :],
                                     op0=ALU.add, op1=ALU.mult).then_inc(s["gain_ok"], 1)
        dve.wait_ge(s["rs_act"], 2)
        link(dve.reciprocal(rs5[:, :, :], rs5[:, :, :]))
        for i in range(3):
            n = TN[i]
            for h in range(GH):
                o = o_tok[0:n, i, GV * h:GV * h + GV]
                dve.scalar_tensor_tensor(out=o, in0=o, scalar=rs5[0:n, i, h:h + 1], in1=toks[0:n, 1, i, GV * h:GV * h + GV],
                                         op0=ALU.mult, op1=ALU.mult)
            dve.tensor_scalar(o_tok[0:n, i, 512:1024], o_tok[0:n, i, 512:1024], rs5[0:n, i, 4:5], None, ALU.mult).then_inc(s["on_ok"], 1)
        for j in range(1, 8, 2):
            dve.wait_ge(s["mT_ps"], j + 1)
            dve.tensor_scalar(mT[:, j, :], bank[j % 4][:, 0:N], g_gla[:, 0:1] if j < 4 else g_fox[:, j - 4:j - 3], None,
                              ALU.mult).then_inc(s["mT_dve"], 1)
        for k in range(KC):
            dve.wait_ge(s["mix_ps"], k + 1)
            dve.scalar_tensor_tensor(out=xT[:, k, 0:NP_], in0=bank[k % 4][:, 0:NP_], scalar=adaT[:, 2, 0, k:k + 1],
                                     in1=xT[:, k, 0:NP_], op0=ALU.mult, op1=ALU.add)
            dve.scalar_tensor_tensor(out=xT[:, k, NP_:N], in0=bank[k % 4][:, NP_:N], scalar=adaT[:, 2, 1, k:k + 1],
                                     in1=xT[:, k, NP_:N], op0=ALU.mult, op1=ALU.add).then_inc(s["x1_ok"], 1)
        dve.wait_ge(s["rstd_ok"], 2)
        link(dve.reciprocal(rstdB[:, :], rstdB[:, :]))
        dve.wait_ge(s["x1_ok"], KC)
        dve.tensor_tensor(h2T[:, :, :], xT[:, :, :], over_k(rstdB[:, :]), ALU.mult).then_inc(s["h2n_ok"], 1)
        dve.wait_ge(s["h2n_ok"], 1)
        dve.wait_ge(s["gain_ok"], 4)
        for k in range(KC):
            dve.tensor_scalar(h2T[:, k, NP_:N], h2T[:, k, NP_:N], gain2[:, 1, k:k + 1], adaT[:, 3, 1, k:k + 1],
                              ALU.mult, ALU.add).then_inc(s["h2_ok"], 1)

        def select(out, vals, width, k, n, last_op):
            v = vals
            thr = t8[0:n, k - 1:k]
            a, b, c = r_a[0:n, 0:width], r_b[0:n, 0:width], r_c[0:n, 0:width]
            link(dve.tensor_scalar(a, v, thr, 0.0, ALU.is_gt, ALU.add, accum_out=r_n[0:n, :]))
            link(dve.tensor_scalar(b, v, thr, None, ALU.is_equal))
            link(dve.tensor_tensor_scan(c, ones[0:n, 0:width], b, 0.0, ALU.mult, ALU.add))
            link(dve.tensor_scalar(c, c, r_n[0:n, 0:1], float(k), ALU.add, ALU.is_le))
            link(dve.tensor_tensor(b, b, c, ALU.mult))
            last_op(dve.tensor_tensor(out, a, b, ALU.add))

        for i in range(3):
            n = TN[i]
            dve.wait_ge(s["rt_sc"], i + 1)
            link(dve.tensor_tensor(ch[0:n, i, :], sc[0:n, i, :], b_rt[0:n, :], ALU.add))
            for g in range(NG):
                last = dve.max(top[0:n, g, :], ch[0:n, i, 8 * g:8 * g + 8])
            link(last)
            link(dve.tensor_tensor(gs[0:n, :], top[0:n, :, 0], top[0:n, :, 1], ALU.add))
            link(dve.max(t8[0:n, :], gs[0:n, :]))
            select(gs[0:n, :], gs[0:n, :], NG, TOPG, n, link)
            link(dve.tensor_scalar(gs[0:n, :], gs[0:n, :], 1.0, -NEG, ALU.subtract, ALU.mult))
            link(dve.tensor_tensor(ch[0:n, i, :].rearrange("p (g m) -> p g m", g=NG), ch[0:n, i, :].rearrange("p (g m) -> p g m", g=NG),
                                   gs[0:n, :].unsqueeze(2).broadcast_to([n, NG, 8]), ALU.add))
            link(dve.max(t8[0:n, :], ch[0:n, i, :]))
            select(ch[0:n, i, :], ch[0:n, i, :], E, TOPK, n, link)
            link(dve.tensor_tensor(wrt[0:n, i, :], sc[0:n, i, :], ch[0:n, i, :], ALU.mult))
            link(dve.tensor_reduce(r_n[0:n, :], wrt[0:n, i, :], AX, ALU.add))
            link(dve.tensor_scalar(r_n[0:n, :], r_n[0:n, :], 1e-20, None, ALU.add))
            link(dve.reciprocal(r_n[0:n, :], r_n[0:n, :]))
            dve.tensor_scalar(wrt[0:n, i, :], wrt[0:n, i, :], r_n[0:n, 0:1], RSCALE, ALU.mult, ALU.mult).then_inc(s["wrt_ok"], 1)
        for j in range(2):
            dve.wait_ge(s["sil_ok"], j + 1)
            dve.tensor_tensor(actT[:, j, :], bank[2 + j][:, 0:N], sil[:, j, :], ALU.mult).then_inc(s["act_ok"], 1)
        for k in range(KC):
            dve.wait_ge(s["dn_ps"], k + 1)
            dve.tensor_copy(acc[:, k, :], bank[5 + k % 2][:, 0:N]).then_inc(s["dn_ok"], 1)
        dve.wait_ge(s["wT_ps"], 1)
        dve.tensor_copy(wT[:, :], bank[4][0:E, 0:N]).then_inc(s["wT_ok"], 1)
        dve.wait_ge(s["wT_ok"], 1)
        with dve.Fori(0, E) as e:
            dve.tensor_scalar(wm[:, :], wT[:, :], ident[0:E, bass.ds(e, 1)], None, ALU.mult).then_inc(s["wm_ok"], 1)
            for j in range(2):
                dve.wait_ge(s["sil_ok"], dve.snap(2 * e + (3 + j)))
                dve.tensor_tensor(actT[:, j, :], bank[2 + j][:, 0:N], sil[:, j, :], ALU.mult).then_inc(s["wT_ok"], 1)
            dve.wait_ge(s["su_ok"], dve.snap(e + 1))
            for j in range(2):
                dve.wait_ge(s["wT_ok"], dve.snap(2 * e + (2 + j)))
                dve.tensor_tensor(actT[:, j, :], bank[4][:, 0:N], actT[:, j, :], ALU.mult).then_inc(s["act_ok"], 1)
            for k in range(KC):
                dve.wait_ge(s["dn_ps"], dve.snap(KC * e + (KC + k + 1)))
                dve.wait_ge(s["dn_ok"], dve.snap(KC * e + (k + 1)))
                dve.tensor_tensor(acc[:, k, :], bank[5 + k % 2][:, 0:N], acc[:, k, :], ALU.add).then_inc(s["dn_ok"], 1)
        dve.wait_ge(s["dn_ok"], KC * (E + 1))
        for k in range(KC):
            dve.scalar_tensor_tensor(out=acc[:, k, 0:NP_], in0=acc[:, k, 0:NP_], scalar=adaT[:, 5, 0, k:k + 1],
                                     in1=xT[:, k, 0:NP_], op0=ALU.mult, op1=ALU.add)
            dve.scalar_tensor_tensor(out=acc[:, k, NP_:N], in0=acc[:, k, NP_:N], scalar=adaT[:, 5, 1, k:k + 1],
                                     in1=xT[:, k, NP_:N], op0=ALU.mult, op1=ALU.add).then_inc(s["fin_ok"], 1)
        dve.wait_ge(s["rstd_ok"], 3)
        link(dve.reciprocal(rstdB[:, :], rstdB[:, :]))
        dve.wait_ge(s["x2_sq"], 2 * KC)
        for k in range(KC):
            last = dve.scalar_tensor_tensor(out=acc[:, k, :], in0=acc[:, k, :], scalar=g_fin[:, k:k + 1], in1=rstdB[:, :],
                                            op0=ALU.mult, op1=ALU.mult)
        last.then_inc(s["h2n_ok"], 1)
        for i in range(3):
            for q in range(2):
                dve.wait_ge(s["y_ps"], 2 * i + q + 1)
                dve.tensor_copy(yout[0:TN[i], i, :].rearrange("t (p k) -> t k p", k=KC)[:, 4 * q:4 * q + 4, :],
                                bank[q][0:TN[i], :].rearrange("t (k p) -> t k p", k=4)).then_inc(s["y_ok"], 1)

    ctx.close()


_INS = ["x_prompt", "x_sample", "state_gla", "cache_fox_k", "cache_fox_v", "cache_fox_logf", "c_prompt", "c_sample",
        "w_ada", "b_ada", "g_norm_mix", "g_norm_ffn", "w_in", "w_gla_gk2", "b_gla_gk", "g_gla_out", "b_fox_f", "g_fox_out",
        "w_out", "w_router", "b_router", "w_exp_gate", "w_exp_up", "w_exp_down", "w_sh_gate", "w_sh_up", "w_sh_down", "g_final"]
_OUTS = [(1, NP_, D), (1, NS_, D), (1, 1, GH, GK, GV), (1, 1, GH, GK, GV), (1, 1, NP_, FH, FD), (1, 1, NP_, FH, FD),
         (1, 1, NP_, FH), (1, 1, NS_, FH, FD), (1, 1, NS_, FH, FD), (1, 1, NS_, FH)]


def kernel(**inputs):
    import numpy as _np
    import concourse.bacc as _bacc
    from concourse import mybir as _mybir
    from concourse.bass_utils import run_bass_kernel_spmd as _run

    nc = _bacc.Bacc("TRN2", target_bir_lowering=False, num_devices=1)
    arrays, args = {}, []
    for name in _INS:
        a = _np.ascontiguousarray(inputs[name])
        arrays[f"in_{name}"] = a
        args.append(nc.dram_tensor(f"in_{name}", a.shape, _mybir.dt.from_np(a.dtype), kind="ExternalInput").ap())
    for i, shape in enumerate(_OUTS):
        args.append(nc.dram_tensor(f"out_{i}", shape, F32, kind="ExternalOutput").ap())
    layer(nc, *args)
    r = _run(nc, [arrays], core_ids=[0])
    return tuple(r.results[0][f"out_{i}"] for i in range(len(_OUTS)))
```

```python
from contextlib import ExitStack

import concourse.bass as bass
from concourse import mybir

ALU = mybir.AluOpType
ACT = mybir.ActivationFunctionType
AX = mybir.AxisListType.X
F32 = mybir.dt.float32
BF16 = mybir.dt.bfloat16
F32R = mybir.dt.float32r
I32 = mybir.dt.int32

P = 128
D = 1024
KC = D // P
NP_, NS_ = 256, 32
N = NP_ + NS_
TN = [128, 128, 32]
T0 = [0, 128, 256]
PAST = 512
GH, GK, GV = 4, 64, 128
FH, FD = 8, 64
LR = 16
E, DE = 64, 256
NG, TOPG, TOPK = 8, 4, 8
RSCALE = 2.5
EPS = 1e-6
NEG = -1e30
BLK = 64
CAP = 64
MAXB = -(-N // CAP)
PAIRS = E // 2
C_GQ, C_GK, C_GV, C_GG, C_LR, C_FQ, C_FK, C_FV, C_FF = 0, 256, 512, 1024, 1536, 1552, 2064, 2576, 3088
SLOT = 2048


def layer(nc, x_prompt, x_sample, state_gla, cache_fox_k, cache_fox_v, cache_fox_logf, c_prompt, c_sample,
          w_ada, b_ada, g_norm_mix, g_norm_ffn, w_in, w_gla_gk2, b_gla_gk, g_gla_out, b_fox_f, g_fox_out,
          w_out, w_router, b_router, w_exp_gate, w_exp_up, w_exp_down, w_sh_gate, w_sh_up, w_sh_down, g_final,
          y_prompt, y_sample, st_prompt, st_sample, k_prompt, v_prompt, f_prompt, k_sample, v_sample, f_sample):
    ctx = ExitStack()

    place = {"at": nc.sbuf_base + (-nc.sbuf_base) % 64}

    def sb_at(name, shape, dt, at):
        return nc.alloc_sbuf_tensor_at(name, shape, dt, offset=at)

    def sb(name, shape, dt=F32):
        size = 2 if dt == BF16 else 4
        for s in shape[1:]:
            size *= s
        at = place["at"]
        place["at"] = at + size + (-size) % 64
        return sb_at(name, shape, dt, at)

    ident = sb("ident", [P, P])
    ones = sb("ones", [P, P])
    upper = sb("upper", [P, P])
    lower = sb("lower", [P, P])
    before = sb("before", [P, P])
    glamask = sb("glamask", [P, BLK])
    identb = sb("identb", [P, P], BF16)
    causal = sb("causal", [P, P], BF16)
    epst = sb("epst", [P, 1])
    g_mix = sb("g_mix", [P, KC])
    g_ffn = sb("g_ffn", [P, KC])
    g_fin = sb("g_fin", [P, KC])
    b_adaT = sb("b_adaT", [P, 6, KC])
    adaT = sb("adaT", [P, 6, 2, KC])
    gain1 = sb("gain1", [P, 2, KC])
    gain2 = sb("gain2", [P, 2, KC])
    g_gla = sb("g_gla", [P, 1])
    g_fox = sb("g_fox", [P, 4])
    b_gk = sb("b_gk", [P, 2])
    b_ff = sb("b_ff", [P, FH])
    b_rt = sb("b_rt", [P, E])
    w_gk2 = sb("w_gk2", [LR, 256])
    w_rt = sb("w_rt", [P, KC, E])
    w_lf = sb("w_lf", [P, KC, LR + FH])
    cT = sb("cT", [P, 2, KC])
    scT = sb("scT", [P, KC, 2])
    xT = sb("xT", [P, KC, N])
    rstdB = sb("rstdB", [P, N])
    hT = sb("hT", [P, KC, N])
    base = place["at"]
    RING = base
    NSLOT = 12
    FRONT = 6
    ring = [sb_at(f"ring{i}", [P, SLOT], F32, RING + 8192 * i) for i in range(NSLOT)]
    pair = [sb_at(f"pair{i}", [P, 2 * SLOT], F32, RING + 16384 * i) for i in range(FRONT // 2)]
    place["at"] = RING + 8192 * FRONT
    gqk = sb("gqk", [P, 4, N])
    zt = sb("zt", [P, 16, N])
    o_tok = sb_at("o_tok", [P, 3, D], F32, place["at"] - 4 * 16 * N)
    prob = [sb_at(f"prob{i}", [P, PAST + NS_], F32, place["at"] - 4 * 16 * N + 12288 + 2176 * i) for i in range(2)]
    toks = sb("toks", [P, 4, 3, 512])
    qA = sb("qA", [FD + 2, FH, N])
    kA = sb("kA", [FD + 2, FH, N])
    x_tok = sb_at("x_tok", [P, 3, D], F32, place["at"])
    kS = sb("kS", [FD + 2, FH, PAST])
    cacheK = sb("cacheK", [P, 4, 512])
    probT = [sb_at(f"probT{i}", [P, 256], F32, place["at"] - 8192 + 1024 * i) for i in range(2)]
    cacheV = sb("cacheV", [P, 4, 512])
    sq = sb_at("sq", [P, KC, N], F32, place["at"])
    xn = sb_at("xn", [P, KC, N], F32, place["at"] + 9216)
    g_t = sb("g_t", [P, 2, N])
    kl_tok = sb_at("kl_tok", [P, 3, 256], F32, place["at"])
    g_a = sb("g_a", [P, 2, N])
    g_b = sb("g_b", [P, 2, N])
    g_c = sb("g_c", [P, 2, N])
    qe = sb("qe", [P, 2, N])
    ke = sb("ke", [P, 2, N])
    qb = sb("qb", [P, 2, N])
    kl = sb("kl", [P, 2, N])
    a_t = sb("a_t", [P, 2, 3, 2, BLK])
    states = sb("states", [P, 6, 2, GV])
    dec = sb("dec", [P, 2, 5])
    logf = sb("logf", [P, 3, FH])
    lf_t = sb("lf_t", [P, 3, FH])
    lf_m = sb("lf_m", [P, 3, FH])
    pastf = sb("pastf", [P, 4, FH])
    crow = sb("crow", [FH, 2, N])
    srow = sb("srow", [FH, PAST])
    glr = sb("glr", [LR, N])
    nmax = sb("nmax", [P, 24])
    rsum = sb("rsum", [P, 24])
    rinv = sb("rinv", [P, 24])
    ssq5 = sb("ssq5", [P, 3, 5])
    rs5 = sb("rs5", [P, 3, 5])
    mT = hT
    ada_row = sb("ada_row", [P, 512])
    junk = ada_row
    assert place["at"] <= nc.sbuf_usable_end, (place["at"], nc.sbuf_usable_end)

    place["at"] = RING + 8192 * NSLOT
    acc = sb("acc", [P, KC, N])
    h2T = sb("h2T", [P, KC, N])
    actT = sb("actT", [P, 2, N])
    sil = sb("sil", [P, 2, N])
    sc = sb("sc", [P, 3, E])
    ch = sb("ch", [P, 3, E])
    top = sb("top", [P, NG, 8])
    gs = sb("gs", [P, NG])
    t8 = sb("t8", [P, 8])
    r_a = sb("r_a", [P, E])
    r_b = sb("r_b", [P, E])
    r_c = sb("r_c", [P, E])
    r_n = sb("r_n", [P, 1])
    wrt = sb("wrt", [P, 3, E])
    posm = sb("posm", [P, 3, E + 2])
    w_hl = sb("w_hl", [P, 3, 2, E + 2], F32R)
    iota = sb("iota", [P, MAXB * CAP])
    iota_i = sb("iota_i", [P, MAXB * CAP], I32)
    mcount = sb("mcount", [1, PAIRS])
    nx = sb("nx", [1, PAIRS])
    nxc = sb("nxc", [1, PAIRS])
    table = sb("table", [1, 2 * PAIRS], I32)
    h2hl = sb("h2hl", [P, 5, KC, P], F32R)
    yout = sb_at("yout", [P, 3, D], F32, place["at"] - 4 * 5 * D)
    sq2 = sb_at("sq2", [P, KC, N], F32, place["at"] - 4 * 3 * D)

    sel = sb("sel", [P, 3, 2, CAP], F32R)
    wp = sb("wp", [P, 3, 2, 2], F32R)
    comb = sb("comb", [P, N], F32R)
    ws = sb("ws", [P, 1])
    xg = sb("xg", [P, KC, P])
    silg = sb("silg", [P, DE])
    hid = sb("hid", [P, DE])
    hidT = sb("hidT", [P, 2, P])
    yhi = sb("yhi", [P, D], F32R)
    ylo = sb("ylo", [P, D], F32R)
    assert place["at"] <= nc.sbuf_usable_end, (place["at"], nc.sbuf_usable_end)

    expert_w = [sb_at(f"expert_w{i}", [P, 3, SLOT], F32, RING + 3 * 8192 * i) for i in range(4)]
    psum = nc.alloc_psum_tensor("psum", [P, 8 * 512], F32)
    bank = [psum[:, 512 * i:512 * i + 512] for i in range(8)]

    ada_d = nc.dram_tensor("ada_d", [2, 6, D], F32, kind="Internal").ap()
    crow_d = nc.dram_tensor("crow_d", [2, FH, N], F32, kind="Internal").ap()
    srow_d = nc.dram_tensor("srow_d", [FH, PAST], F32, kind="Internal").ap()

    def sem(name):
        return ctx.enter_context(nc.semaphore(name))

    s = {n: sem(n) for n in (
        "x_in c_in small_in cache_in state_in consts zeros xT_ps xT_ok sq_ok ssq_ps rstd_ok rinv_ok xn_ok sc_ok ada_ps ada_row ada_out adaT_in "
        "gain_ok hT_ok z_ps z_act z_dve narrow_ps glr_ok ff_ok lf_abs lf_ln logf_ok f_out crow_ps crow_ok crow_out rows_in ones_ok "
        "tok_ps tok_act tok_dve kv_out cK_ps cK_act cK_dve gate_ps gate_x gate_abs gate_ln cum_ok gexp_ok gprod_ok klT_ps klT_ok aT_ps aT_ok "
        "upd_ps state_ok st_out go_ps go_ok sc_ps max_ok exp_ok pT_ps pT_ok po_ps po_ok ssq_act rs_act on_ok mT_ps mT_act mT_dve "
        "mix_ps x1_ok d_chain a_chain w_used x2_sq h2n_ok h2_ok rt_ps rt_sc wrt_ok gu_ps sil_ok act_ok "
        "dn_ps acc_ok h2t_ps h2hi_ok h2lo_ok pos_ps pos_ok table_ok iota_ok sel_ok slots_ps ws_ok comb_ok xg_ps xg_ok pgu_ps sl_ok hid_ok hidT_ps hidT_ok yd_ps yhi_ok ylo_ok comb_ps fin_ok y_ps y_ok out_done").split()}
    ring_in = [sem(f"ring_in{i}") for i in range(NSLOT)]

    wa = w_ada[0].rearrange("(p k) n -> p k n", k=KC)
    wi = w_in[0].rearrange("(p k) n -> p k n", k=KC)
    wo = w_out[0].rearrange("(j p) n -> p j n", p=P)
    GROUPS = [C_GQ, C_GV, C_GG, C_FQ, C_FK, C_FV]
    pieces = []
    for k in range(KC):
        pieces.append((wa[:, k, 0:2048], 1))
    for c in GROUPS:
        pieces.append((wi[:, :, c:c + 512], 2))
    for r in (1, 2):
        for k in range(KC):
            pieces.append((wa[:, k, 2048 * r:2048 * r + 2048], 1))
    for j in range(0, 8, 4):
        pieces.append((wo[:, j:j + 4, :], 2))
    at, slots_of, loads, owner, waits_of, turn = 0, [], [0] * NSLOT, {}, [], []
    for n, (_, w) in enumerate(pieces):
        assert w == 1 or at % 2 == 0
        sl = [(at + i) % FRONT for i in range(w)]
        at += w
        waits_of.append(max([owner[q] for q in sl if q in owner], default=-1))
        for q in sl:
            owner[q] = n
        slots_of.append(sl)
        loads[sl[0]] += 1
        turn.append(loads[sl[0]])
    FIRST_WIN, FIRST_R1, FIRST_WO = KC, KC + 6, KC + 6 + 2 * KC
    NPIECE = len(pieces)

    def piece_in(eng, n):
        eng.wait_ge(ring_in[slots_of[n][0]], 16 * turn[n])

    def piece(n):
        return ring[slots_of[n][0]] if pieces[n][1] == 1 else pair[slots_of[n][0] // 2]

    SHARED = 6
    loads[SHARED] += 1
    loads[SHARED + 1] += 1
    loads[SHARED + 2] += 1
    PER = 4

    block = ctx.enter_context(nc.Block())
    small = [
        (g_mix[:, :], g_norm_mix[0].rearrange("(p k) -> p k", k=KC)),
        (g_ffn[:, :], g_norm_ffn[0].rearrange("(p k) -> p k", k=KC)),
        (g_fin[:, :], g_final.rearrange("(p k) -> p k", k=KC)),
        (b_adaT[:, :, :], b_ada[0].rearrange("(m p k) -> p m k", m=6, k=KC)),
        (g_gla[:, :], g_gla_out[0].rearrange("(p o) -> p o", o=1)),
        (g_fox[:, :], g_fox_out[0].rearrange("(j p) -> p j", p=P)),
        (b_gk[:, :], b_gla_gk[0].rearrange("(j p) -> p j", p=P)),
        (b_ff[:, :], b_fox_f[0].partition_broadcast(P)),
        (b_rt[:, :], b_router[0].partition_broadcast(P)),
        (w_gk2[:, :], w_gla_gk2[0]),
        (w_rt[:, :, :], w_router[0].rearrange("(p k) n -> p k n", k=KC)),
        (w_lf[:, :, 0:LR], wi[:, :, C_LR:C_LR + LR]),
        (w_lf[:, :, LR:], wi[:, :, C_FF:C_FF + FH]),
    ]
    SMALL = 16 * len(small)
    NKEY = (128, 256, PAST + NS_)

    def score(u):
        b = 4 + 2 * (u % 2)
        return psum[:, 512 * b:512 * b + 1024]

    def divide(dve, i, link):
        n = TN[i]
        dve.wait_ge(s["po_ps"], 8 * i + 8)
        link(dve.reciprocal(rinv[0:n, 8 * i:8 * i + 8], rsum[0:n, 8 * i:8 * i + 8]))
        dve.tensor_tensor(o_tok[0:n, i, 512:1024].rearrange("t (h d) -> t h d", h=FH),
                          bank[2 + i % 2][0:n, :].rearrange("t (h d) -> t h d", h=FH),
                          rinv[0:n, 8 * i:8 * i + 8].unsqueeze(2).broadcast_to([n, FH, FD]), ALU.mult).then_inc(s["po_ok"], 1)

    def num(eng, v):
        return v if isinstance(v, int) else eng.snap(v)

    def pair_blocks(eng, b):
        b = num(eng, b)
        further = eng.value_load(table[0:1, bass.ds(b, 1)], min_val=0, max_val=MAXB - 1)
        first = eng.value_load(table[0:1, bass.ds(num(eng, b + PAIRS), 1)], min_val=0, max_val=PAIRS * MAXB - 1)
        return further, first

    def each_block(eng, b, body):
        further, first = pair_blocks(eng, b)
        with eng.If(further > 0):
            with eng.Fori(0, further) as j:
                body(eng.snap(first + j), j, False)
        body(eng.snap(first + further), further, True)

    def total_blocks(eng):
        further, first = pair_blocks(eng, PAIRS - 1)
        return eng.snap(first + further + 1)

    def update(b, c):
        w = 2 * (b // 2) % 4 + c
        return bank[2 if b == 4 else b % 2][:, GV * w:GV * w + GV]

    def inter(i, q):
        if i == 2:
            return bank[q][:, 0:256]
        return bank[6 + q][:, 256 * i:256 * i + 256]

    def silu_gate(i):
        return toks[0:TN[i], 1, i, :]

    @block.sync
    def _(sp):
        for i, (src, tn) in enumerate(((x_prompt[0, 0:128], 128), (x_prompt[0, 128:256], 128), (x_sample[0], 32))):
            sp.dma_start(x_tok[0:tn, i, :], src).then_inc(s["x_in"], 16)
        for n, (src, w) in enumerate(pieces):
            if waits_of[n] >= 0:
                sp.wait_ge(s["w_used"], waits_of[n] + 1)
            dst = piece(n)[:, :]
            if w == 2:
                dst = dst.rearrange("p (k n) -> p k n", n=src.shape[2])
            sp.dma_start(dst, src).then_inc(ring_in[slots_of[n][0]], 16)
        sp.wait_ge(s["x1_ok"], KC)
        sp.wait_ge(s["kv_out"], 96)
        sp.wait_ge(s["st_out"], 64)
        sp.wait_ge(s["f_out"], 32)
        for q, w, k in ((0, w_sh_gate, KC), (1, w_sh_up, KC), (2, w_sh_down, 2)):
            sp.dma_start(ring[SHARED + q][:, :], w[0].rearrange("(p k) n -> p (k n)", k=k)).then_inc(ring_in[SHARED + q], 16)

        GATE_UP, DOWN = ((0, w_exp_gate, KC), (1, w_exp_up, KC)), ((2, w_exp_down, 2),)

        def expert(u, e, parts):
            for q, w, k in parts:
                src = w[0].rearrange("e (p k) n -> e p (k n)", k=k)[bass.ds(e, 1)].rearrange("e p n -> (e p) n")
                sp.dma_start(expert_w[u][:, q, :], src).then_inc(ring_in[3 * u + q], 16)

        for u in range(4):
            sp.wait_ge(s["w_used"], NPIECE + (1 if u == 2 else 0))
            expert(u, u, GATE_UP + DOWN)
        sp.wait_ge(s["table_ok"], 1)
        with sp.Fori(1, PAIRS // 2) as it:
            for u in range(2):
                further, first = pair_blocks(sp, it * 2 + (u - 2))
                done = sp.snap(first + further + 1)
                ab = [sp.snap(it * 4 + (2 * u + x)) for x in range(2)]
                sp.wait_ge(s["pgu_ps"], done)
                for x in range(2):
                    expert(2 * u + x, ab[x], GATE_UP)
                sp.wait_ge(s["yd_ps"], done)
                for x in range(2):
                    expert(2 * u + x, ab[x], DOWN)

    @block.scalar
    def _(act):
        act.dma_start(cT[:, 0, :], c_prompt[0].rearrange("(p k) -> p k", k=KC)).then_inc(s["c_in"], 16)
        act.dma_start(cT[:, 1, :], c_sample[0].rearrange("(p k) -> p k", k=KC)).then_inc(s["c_in"], 16)
        with nc.allow_non_contiguous_dma(reason="vectors of a few hundred elements"):
            for dst, src in small:
                act.dma_start(dst, src).then_inc(s["small_in"], 16)
        act.dma_start(cacheK[:, :, :], cache_fox_k[0, 0].rearrange("(j p) h d -> p j (h d)", p=P)).then_inc(s["cache_in"], 16)
        act.dma_start(cacheV[:, :, :], cache_fox_v[0, 0].rearrange("(j p) h d -> p j (h d)", p=P)).then_inc(s["cache_in"], 16)
        act.dma_start(pastf[:, :, :], cache_fox_logf[0, 0].rearrange("(j p) h -> p j h", p=P)).then_inc(s["cache_in"], 16)
        for c in range(2):
            act.dma_start(states[:, 4, c, :], state_gla[0, 0, 2 * c:2 * c + 2].rearrange("h k v -> (h k) v")).then_inc(s["state_in"], 16)
        act.wait_ge(s["c_in"], 32)
        act.activation(scT[:, :, :].rearrange("p k g -> p g k"), cT[:, :, :], ACT.Silu).then_inc(s["sc_ok"], 1)
        for k in range(KC):
            act.wait_ge(s["xT_ok"], k + 1)
            act.activation(sq[:, k, :], xT[:, k, :], ACT.Square).then_inc(s["sq_ok"], 1)
        act.wait_ge(s["consts"], 1)
        act.wait_ge(s["ssq_ps"], 1)
        act.activation(rstdB[:, :], bank[6][:, 0:N], ACT.Sqrt, bias=epst[:, 0:1], scale=1.0 / D).then_inc(s["rstd_ok"], 1)

        def ada_rows(r):
            act.wait_ge(s["ada_ps"], r + 1)
            if r:
                act.wait_ge(s["ada_out"], 64 * r)
            for j in range(4):
                act.copy(ada_row[32 * j:32 * j + 2, :], bank[5][32 * j:32 * j + 2, :]).then_inc(s["ada_row"], 1)
            act.wait_ge(s["ada_row"], 4 * r + 4)
            for j in range(4):
                g = 4 * r + j
                act.dma_start(ada_d[:, g // 2, 512 * (g % 2):512 * (g % 2) + 512],
                              ada_row[32 * j:32 * j + 2, :]).then_inc(s["ada_out"], 16)
            act.wait_ge(s["ada_out"], 64 * (r + 1))
            for m in (2 * r, 2 * r + 1):
                act.dma_start(adaT[:, m, :, :], ada_d[:, m].rearrange("g (p k) -> p g k", k=KC)).then_inc(s["adaT_in"], 16)

        ada_rows(0)
        act.wait_ge(s["gain_ok"], 2)
        act.wait_ge(s["xn_ok"], 1)
        for k in range(KC):
            act.activation(hT[:, k, 0:NP_], xn[:, k, 0:NP_], ACT.Identity, bias=adaT[:, 0, 0, k:k + 1],
                           scale=gain1[:, 0, k:k + 1]).then_inc(s["hT_ok"], 1)
        for c in range(1, 24, 2):
            act.wait_ge(s["z_ps"], c + 1)
            b = bank[c % 4]
            if c < 2:
                last = act.mul(gqk[:, c, :], b[:, 0:N], GK ** -0.5)
            elif c < 4:
                last = act.copy(gqk[:, c, :], b[:, 0:N])
            elif 12 <= c < 16:
                act.mul(qA[0:FD, 2 * (c - 12), :], b[0:FD, 0:N], FD ** -0.5)
                last = act.mul(qA[0:FD, 2 * (c - 12) + 1, :], b[FD:P, 0:N], FD ** -0.5)
            elif 16 <= c < 20:
                act.copy(kA[0:FD, 2 * (c - 16), :], b[0:FD, 0:N])
                act.copy(kA[0:FD, 2 * (c - 16) + 1, :], b[FD:P, 0:N])
                last = act.copy(zt[:, 8 + c - 16, :], b[:, 0:N])
            else:
                last = act.copy(zt[:, c - 4 if c < 12 else c - 8, :], b[:, 0:N])
            last.then_inc(s["z_act"], 1)
        act.wait_ge(s["narrow_ps"], 1)
        act.copy(glr[:, :], bank[4][0:LR, 0:N]).then_inc(s["glr_ok"], 1)
        act.wait_ge(s["lf_abs"], 1)
        act.activation(logf[:, :, :], lf_t[:, :, :], ACT.Exp, scale=-1.0).then_inc(s["a_chain"], 1)
        act.wait_ge(s["a_chain"], 1)
        act.activation(lf_t[:, :, :], logf[:, :, :], ACT.Ln, bias=1.0).then_inc(s["lf_ln"], 1)
        act.wait_ge(s["gate_abs"], 1)
        act.activation(g_c[:, :, :], g_a[:, :, :], ACT.Exp, scale=-1.0).then_inc(s["a_chain"], 1)
        act.wait_ge(s["a_chain"], 2)
        act.activation(g_a[:, :, :], g_c[:, :, :], ACT.Ln, bias=1.0).then_inc(s["gate_ln"], 1)
        act.wait_ge(s["cum_ok"], 4)
        act.activation(qe[:, :, :], g_a[:, :, :], ACT.Exp).then_inc(s["gexp_ok"], 1)
        act.activation(ke[:, :, :], g_a[:, :, :], ACT.Exp, scale=-1.0).then_inc(s["gexp_ok"], 1)
        act.activation(qb[:, :, :], g_t[:, :, :], ACT.Exp).then_inc(s["gexp_ok"], 1)
        act.activation(kl[:, :, :], g_b[:, :, :], ACT.Exp).then_inc(s["gexp_ok"], 1)
        act.activation(dec[:, :, 0:4], g_t[:, :, BLK - 1:NP_:BLK], ACT.Exp).then_inc(s["gexp_ok"], 1)
        act.activation(dec[:, :, 4:5], g_t[:, :, N - 1:N], ACT.Exp).then_inc(s["gexp_ok"], 1)
        for c in range(4):
            act.wait_ge(s["cK_ps"], c + 1)
            act.copy(kS[0:FD, 2 * c + 1, :], bank[c][FD:P, :]).then_inc(s["cK_act"], 1)
        for i in range(3):
            act.wait_ge(s["tok_ps"], 3 + i + 1)
            act.activation(silu_gate(i), bank[4 + (3 + i) % 4][0:TN[i], :], ACT.Silu).then_inc(s["tok_act"], 1)
        for u in range(24):
            i = u // 8
            act.wait_ge(s["max_ok"], u + 1)
            if u >= 2:
                act.wait_ge(s["pT_ps"], u - 1)
            act.activation(prob[u % 2][0:TN[i], 0:NKEY[i]], score(u)[0:TN[i], 0:NKEY[i]], ACT.Exp, bias=nmax[0:TN[i], u:u + 1],
                           accum_out=rsum[0:TN[i], u:u + 1]).then_inc(s["exp_ok"], 1)
        ada_rows(1)
        ada_rows(2)
        for i in range(3):
            act.wait_ge(s["go_ok"], i + 1)
            act.wait_ge(s["po_ok"], i + 1)
            if i == 0:
                act.wait_ge(s["ada_out"], 64 * 3)
                act.wait_ge(s["zeros"], 2)
            for j in range(5):
                lo, hi = (GV * j, GV * j + GV) if j < 4 else (512, 1024)
                if i or j:
                    act.wait_ge(s["ssq_act"], 5 * i + j)
                act.activation(junk[0:TN[i], 0:hi - lo], o_tok[0:TN[i], i, lo:hi], ACT.Square,
                               accum_out=ssq5[0:TN[i], i, j:j + 1]).then_inc(s["ssq_act"], 1)
        act.wait_ge(s["ssq_act"], 15)
        act.activation(rs5[:, :, 0:4], ssq5[:, :, 0:4], ACT.Sqrt, bias=epst[:, 0:1], scale=1.0 / GV).then_inc(s["rs_act"], 1)
        act.activation(rs5[:, :, 4:5], ssq5[:, :, 4:5], ACT.Sqrt, bias=epst[:, 0:1], scale=1.0 / 512).then_inc(s["rs_act"], 1)
        for j in range(0, 8, 2):
            act.wait_ge(s["mT_ps"], j + 1)
            act.mul(mT[:, j, :], bank[j % 4][:, 0:N], g_gla[:, 0:1] if j < 4 else g_fox[:, j - 4:j - 3]).then_inc(s["mT_act"], 1)
        for k in range(KC):
            act.wait_ge(s["x1_ok"], k + 1 if k < KC - 1 else KC)
            if k == 0:
                act.wait_ge(s["x1_ok"], KC)
            act.activation(sq2[:, k, :], xT[:, k, :], ACT.Square).then_inc(s["x2_sq"], 1)
        act.wait_ge(s["ssq_ps"], 2)
        act.activation(rstdB[:, :], bank[6][:, 0:N], ACT.Sqrt, bias=epst[:, 0:1], scale=1.0 / D).then_inc(s["rstd_ok"], 1)
        act.wait_ge(s["h2n_ok"], 1)
        for k in range(KC):
            act.activation(h2T[:, k, 0:NP_], h2T[:, k, 0:NP_], ACT.Identity, bias=adaT[:, 3, 0, k:k + 1],
                           scale=gain2[:, 0, k:k + 1]).then_inc(s["h2_ok"], 1)
        act.wait_ge(s["rt_ps"], 1)
        for i in range(3):
            act.activation(sc[0:TN[i], i, :], bank[5][0:TN[i], E * i:E * i + E], ACT.Sigmoid).then_inc(s["rt_sc"], 1)
        act.wait_ge(s["gu_ps"], 1)
        for j in range(2):
            act.activation(sil[:, j, :], bank[j][:, 0:N], ACT.Silu).then_inc(s["sil_ok"], 1)
        for q in range(6):
            i = q // 2
            act.wait_ge(s["h2t_ps"], q + 1)
            act.copy(h2hl[0:TN[i], 2 * i, 4 * (q % 2):4 * (q % 2) + 4, :], bank[4 + q % 2][0:TN[i], :].rearrange("t (k p) -> t k p", k=4)).then_inc(s["h2hi_ok"], 1)
        act.wait_ge(s["table_ok"], 1)

        def gathered(n):
            act.wait_ge(s["xg_ps"], num(act, n + 1))
            for q in range(2):
                last = act.copy(xg[:, 4 * q:4 * q + 4, :], bank[q][:, :].rearrange("p (k n) -> p k n", k=4))
            last.then_inc(s["xg_ok"], 1)

        def act_block(n, j, last):
            act.wait_ge(s["pgu_ps"], num(act, n + 1))
            act.activation(silg[:, :], bank[3][:, 0:DE], ACT.Silu).then_inc(s["sl_ok"], 1)
            act.wait_ge(s["hidT_ps"], num(act, n + 1))
            act.copy(hidT[:, :, :], bank[4][:, 0:2 * P].rearrange("p (j n) -> p j n", j=2)).then_inc(s["hidT_ok"], 1)
            gathered(n + 1)
            act.wait_ge(s["yd_ps"], num(act, n + 1))
            act.copy(yhi[:, :], psum[:, 4 * 512:6 * 512]).then_inc(s["yhi_ok"], 1)

        gathered(0)
        with act.Fori(0, PAIRS // 2) as it:
            for u in range(2):
                each_block(act, it * 2 + u, act_block)
        for k in range(KC):
            act.wait_ge(s["fin_ok"], k + 1)
            act.activation(sq2[:, k, :], acc[:, k, :], ACT.Square).then_inc(s["x2_sq"], 1)
        act.wait_ge(s["ssq_ps"], 3)
        act.activation(rstdB[:, :], bank[6][:, 0:N], ACT.Sqrt, bias=epst[:, 0:1], scale=1.0 / D).then_inc(s["rstd_ok"], 1)
        for i in range(3):
            dst = y_sample[0] if i == 2 else y_prompt[0, 128 * i:128 * i + 128]
            act.wait_ge(s["y_ok"], 2 * i + 2)
            act.dma_start(dst, yout[0:TN[i], i, :]).then_inc(s["out_done"], 16)
        act.wait_ge(s["out_done"], 48)

    @block.gpsimd
    def _(pool):
        z = s["zeros"]
        pool.memset(ident[:, :], 0.0).then_inc(z, 1)
        pool.memset(ssq5[:, :, :], 1.0).then_inc(z, 1)
        pool.memset(identb[:, :], 0.0).then_inc(z, 1)
        pool.memset(ones[:, :], 1.0).then_inc(z, 1)
        pool.memset(causal[:, :], 0.0).then_inc(z, 1)
        pool.memset(epst[:, :], EPS).then_inc(z, 1)
        pool.wait_ge(z, 6)
        for t in (ident, identb):
            pool.affine_select(out=t[:, :], in_=t[:, :], compare_op=ALU.not_equal, fill=1.0, base=0,
                               pattern=[[-1, P]], channel_multiplier=1).then_inc(z, 1)
        pool.affine_select(out=upper[:, :], in_=ones[:, :], compare_op=ALU.is_ge, fill=0.0, base=0,
                           pattern=[[1, P]], channel_multiplier=-1).then_inc(z, 1)
        pool.affine_select(out=lower[:, :], in_=ones[:, :], compare_op=ALU.is_gt, fill=0.0, base=0,
                           pattern=[[-1, P]], channel_multiplier=1).then_inc(z, 1)
        pool.wait_ge(z, 10)
        pool.affine_select(out=glamask[0:BLK, :], in_=ones[0:BLK, 0:BLK], compare_op=ALU.is_ge, fill=0.0, base=0,
                           pattern=[[1, BLK]], channel_multiplier=-1).then_inc(z, 1)
        pool.wait_ge(z, 11)
        pool.affine_select(out=before[:, :], in_=ones[:, :], compare_op=ALU.is_gt, fill=0.0, base=0,
                           pattern=[[1, P]], channel_multiplier=-1).then_inc(z, 1)
        pool.wait_ge(z, 12)
        pool.affine_select(out=glamask[BLK:P, :], in_=ones[BLK:P, 0:BLK], compare_op=ALU.is_ge, fill=0.0, base=0,
                           pattern=[[1, BLK]], channel_multiplier=-1).then_inc(z, 1)
        pool.wait_ge(z, 13)
        pool.affine_select(out=causal[:, :], in_=causal[:, :], compare_op=ALU.is_ge, fill=NEG, base=0,
                           pattern=[[-1, P]], channel_multiplier=1).then_inc(s["consts"], 1)
        pool.wait_ge(s["consts"], 1)
        pool.memset(qA[FD:FD + 2, :, :], 1.0).then_inc(s["ones_ok"], 1)
        pool.wait_ge(s["ones_ok"], 1)
        pool.memset(kA[FD:FD + 2, :, :], 1.0).then_inc(s["ones_ok"], 1)
        pool.wait_ge(s["ones_ok"], 2)
        pool.wait_ge(s["xT_ps"], 8)
        pool.memset(kS[FD:FD + 2, :, :], 1.0).then_inc(s["ones_ok"], 1)
        pool.wait_ge(s["ones_ok"], 3)
        pool.memset(a_t[:, :, :, :, :], 0.0).then_inc(z, 1)
        pool.wait_ge(s["logf_ok"], 1)
        pool.dma_start(f_prompt[0, 0].rearrange("(i p) h -> p i h", p=P), logf[:, 0:2, :]).then_inc(s["f_out"], 16)
        pool.dma_start(f_sample[0, 0], logf[0:NS_, 2, :]).then_inc(s["f_out"], 16)
        pool.wait_ge(s["crow_ok"], 3)
        pool.dma_start(crow_d.rearrange("a h n -> h a n"), crow[:, :, :]).then_inc(s["crow_out"], 16)
        pool.dma_start(srow_d, srow[:, :]).then_inc(s["crow_out"], 16)
        pool.wait_ge(s["crow_out"], 32)
        pool.wait_ge(s["ones_ok"], 3)
        pool.dma_start(qA[FD + 1:FD + 2, :, :], crow_d[0:1]).then_inc(s["rows_in"], 16)
        pool.dma_start(kA[FD:FD + 1, :, :], crow_d[1:2]).then_inc(s["rows_in"], 16)
        pool.dma_start(kS[FD:FD + 1, :, :], srow_d.rearrange("(o h) n -> o h n", o=1)).then_inc(s["rows_in"], 16)
        pool.wait_ge(s["state_ok"], 10)
        for c in range(2):
            pool.dma_start(st_prompt[0, 0, 2 * c:2 * c + 2].rearrange("h k v -> (h k) v"), states[:, 3, c, :]).then_inc(s["st_out"], 16)
            pool.dma_start(st_sample[0, 0, 2 * c:2 * c + 2].rearrange("h k v -> (h k) v"), states[:, 5, c, :]).then_inc(s["st_out"], 16)
        pool.wait_ge(s["tok_dve"], 9)
        for q, (kp, ks_) in enumerate(((k_prompt, k_sample), (v_prompt, v_sample))):
            for i in range(2):
                pool.dma_start(kp[0, 0, 128 * i:128 * i + 128].rearrange("t h d -> t (h d)"), toks[:, 2 + q, i, :]).then_inc(s["kv_out"], 16)
            pool.dma_start(ks_[0, 0].rearrange("t h d -> t (h d)"), toks[0:NS_, 2 + q, 2, :]).then_inc(s["kv_out"], 16)
        pool.wait_ge(s["x1_ok"], KC)
        pool.wait_ge(s["kv_out"], 96)
        pool.iota(iota_i[:, :], pattern=[[1, MAXB * CAP]], base=0, channel_multiplier=0).then_inc(s["iota_ok"], 1)
        pool.wait_ge(s["iota_ok"], 1)
        pool.tensor_copy(iota[:, :], iota_i[:, :]).then_inc(s["iota_ok"], 1)
        pool.wait_ge(s["iota_ok"], 2)
        pool.memset(posm[:, :, :], -1.0).then_inc(s["iota_ok"], 1)
        pool.wait_ge(s["iota_ok"], 3)
        pool.memset(w_hl[:, :, :, :].bitcast(F32), 0.0).then_inc(s["iota_ok"], 1)
        pool.wait_ge(s["iota_ok"], 4)
        pool.wait_ge(s["x2_sq"], KC)
        pool.wait_ge(s["ssq_ps"], 2)
        pool.memset(h2hl[:, 4, :, :].bitcast(F32), 0.0).then_inc(s["iota_ok"], 1)
        pool.wait_ge(s["st_out"], 64)
        pool.wait_ge(s["f_out"], 32)

    @block.tensor
    def _(pe):
        mm, tr = nc.tensor.matmul, nc.tensor.transpose
        pe.wait_ge(s["consts"], 1)
        pe.wait_ge(s["x_in"], 48)
        for k in range(KC):
            if k >= 4:
                pe.wait_ge(s["xT_ok"], k - 3)
            for i in range(3):
                last = tr(bank[k % 4][:, T0[i]:T0[i] + TN[i]], x_tok[0:TN[i], i, k::KC], ident[0:TN[i], 0:TN[i]])
            last.then_inc(s["xT_ps"], 1)

        def sumsq(src, sem_, n0):
            for k in range(KC):
                pe.wait_ge(sem_, n0 + k + 1)
                last = mm(bank[6][:, 0:N], ones[:, :], src[:, k, :], start=k == 0, stop=k == KC - 1)
            last.then_inc(s["ssq_ps"], 1)

        sumsq(sq, s["sq_ok"], 0)

        def ada(r):
            for k in range(KC):
                n = k if r == 0 else FIRST_R1 + KC * (r - 1) + k
                piece_in(pe, n)
                for j in range(4):
                    last = mm(bank[5][32 * j:32 * j + 2, :], scT[:, k, :], piece(n)[:, 512 * j:512 * j + 512],
                              start=k == 0, stop=k == KC - 1, tile_position=(0, 32 * j))
                last.then_inc(s["w_used"], 1)
            pe.wait_ge(s["w_used"], FIRST_WIN if r == 0 else FIRST_R1 + KC * r)
            mm(bank[7][0:2, 0:2], ident[:, 0:2], ident[:, 0:2], start=True, stop=True).then_inc(s["ada_ps"], 1)

        pe.wait_ge(s["sc_ok"], 1)
        ada(0)

        pe.wait_ge(s["hT_ok"], 24)
        for g in range(6):
            piece_in(pe, FIRST_WIN + g)
            w = piece(FIRST_WIN + g)[:, :].rearrange("p (k n) -> p k n", k=KC)
            for q in range(4):
                c = 4 * g + q
                if c >= 4:
                    pe.wait_ge(s["z_act" if c % 2 else "z_dve"], (c - 4) // 2 + 1)
                for k in range(KC):
                    last = mm(bank[c % 4][:, 0:N], w[:, k, P * q:P * q + P], hT[:, k, :], start=k == 0, stop=k == KC - 1)
                last.then_inc(s["z_ps"], 1)
            pe.wait_ge(s["z_ps"], 4 * g + 4)
            mm(bank[7][0:2, 0:2], ident[:, 0:2], ident[:, 0:2], start=True, stop=True).then_inc(s["w_used"], 1)
        pe.wait_ge(s["small_in"], SMALL)
        for k in range(KC):
            mm(bank[4][0:LR, 0:N], w_lf[:, k, 0:LR], hT[:, k, :], start=k == 0, stop=k == KC - 1)
        for i in range(3):
            for k in range(KC):
                last = mm(bank[5][0:TN[i], FH * i:FH * i + FH], hT[:, k, T0[i]:T0[i] + TN[i]], w_lf[:, k, LR:],
                          start=k == 0, stop=k == KC - 1)
        last.then_inc(s["narrow_ps"], 1)
        pe.wait_ge(s["z_act"], 12)
        pe.wait_ge(s["z_dve"], 12)
        pe.wait_ge(s["cache_in"], 48)
        for c in range(4):
            for j in range(4):
                last = tr(bank[c][:, P * j:P * j + P], cacheK[:, j, P * c:P * c + P], ident[:, :])
            last.then_inc(s["cK_ps"], 1)
        pe.wait_ge(s["glr_ok"], 1)
        pe.wait_ge(s["ff_ok"], 1)
        for c in range(2):
            last = mm(bank[4 + c][:, 0:N], w_gk2[:, P * c:P * c + P], glr[:, :], start=True, stop=True)
        last.then_inc(s["gate_ps"], 1)
        pe.wait_ge(s["logf_ok"], 1)
        cb = bank[6]
        mm(cb[0:FH, 0:128], logf[:, 0, :], upper[:, :], start=True, stop=True)
        mm(cb[0:FH, 128:256], logf[:, 0, :], ones[:, :], start=True, stop=False)
        mm(cb[0:FH, 128:256], logf[:, 1, :], upper[:, :], start=False, stop=True)
        mm(cb[0:FH, 256:N], logf[0:NS_, 2, :], upper[0:NS_, 0:NS_], start=True, stop=True).then_inc(s["crow_ps"], 1)
        for j in range(4):
            for t in range(j, 4):
                last = mm(bank[7][0:FH, P * j:P * j + P], pastf[:, t, :], (lower if t == j else ones)[:, :],
                          start=t == j, stop=t == 3)
        last.then_inc(s["crow_ps"], 1)
        pe.wait_ge(s["gate_x"], 1)
        pe.wait_ge(s["crow_ok"], 3)
        for q in range(12):
            kind, i = q // 3, q % 3
            if q >= 4:
                kb, ib = (q - 4) // 3, (q - 4) % 3
                pe.wait_ge(s["tok_act" if kb == 1 else "tok_dve"], ib + 1 + (0 if kb < 2 else 3 * (kb - 1)))
            for j in range(4):
                last = tr(bank[4 + q % 4][0:TN[i], P * j:P * j + P], zt[:, 4 * kind + j, T0[i]:T0[i] + TN[i]], ident[:, :])
            last.then_inc(s["tok_ps"], 1)
        pe.wait_ge(s["tok_dve"], 9)
        pe.wait_ge(s["tok_act"], 3)
        pe.wait_ge(s["gprod_ok"], 4)
        for i in range(3):
            for c in range(2):
                o = 256 * (i % 2) + P * c
                last = tr(bank[4 + i // 2][0:TN[i], o:o + P], kl[:, c, T0[i]:T0[i] + TN[i]], ident[:, :])
        last.then_inc(s["klT_ps"], 1)
        def blocks():
            for b in range(5):
                i, pb, n = b // 2, 64 * (b % 2), BLK if b < 4 else NS_
                yield b, i, pb, n
        for b, i, pb, n in blocks():
            for h in range(GH):
                r, c = 64 * (h % 2), h // 2
                t0 = T0[i] + pb
                o = P * i + BLK * c
                last = mm(bank[6 + h % 2][pb:pb + n, o:o + n], ke[r:r + GK, c, t0:t0 + n], qe[r:r + GK, c, t0:t0 + n],
                          start=True, stop=True)
        last.then_inc(s["aT_ps"], 1)
        pe.wait_ge(s["cK_act"], 4)
        pe.wait_ge(s["cK_dve"], 4)
        pe.wait_ge(s["klT_ok"], 1)
        for b, i, pb, n in blocks():
            for h in range(GH):
                r, c = 64 * (h % 2), h // 2
                last = mm(update(b, c)[r:r + GK, :], kl_tok[pb:pb + n, i, GK * h:GK * h + GK],
                          toks[pb:pb + n, 0, i, GV * h:GV * h + GV], start=True, stop=True)
        last.then_inc(s["upd_ps"], 1)
        pe.wait_ge(s["aT_ok"], 4)
        pe.wait_ge(s["state_ok"], 10)
        for b, i, pb, n in blocks():
            for h in range(GH):
                r, c = 64 * (h % 2), h // 2
                t0 = T0[i] + pb
                mm(bank[3 + i][pb:pb + n, GV * h:GV * h + GV], a_t[pb:pb + n, h % 2, i, c, 0:n],
                   toks[pb:pb + n, 0, i, GV * h:GV * h + GV], start=True, stop=True)
                if b:
                    last = mm(inter(i, h % 2)[pb:pb + n, GV * c:GV * c + GV], qb[r:r + GK, c, t0:t0 + n],
                              states[r:r + GK, b - 1 if b < 4 else 4, c, :], start=True, stop=True)
            if b % 2 or b == 4:
                last.then_inc(s["go_ps"], 1)
        pe.wait_ge(s["rows_in"], 48)

        def scores(u):
            i, h = u // 8, u % 8
            if u < 2:
                pe.wait_ge(s["go_ok"], 3)
            else:
                pe.wait_ge(s["exp_ok"], u - 1)
            q = qA[:, h, T0[i]:T0[i] + TN[i]]
            out = score(u)[0:TN[i]]
            if i < 2:
                d = P * i
                if i:
                    mm(out[:, 0:P], q, kA[:, h, 0:P], start=True, stop=True)
                mm(out[:, d:d + P], q, kA[:, h, d:d + P], start=True, stop=False)
                last = mm(out[:, d:d + P], identb[:, :], causal[:, :], start=False, stop=True)
            else:
                mm(out[:, 0:PAST], q, kS[:, h, :], start=True, stop=True)
                mm(out[:, PAST:PAST + NS_], q, kA[:, h, NP_:N], start=True, stop=False)
                last = mm(out[:, PAST:PAST + NS_], identb[0:NS_, 0:NS_], causal[0:NS_, 0:NS_], start=False, stop=True)
            last.then_inc(s["sc_ps"], 1)

        def transposed(u):
            i, n = u // 8, TN[u // 8]
            pe.wait_ge(s["exp_ok"], u + 1)
            if u >= 2:
                pe.wait_ge(s["pT_ok"], u - 1)
            for t in range((NKEY[i] + P - 1) // P):
                w = min(P, NKEY[i] - P * t)
                last = tr(bank[u % 2][0:w, n * t:n * t + n], prob[u % 2][0:n, P * t:P * t + w], ident[0:n, 0:n])
            last.then_inc(s["pT_ps"], 1)

        def values(u):
            i, h, n = u // 8, u % 8, TN[u // 8]
            pe.wait_ge(s["pT_ok"], u + 1)
            if h == 0 and i == 2:
                pe.wait_ge(s["po_ok"], 1)
            nt = (NKEY[i] + P - 1) // P
            for t in range(nt):
                w = min(P, NKEY[i] - P * t)
                v = cacheV[:, t, FD * h:FD * h + FD] if i == 2 and t < 4 else toks[0:w, 3, 2 if i == 2 else t, FD * h:FD * h + FD]
                last = mm(bank[2 + i % 2][0:n, FD * h:FD * h + FD], probT[u % 2][0:w, n * t:n * t + n], v, start=t == 0, stop=t == nt - 1)
            last.then_inc(s["po_ps"], 1)

        scores(0)
        for u in range(24):
            if u + 1 < 24:
                scores(u + 1)
            transposed(u)
            if u:
                values(u - 1)
        values(23)
        pe.wait_ge(s["exp_ok"], 24)
        ada(1)
        pe.wait_ge(s["ada_row"], 8)
        ada(2)
        pe.wait_ge(s["po_ok"], 3)
        for j in range(8):
            if j >= 4:
                pe.wait_ge(s["mT_dve" if j % 2 else "mT_act"], (j - 4) // 2 + 1)
            for i in range(3):
                pe.wait_ge(s["on_ok"], 3)
                last = tr(bank[j % 4][:, T0[i]:T0[i] + TN[i]], o_tok[0:TN[i], i, P * j:P * j + P], ident[0:TN[i], 0:TN[i]])
            last.then_inc(s["mT_ps"], 1)
        pe.wait_ge(s["mT_act"], 4)
        pe.wait_ge(s["mT_dve"], 4)
        piece_in(pe, FIRST_WO)
        piece_in(pe, FIRST_WO + 1)
        for k in range(KC):
            if k >= 4:
                pe.wait_ge(s["x1_ok"], k - 3)
            for j in range(8):
                w = piece(FIRST_WO + j // 4)[:, :].rearrange("p (j n) -> p j n", j=4)[:, j % 4, k::KC]
                last = mm(bank[k % 4][:, 0:N], w, mT[:, j, :], start=j == 0, stop=j == 7)
            last.then_inc(s["mix_ps"], 1)
        pe.wait_ge(s["mix_ps"], KC)
        for _ in range(2):
            mm(bank[7][0:2, 0:2], ident[:, 0:2], ident[:, 0:2], start=True, stop=True).then_inc(s["w_used"], 1)
        sumsq(sq2, s["x2_sq"], 0)
        pe.wait_ge(s["h2_ok"], 16)
        for i in range(3):
            for k in range(KC):
                last = mm(bank[5][0:TN[i], E * i:E * i + E], h2T[:, k, T0[i]:T0[i] + TN[i]], w_rt[:, k, :],
                          start=k == 0, stop=k == KC - 1)
        last.then_inc(s["rt_ps"], 1)

        def gate_up(q0):
            for j in range(2):
                for w in range(2):
                    wt = ring[q0 + w][:, :].rearrange("p (k n) -> p k n", k=KC)
                    for k in range(KC):
                        last = mm(bank[j + 2 * w][:, 0:N], wt[:, k, j::2], h2T[:, k, :], start=k == 0, stop=k == KC - 1)
            last.then_inc(s["gu_ps"], 1)

        def down(q0, wait_dn):
            wt = ring[q0 + 2][:, :].rearrange("p (j n) -> p j n", j=2)
            for k in range(KC):
                wait_dn(k)
                for j in range(2):
                    last = mm(bank[5 + k % 2][:, 0:N], wt[:, j, k::KC], actT[:, j, :], start=j == 0, stop=j == 1)
                last.then_inc(s["dn_ps"], 1)

        for q in range(3):
            pe.wait_ge(ring_in[SHARED + q], 16)
        gate_up(SHARED)
        pe.wait_ge(s["rt_sc"], 3)
        for q in range(6):
            i = q // 2
            if q >= 2:
                pe.wait_ge(s["h2lo_ok"], q - 1)
            for k in range(4):
                last = tr(bank[4 + q % 2][0:TN[i], P * k:P * k + P], h2T[:, 4 * (q % 2) + k, T0[i]:T0[i] + TN[i]], ident[:, :])
            last.then_inc(s["h2t_ps"], 1)
        pe.wait_ge(s["act_ok"], 2)
        pe.wait_ge(s["rstd_ok"], 2)
        pe.wait_ge(s["h2lo_ok"], 6)
        down(SHARED, lambda k: pe.wait_ge(s["acc_ok"], k - 1) if k >= 2 else None)
        pe.wait_ge(s["dn_ps"], KC)
        mm(bank[7][0:2, 0:2], ident[:, 0:2], ident[:, 0:2], start=True, stop=True).then_inc(s["w_used"], 1)
        pe.wait_ge(s["wrt_ok"], 3)
        pb = bank[4]
        for i in range(3):
            n = TN[i]
            for j in range(i):
                mm(pb[0:n, E * i:E * i + E], ones[:, 0:n], ch[:, j, :], start=j == 0, stop=False)
            mm(pb[0:n, E * i:E * i + E], before[0:n, 0:n], ch[0:n, i, :], start=i == 0, stop=True)
        for i in range(3):
            last = mm(pb[0:1, 3 * E:4 * E], ones[0:TN[i], 0:1], ch[0:TN[i], i, :], start=i == 0, stop=i == 2)
        last.then_inc(s["pos_ps"], 1)
        pe.wait_ge(s["acc_ok"], KC)
        pe.wait_ge(s["iota_ok"], 5)
        pe.wait_ge(s["table_ok"], 1)

        def gather(n, between=None):
            pe.wait_ge(s["sel_ok"], num(pe, n + 1))
            for k in range(KC):
                for q in range(5):
                    last = mm(bank[k // 4][:, P * (k % 4):P * (k % 4) + P], h2hl[:, q, k, :], sel[:, q // 2, :, :],
                              start=q == 0, stop=q == 4)
                if k == KC - 1:
                    last.then_inc(s["xg_ps"], 1)
                if between:
                    between(k)

        def combine(n, k):
            pe.wait_ge(s["acc_ok"], num(pe, n * KC + (KC + k - 1)))
            mm(bank[6 + k % 2][:, 0:N], yhi[:, k::KC], comb[:, :], start=True, stop=False)
            mm(bank[6 + k % 2][:, 0:N], ylo[:, k::KC], comb[:, :], start=False, stop=True).then_inc(s["comb_ps"], 1)

        def pe_block(u, n, b, j, last_of_pair):
            pe.wait_ge(s["comb_ok"], num(pe, n + 1))
            for i in range(3):
                tr(bank[2][:, P * i:P * i + P], sel[:, i, :, :].bitcast(F32), ident[:, :])
            for i in range(3):
                last = mm(bank[2][:, 3 * P:3 * P + 4], sel[:, i, :, :], wp[:, i, :, :], start=i == 0, stop=i == 2)
            last.then_inc(s["slots_ps"], 1)
            for q in range(6):
                pe.wait_ge(ring_in[6 * u + q], num(pe, b * 8 + (16 + 16 * loads[6 * u + q] - 8 * u)))
            pe.wait_ge(s["xg_ok"], num(pe, n + 1))
            for k in range(KC):
                for x in range(2):
                    last = mm(bank[3][CAP * x:CAP * x + CAP, :].rearrange("p (g n) -> p g n", g=2), xg[:, k, CAP * x:CAP * x + CAP],
                              expert_w[2 * u + x][:, 0:2, DE * k:DE * k + DE], start=k == 0, stop=k == KC - 1,
                              tile_position=(0, CAP * x))
            last.then_inc(s["pgu_ps"], 1)

            def between(k):
                if k == 0:
                    pe.wait_ge(s["ylo_ok"], num(pe, n + 1))
                combine(n, k)
                if k == 3:
                    pe.wait_ge(s["hid_ok"], num(pe, n + 1))
                    for j in range(2):
                        last = tr(bank[4][:, P * j:P * j + P], hid[:, j::2], ident[:, :])
                    last.then_inc(s["hidT_ps"], 1)
            gather(n + 1, between)
            pe.wait_ge(s["hidT_ok"], num(pe, n + 1))
            for half in range(2):
                for j in range(2):
                    for x in range(2):
                        o = D * j + 512 * half
                        last = mm(bank[4 + half][CAP * x:CAP * x + CAP, :], hidT[:, j, CAP * x:CAP * x + CAP],
                                  expert_w[2 * u + x][:, 2, o:o + 512], start=j == 0, stop=j == 1, tile_position=(0, CAP * x))
            last.then_inc(s["yd_ps"], 1)

        gather(0)
        with pe.Fori(0, PAIRS // 2) as it:
            for u in range(2):
                each_block(pe, it * 2 + u, lambda n, j, last: pe_block(u, n, it * 2 + u, j, last))
        n = total_blocks(pe)
        pe.wait_ge(s["ylo_ok"], num(pe, n + 1))
        for k in range(KC):
            combine(n, k)
        sumsq(sq2, s["x2_sq"], KC)
        for i in range(3):
            for k in range(KC):
                if i == 0 and k == 0:
                    pe.wait_ge(s["h2n_ok"], 2)
                if k % 4 == 0 and i >= 1:
                    n = 2 * (i - 1) + k // 4
                    pe.wait_ge(s["y_ok"], n + 1)
                last = tr(bank[k // 4][0:TN[i], P * (k % 4):P * (k % 4) + P], acc[:, k, T0[i]:T0[i] + TN[i]], ident[:, :])
                if k % 4 == 3:
                    last.then_inc(s["y_ps"], 1)

    @block.vector
    def _(dve):
        chain = [0]

        def link(ins):
            chain[0] += 1
            ins.then_inc(s["d_chain"], 1)
            dve.wait_ge(s["d_chain"], chain[0])

        def over_k(ap):
            return ap.unsqueeze(1).broadcast_to([P, KC, N])

        for k in range(KC):
            dve.wait_ge(s["xT_ps"], k + 1)
            dve.tensor_copy(xT[:, k, :], bank[k % 4][:, 0:N]).then_inc(s["xT_ok"], 1)
        dve.wait_ge(s["rstd_ok"], 1)
        link(dve.reciprocal(rstdB[:, :], rstdB[:, :]))
        dve.wait_ge(s["xT_ok"], KC)
        dve.tensor_tensor(xn[:, :, :], xT[:, :, :], over_k(rstdB[:, :]), ALU.mult).then_inc(s["xn_ok"], 1)

        def modulation(r):
            dve.wait_ge(s["small_in"], SMALL)
            dve.wait_ge(s["adaT_in"], 96 if r else 32)
            m = adaT[:, 2 * r:2 * r + 2, :, :]
            link(dve.tensor_tensor(m, m, b_adaT[:, 2 * r:2 * r + 2, :].unsqueeze(2).broadcast_to([P, 2, 2, KC]), ALU.add))

        modulation(0)
        for g in range(2):
            dve.scalar_tensor_tensor(out=gain1[:, g, :], in0=adaT[:, 1, g, :], scalar=1.0, in1=g_mix[:, :],
                                     op0=ALU.add, op1=ALU.mult).then_inc(s["gain_ok"], 1)
        dve.wait_ge(s["gain_ok"], 2)
        dve.wait_ge(s["xn_ok"], 1)
        for k in range(KC):
            dve.tensor_scalar(hT[:, k, NP_:N], xn[:, k, NP_:N], gain1[:, 1, k:k + 1], adaT[:, 0, 1, k:k + 1],
                              ALU.mult, ALU.add).then_inc(s["hT_ok"], 1)
        dve.wait_ge(s["hT_ok"], 16)
        dve.memset(lf_t[:, :, :], 0.0).then_inc(s["hT_ok"], 8)
        for c in range(0, 24, 2):
            dve.wait_ge(s["z_ps"], c + 1)
            b = bank[c % 4]
            if c < 2:
                last = dve.tensor_scalar(gqk[:, c, :], b[:, 0:N], GK ** -0.5, None, ALU.mult)
            elif c < 4:
                last = dve.tensor_copy(gqk[:, c, :], b[:, 0:N])
            elif 12 <= c < 16:
                dve.tensor_scalar(qA[0:FD, 2 * (c - 12), :], b[0:FD, 0:N], FD ** -0.5, None, ALU.mult)
                last = dve.tensor_scalar(qA[0:FD, 2 * (c - 12) + 1, :], b[FD:P, 0:N], FD ** -0.5, None, ALU.mult)
            elif 16 <= c < 20:
                dve.tensor_copy(kA[0:FD, 2 * (c - 16), :], b[0:FD, 0:N])
                dve.tensor_copy(kA[0:FD, 2 * (c - 16) + 1, :], b[FD:P, 0:N])
                last = dve.tensor_copy(zt[:, 8 + c - 16, :], b[:, 0:N])
            else:
                last = dve.tensor_copy(zt[:, c - 4 if c < 12 else c - 8, :], b[:, 0:N])
            last.then_inc(s["z_dve"], 1)
        dve.wait_ge(s["narrow_ps"], 1)
        for i in range(3):
            last = dve.tensor_tensor(lf_t[0:TN[i], i, :], bank[5][0:TN[i], FH * i:FH * i + FH], b_ff[0:TN[i], :], ALU.add)
            if i == 2:
                last.then_inc(s["ff_ok"], 1)
            else:
                link(last)
        dve.wait_ge(s["ff_ok"], 1)
        link(dve.tensor_scalar(lf_m[:, :, :], lf_t[:, :, :], 0.0, None, ALU.min))
        dve.scalar_tensor_tensor(out=lf_t[:, :, :], in0=lf_m[:, :, :], scalar=-2.0, in1=lf_t[:, :, :], op0=ALU.mult,
                                 op1=ALU.add).then_inc(s["lf_abs"], 1)
        dve.wait_ge(s["lf_ln"], 1)
        dve.tensor_tensor(logf[:, :, :], lf_m[:, :, :], lf_t[:, :, :], ALU.subtract).then_inc(s["logf_ok"], 1)
        for c in range(4):
            dve.wait_ge(s["cK_ps"], c + 1)
            dve.tensor_copy(kS[0:FD, 2 * c, :], bank[c][0:FD, :]).then_inc(s["cK_dve"], 1)
        dve.wait_ge(s["gate_ps"], 1)
        for c in range(2):
            last = dve.tensor_scalar(g_t[:, c, :], bank[4 + c][:, 0:N], b_gk[:, c:c + 1], None, ALU.add)
            if c:
                last.then_inc(s["gate_x"], 1)
            else:
                link(last)
        dve.wait_ge(s["gate_x"], 1)
        link(dve.tensor_scalar(g_b[:, :, :], g_t[:, :, :], 0.0, None, ALU.min))
        dve.scalar_tensor_tensor(out=g_a[:, :, :], in0=g_b[:, :, :], scalar=-2.0, in1=g_t[:, :, :], op0=ALU.mult,
                                 op1=ALU.add).then_inc(s["gate_abs"], 1)
        dve.wait_ge(s["crow_ps"], 1)
        dve.tensor_copy(crow[:, 0, :], bank[6][0:FH, 0:N]).then_inc(s["crow_ok"], 1)
        dve.tensor_scalar(crow[:, 1, :], bank[6][0:FH, 0:N], -1.0, None, ALU.mult).then_inc(s["crow_ok"], 1)
        dve.wait_ge(s["crow_ps"], 2)
        dve.tensor_copy(srow[:, :], bank[7][0:FH, :]).then_inc(s["crow_ok"], 1)
        dve.wait_ge(s["gate_ln"], 1)
        link(dve.tensor_tensor(g_t[:, :, :], g_b[:, :, :], g_a[:, :, :], ALU.subtract))
        link(dve.tensor_scalar(g_b[:, :, :], g_t[:, :, :], 1.0 / 16.0, None, ALU.mult))
        for c in range(2):
            for b in range(5):
                t0, n = BLK * b, BLK if b < 4 else NS_
                last = dve.tensor_tensor_scan(g_t[:, c, t0:t0 + n], ones[:, 0:n], g_b[:, c, t0:t0 + n], 0.0, ALU.mult, ALU.add)
        link(last)

        def by_block(t, c):
            return t[:, c, 0:NP_].rearrange("p (b n) -> p b n", n=BLK)

        for c in range(2):
            def col(at):
                return g_t[:, c, at:NP_:BLK].unsqueeze(2).broadcast_to([P, 4, BLK])

            def scol(at):
                return g_t[:, c, at:at + 1].broadcast_to([P, NS_])
            dve.tensor_tensor(by_block(g_a, c), by_block(g_t, c), col(BLK // 2), ALU.subtract)
            dve.tensor_tensor(g_a[:, c, NP_:N], g_t[:, c, NP_:N], scol(NP_ + NS_ // 2), ALU.subtract).then_inc(s["cum_ok"], 1)
            dve.tensor_tensor(by_block(g_b, c), col(BLK - 1), by_block(g_t, c), ALU.subtract)
            dve.tensor_tensor(g_b[:, c, NP_:N], scol(N - 1), g_t[:, c, NP_:N], ALU.subtract).then_inc(s["cum_ok"], 1)
        for n, (t, z0) in enumerate(((qe, 0), (ke, 2), (qb, 0), (kl, 2))):
            dve.wait_ge(s["gexp_ok"], n + 1)
            dve.tensor_tensor(t[:, :, :], t[:, :, :], gqk[:, z0:z0 + 2, :], ALU.mult).then_inc(s["gprod_ok"], 1)
        for q in range(12):
            kind, i = q // 3, q % 3
            if kind != 1:
                dve.wait_ge(s["tok_ps"], q + 1)
                dve.tensor_copy(toks[0:TN[i], kind, i, :], bank[4 + q % 4][0:TN[i], :]).then_inc(s["tok_dve"], 1)
        dve.wait_ge(s["klT_ps"], 1)
        link(dve.tensor_copy(kl_tok[:, 0:2, :], bank[4][:, :].rearrange("p (i n) -> p i n", i=2)))
        dve.tensor_copy(kl_tok[0:NS_, 2, :], bank[5][0:NS_, 0:256]).then_inc(s["klT_ok"], 1)
        dve.wait_ge(s["aT_ps"], 1)
        dve.wait_ge(s["zeros"], 14)
        mask = glamask[:, :].bitcast(I32)
        for q in range(2):
            dve.copy_predicated(a_t[:, q, 0:2, :, :].rearrange("p i c n -> p (i c) n"), mask.unsqueeze(1).broadcast_to([P, 4, BLK]),
                                bank[6 + q][:, 0:256].rearrange("p (g n) -> p g n", n=BLK)).then_inc(s["aT_ok"], 1)
            dve.copy_predicated(a_t[0:NS_, q, 2, :, 0:NS_], mask[0:NS_, 0:NS_].unsqueeze(1).broadcast_to([NS_, 2, NS_]),
                                bank[6 + q][0:NS_, 256:384].rearrange("p (g n) -> p g n", n=BLK)[:, :, 0:NS_]).then_inc(s["aT_ok"], 1)
        dve.wait_ge(s["upd_ps"], 1)
        dve.wait_ge(s["gexp_ok"], 6)
        dve.wait_ge(s["state_in"], 32)

        for c in range(2):
            dve.tensor_copy(states[:, 0, c, :], update(0, c)).then_inc(s["state_ok"], 1)
            dve.scalar_tensor_tensor(out=states[:, 5, c, :], in0=states[:, 4, c, :], scalar=dec[:, c, 4:5], in1=update(4, c),
                                     op0=ALU.mult, op1=ALU.add).then_inc(s["state_ok"], 1)
        for b in range(1, 4):
            dve.wait_ge(s["state_ok"], 2 + 2 * b)
            for c in range(2):
                dve.scalar_tensor_tensor(out=states[:, b, c, :], in0=states[:, b - 1, c, :], scalar=dec[:, c, b:b + 1],
                                         in1=update(b, c), op0=ALU.mult, op1=ALU.add).then_inc(s["state_ok"], 1)
        for i in range(3):
            dve.wait_ge(s["go_ps"], max(i + 1, 2))
            link(dve.tensor_copy(o_tok[0:TN[i], i, 0:512], bank[3 + i][0:TN[i], :]))
            lo = BLK if i == 0 else 0
            for q in range(2):
                o = o_tok[lo:TN[i], i, 0:512].rearrange("t (c q v) -> t c q v", c=2, q=2)[:, :, q, :]
                last = dve.tensor_tensor(o, inter(i, q)[lo:TN[i], :].rearrange("t (c v) -> t c v", c=2), o, ALU.add)
            last.then_inc(s["go_ok"], 1)
        def maxima(u):
            i, n = u // 8, TN[u // 8]
            dve.wait_ge(s["sc_ps"], u + 1)
            dve.tensor_reduce(nmax[0:n, u:u + 1], score(u)[0:n, 0:NKEY[i]], AX, ALU.max, negate=True).then_inc(s["max_ok"], 1)

        maxima(0)
        for u in range(24):
            i, n = u // 8, TN[u // 8]
            if u + 1 < 24:
                maxima(u + 1)
            dve.wait_ge(s["pT_ps"], u + 1)
            if u >= 2:
                dve.wait_ge(s["po_ps"], u - 1)
            if i < 2:
                dve.tensor_copy(probT[u % 2][:, 0:n * (i + 1)], bank[u % 2][:, 0:n * (i + 1)]).then_inc(s["pT_ok"], 1)
            else:
                link(dve.tensor_copy(probT[u % 2][:, 0:4 * n], bank[u % 2][:, 0:4 * n]))
                dve.tensor_copy(probT[u % 2][0:NS_, 4 * n:5 * n], bank[u % 2][0:NS_, 4 * n:5 * n]).then_inc(s["pT_ok"], 1)
            if u % 8 == 0 and u:
                divide(dve, i - 1, link)
        divide(dve, 2, link)
        modulation(1)
        modulation(2)
        for g in range(2):
            dve.scalar_tensor_tensor(out=gain2[:, g, :], in0=adaT[:, 4, g, :], scalar=1.0, in1=g_ffn[:, :],
                                     op0=ALU.add, op1=ALU.mult).then_inc(s["gain_ok"], 1)
        dve.wait_ge(s["rs_act"], 2)
        link(dve.reciprocal(rs5[:, :, :], rs5[:, :, :]))
        for i in range(3):
            n = TN[i]
            for h in range(GH):
                o = o_tok[0:n, i, GV * h:GV * h + GV]
                dve.scalar_tensor_tensor(out=o, in0=o, scalar=rs5[0:n, i, h:h + 1], in1=toks[0:n, 1, i, GV * h:GV * h + GV],
                                         op0=ALU.mult, op1=ALU.mult)
            dve.tensor_scalar(o_tok[0:n, i, 512:1024], o_tok[0:n, i, 512:1024], rs5[0:n, i, 4:5], None, ALU.mult).then_inc(s["on_ok"], 1)
        for j in range(1, 8, 2):
            dve.wait_ge(s["mT_ps"], j + 1)
            dve.tensor_scalar(mT[:, j, :], bank[j % 4][:, 0:N], g_gla[:, 0:1] if j < 4 else g_fox[:, j - 4:j - 3], None,
                              ALU.mult).then_inc(s["mT_dve"], 1)
        for k in range(KC):
            dve.wait_ge(s["mix_ps"], k + 1)
            dve.scalar_tensor_tensor(out=xT[:, k, 0:NP_], in0=bank[k % 4][:, 0:NP_], scalar=adaT[:, 2, 0, k:k + 1],
                                     in1=xT[:, k, 0:NP_], op0=ALU.mult, op1=ALU.add)
            dve.scalar_tensor_tensor(out=xT[:, k, NP_:N], in0=bank[k % 4][:, NP_:N], scalar=adaT[:, 2, 1, k:k + 1],
                                     in1=xT[:, k, NP_:N], op0=ALU.mult, op1=ALU.add).then_inc(s["x1_ok"], 1)
        dve.wait_ge(s["rstd_ok"], 2)
        link(dve.reciprocal(rstdB[:, :], rstdB[:, :]))
        dve.wait_ge(s["x1_ok"], KC)
        dve.tensor_tensor(h2T[:, :, :], xT[:, :, :], over_k(rstdB[:, :]), ALU.mult).then_inc(s["h2n_ok"], 1)
        dve.wait_ge(s["h2n_ok"], 1)
        dve.wait_ge(s["gain_ok"], 4)
        for k in range(KC):
            dve.tensor_scalar(h2T[:, k, NP_:N], h2T[:, k, NP_:N], gain2[:, 1, k:k + 1], adaT[:, 3, 1, k:k + 1],
                              ALU.mult, ALU.add).then_inc(s["h2_ok"], 1)

        def select(out, vals, width, k, n, last_op):
            v = vals
            thr = t8[0:n, k - 1:k]
            a, b, c = r_a[0:n, 0:width], r_b[0:n, 0:width], r_c[0:n, 0:width]
            link(dve.tensor_scalar(a, v, thr, 0.0, ALU.is_gt, ALU.add, accum_out=r_n[0:n, :]))
            link(dve.tensor_scalar(b, v, thr, None, ALU.is_equal))
            link(dve.tensor_tensor_scan(c, ones[0:n, 0:width], b, 0.0, ALU.mult, ALU.add))
            link(dve.tensor_scalar(c, c, r_n[0:n, 0:1], float(k), ALU.add, ALU.is_le))
            link(dve.tensor_tensor(b, b, c, ALU.mult))
            last_op(dve.tensor_tensor(out, a, b, ALU.add))

        for i in range(3):
            n = TN[i]
            dve.wait_ge(s["rt_sc"], i + 1)
            link(dve.tensor_tensor(ch[0:n, i, :], sc[0:n, i, :], b_rt[0:n, :], ALU.add))
            for g in range(NG):
                last = dve.max(top[0:n, g, :], ch[0:n, i, 8 * g:8 * g + 8])
            link(last)
            link(dve.tensor_tensor(gs[0:n, :], top[0:n, :, 0], top[0:n, :, 1], ALU.add))
            link(dve.max(t8[0:n, :], gs[0:n, :]))
            select(gs[0:n, :], gs[0:n, :], NG, TOPG, n, link)
            link(dve.tensor_scalar(gs[0:n, :], gs[0:n, :], 1.0, -NEG, ALU.subtract, ALU.mult))
            link(dve.tensor_tensor(ch[0:n, i, :].rearrange("p (g m) -> p g m", g=NG), ch[0:n, i, :].rearrange("p (g m) -> p g m", g=NG),
                                   gs[0:n, :].unsqueeze(2).broadcast_to([n, NG, 8]), ALU.add))
            link(dve.max(t8[0:n, :], ch[0:n, i, :]))
            select(ch[0:n, i, :], ch[0:n, i, :], E, TOPK, n, link)
            link(dve.tensor_tensor(wrt[0:n, i, :], sc[0:n, i, :], ch[0:n, i, :], ALU.mult))
            link(dve.tensor_reduce(r_n[0:n, :], wrt[0:n, i, :], AX, ALU.add))
            link(dve.tensor_scalar(r_n[0:n, :], r_n[0:n, :], 1e-20, None, ALU.add))
            link(dve.reciprocal(r_n[0:n, :], r_n[0:n, :]))
            dve.tensor_scalar(wrt[0:n, i, :], wrt[0:n, i, :], r_n[0:n, 0:1], RSCALE, ALU.mult, ALU.mult).then_inc(s["wrt_ok"], 1)
        for j in range(2):
            dve.wait_ge(s["sil_ok"], j + 1)
            dve.tensor_tensor(actT[:, j, :], bank[2 + j][:, 0:N], sil[:, j, :], ALU.mult).then_inc(s["act_ok"], 1)
        dve.wait_ge(s["iota_ok"], 5)
        for q in range(6):
            i, k = q // 2, 4 * (q % 2)
            dve.wait_ge(s["h2hi_ok"], q + 1)
            low = h2hl[NS_:2 * NS_, 4, k:k + 4, :] if i == 2 else h2hl[:, 2 * i + 1, k:k + 4, :]
            dve.tensor_tensor(low, bank[4 + q % 2][0:TN[i], :].rearrange("t (k p) -> t k p", k=4),
                              h2hl[0:TN[i], 2 * i, k:k + 4, :].bitcast(F32), ALU.subtract).then_inc(s["h2lo_ok"], 1)
        for k in range(KC):
            dve.wait_ge(s["dn_ps"], k + 1)
            dve.tensor_copy(acc[:, k, :], bank[5 + k % 2][:, 0:N]).then_inc(s["acc_ok"], 1)
        dve.wait_ge(s["iota_ok"], 5)
        dve.wait_ge(s["pos_ps"], 1)
        for i in range(3):
            n = TN[i]
            link(dve.scalar_tensor_tensor(out=posm[0:n, i, 0:E], in0=bank[4][0:n, E * i:E * i + E], scalar=1.0, in1=ch[0:n, i, :],
                                          op0=ALU.add, op1=ALU.mult))
            link(dve.tensor_scalar(posm[0:n, i, 0:E], posm[0:n, i, 0:E], 1.0, None, ALU.subtract))
            if i == 2:
                link(dve.tensor_copy(posm[NS_:2 * NS_, i, 0:E], posm[0:NS_, i, 0:E]))
            link(dve.tensor_copy(w_hl[0:n, i, 0, 0:E], wrt[0:n, i, :]))
            link(dve.tensor_tensor(w_hl[0:n, i, 1, 0:E], wrt[0:n, i, :], w_hl[0:n, i, 0, 0:E].bitcast(F32), ALU.subtract))
        link(dve.tensor_reduce(mcount[:, :], bank[4][0:1, 3 * E:4 * E].rearrange("o (g m) -> o g m", m=2), AX, ALU.max))
        link(dve.tensor_scalar(nx[:, :], mcount[:, :], float(CAP), None, ALU.is_gt))
        for j in range(2, MAXB):
            link(dve.scalar_tensor_tensor(out=nx[:, :], in0=mcount[:, :], scalar=float(CAP * j), in1=nx[:, :], op0=ALU.is_gt, op1=ALU.add))
        link(dve.tensor_copy(table[:, 0:PAIRS], nx[:, :]))
        link(dve.tensor_tensor_scan(nxc[:, :], ones[0:1, 0:PAIRS], nx[:, :], 0.0, ALU.mult, ALU.add))
        link(dve.tensor_tensor(nxc[:, :], nxc[:, :], nx[:, :], ALU.subtract))
        dve.tensor_tensor(table[:, PAIRS:2 * PAIRS], nxc[:, :], iota[0:1, 0:PAIRS], ALU.add).then_inc(s["table_ok"], 1)
        dve.wait_ge(s["table_ok"], 1)

        def select_slots(b, at):
            e2 = num(dve, b * 2)
            dve.tensor_tensor(sel[:, :, :, :], iota[:, bass.ds(at, CAP)].unsqueeze(1).unsqueeze(1).broadcast_to([P, 3, 2, CAP]),
                              posm[:, :, bass.ds(e2, 2)].unsqueeze(3).broadcast_to([P, 3, 2, CAP]), ALU.is_equal)
            dve.tensor_copy(wp[:, :, :, :], w_hl[:, :, :, bass.ds(e2, 2)].bitcast(F32)).then_inc(s["sel_ok"], 1)

        def add(n, k):
            dve.wait_ge(s["comb_ps"], num(dve, n * KC + (k + 1)))
            dve.wait_ge(s["acc_ok"], num(dve, n * KC + (k + 1)))
            dve.tensor_tensor(acc[:, k, :], bank[6 + k % 2][:, 0:N], acc[:, k, :], ALU.add).then_inc(s["acc_ok"], 1)

        def dve_block(n, b, j, last_of_pair):
            dve.wait_ge(s["slots_ps"], num(dve, n + 1))
            for x in range(2):
                last = dve.tensor_reduce(ws[CAP * x:CAP * x + CAP, :], bank[2][CAP * x:CAP * x + CAP, 3 * P + x:3 * P + 4:2], AX, ALU.add)
            last.then_inc(s["ws_ok"], 1)
            if last_of_pair:
                select_slots(b + 1, 0)
            else:
                select_slots(b, dve.snap((j + 1) * CAP))
            dve.wait_ge(s["sl_ok"], num(dve, n + 1))
            dve.wait_ge(s["ws_ok"], num(dve, n + 1))
            dve.scalar_tensor_tensor(out=hid[:, :], in0=bank[3][:, DE:2 * DE], scalar=ws[:, 0:1], in1=silg[:, :],
                                     op0=ALU.mult, op1=ALU.mult).then_inc(s["hid_ok"], 1)
            for k in range(KC):
                add(n, k)
            dve.tensor_copy(comb[:, :], bank[2][:, 0:N]).then_inc(s["comb_ok"], 1)
            dve.wait_ge(s["yhi_ok"], num(dve, n + 1))
            dve.tensor_tensor(ylo[:, :], psum[:, 4 * 512:6 * 512], yhi[:, :].bitcast(F32), ALU.subtract).then_inc(s["ylo_ok"], 1)

        dve.memset(comb[:, :].bitcast(F32), 0.0).then_inc(s["comb_ok"], 1)
        dve.memset(yhi[:, :].bitcast(F32), 0.0)
        dve.memset(ylo[:, :].bitcast(F32), 0.0).then_inc(s["ylo_ok"], 1)
        select_slots(0, 0)
        with dve.Fori(0, PAIRS // 2) as it:
            for u in range(2):
                each_block(dve, it * 2 + u, lambda n, j, last: dve_block(n, it * 2 + u, j, last))
        n = total_blocks(dve)
        for k in range(KC):
            add(n, k)
        dve.wait_ge(s["acc_ok"], num(dve, n * KC + 2 * KC))
        for k in range(KC):
            dve.scalar_tensor_tensor(out=acc[:, k, 0:NP_], in0=acc[:, k, 0:NP_], scalar=adaT[:, 5, 0, k:k + 1],
                                     in1=xT[:, k, 0:NP_], op0=ALU.mult, op1=ALU.add)
            dve.scalar_tensor_tensor(out=acc[:, k, NP_:N], in0=acc[:, k, NP_:N], scalar=adaT[:, 5, 1, k:k + 1],
                                     in1=xT[:, k, NP_:N], op0=ALU.mult, op1=ALU.add).then_inc(s["fin_ok"], 1)
        dve.wait_ge(s["rstd_ok"], 3)
        link(dve.reciprocal(rstdB[:, :], rstdB[:, :]))
        dve.wait_ge(s["x2_sq"], 2 * KC)
        for k in range(KC):
            last = dve.scalar_tensor_tensor(out=acc[:, k, :], in0=acc[:, k, :], scalar=g_fin[:, k:k + 1], in1=rstdB[:, :],
                                            op0=ALU.mult, op1=ALU.mult)
        last.then_inc(s["h2n_ok"], 1)
        for i in range(3):
            for q in range(2):
                dve.wait_ge(s["y_ps"], 2 * i + q + 1)
                dve.tensor_copy(yout[0:TN[i], i, :].rearrange("t (p k) -> t k p", k=KC)[:, 4 * q:4 * q + 4, :],
                                bank[q][0:TN[i], :].rearrange("t (k p) -> t k p", k=4)).then_inc(s["y_ok"], 1)

    ctx.close()


_INS = ["x_prompt", "x_sample", "state_gla", "cache_fox_k", "cache_fox_v", "cache_fox_logf", "c_prompt", "c_sample",
        "w_ada", "b_ada", "g_norm_mix", "g_norm_ffn", "w_in", "w_gla_gk2", "b_gla_gk", "g_gla_out", "b_fox_f", "g_fox_out",
        "w_out", "w_router", "b_router", "w_exp_gate", "w_exp_up", "w_exp_down", "w_sh_gate", "w_sh_up", "w_sh_down", "g_final"]
_OUTS = [(1, NP_, D), (1, NS_, D), (1, 1, GH, GK, GV), (1, 1, GH, GK, GV), (1, 1, NP_, FH, FD), (1, 1, NP_, FH, FD),
         (1, 1, NP_, FH), (1, 1, NS_, FH, FD), (1, 1, NS_, FH, FD), (1, 1, NS_, FH)]


def kernel(**inputs):
    import numpy as _np
    import concourse.bacc as _bacc
    from concourse import mybir as _mybir
    from concourse.bass_utils import run_bass_kernel_spmd as _run

    nc = _bacc.Bacc("TRN2", target_bir_lowering=False, num_devices=1)
    arrays, args = {}, []
    for name in _INS:
        a = _np.ascontiguousarray(inputs[name])
        arrays[f"in_{name}"] = a
        args.append(nc.dram_tensor(f"in_{name}", a.shape, _mybir.dt.from_np(a.dtype), kind="ExternalInput").ap())
    for i, shape in enumerate(_OUTS):
        args.append(nc.dram_tensor(f"out_{i}", shape, F32, kind="ExternalOutput").ap())
    layer(nc, *args)
    r = _run(nc, [arrays], core_ids=[0])
    return tuple(r.results[0][f"out_{i}"] for i in range(len(_OUTS)))
```

```python
from contextlib import ExitStack

import concourse.bass as bass
from concourse import mybir

ALU = mybir.AluOpType
ACT = mybir.ActivationFunctionType
AX = mybir.AxisListType.X
F32 = mybir.dt.float32
BF16 = mybir.dt.bfloat16
F32R = mybir.dt.float32r
I32 = mybir.dt.int32

P = 128
D = 1024
KC = D // P
NP_, NS_ = 256, 32
N = NP_ + NS_
TN = [128, 128, 32]
T0 = [0, 128, 256]
PAST = 512
GH, GK, GV = 4, 64, 128
FH, FD = 8, 64
LR = 16
E, DE = 64, 256
NG, TOPG, TOPK = 8, 4, 8
RSCALE = 2.5
EPS = 1e-6
NEG = -1e30
BLK = 64
CAP = 64
MAXB = -(-N // CAP)
PAIRS = E // 2
C_GQ, C_GK, C_GV, C_GG, C_LR, C_FQ, C_FK, C_FV, C_FF = 0, 256, 512, 1024, 1536, 1552, 2064, 2576, 3088
SLOT = 2048


def layer(nc, x_prompt, x_sample, state_gla, cache_fox_k, cache_fox_v, cache_fox_logf, c_prompt, c_sample,
          w_ada, b_ada, g_norm_mix, g_norm_ffn, w_in, w_gla_gk2, b_gla_gk, g_gla_out, b_fox_f, g_fox_out,
          w_out, w_router, b_router, w_exp_gate, w_exp_up, w_exp_down, w_sh_gate, w_sh_up, w_sh_down, g_final,
          y_prompt, y_sample, st_prompt, st_sample, k_prompt, v_prompt, f_prompt, k_sample, v_sample, f_sample):
    ctx = ExitStack()

    place = {"at": nc.sbuf_base + (-nc.sbuf_base) % 64}

    def sb_at(name, shape, dt, at):
        return nc.alloc_sbuf_tensor_at(name, shape, dt, offset=at)

    def sb(name, shape, dt=F32):
        size = 2 if dt == BF16 else 4
        for s in shape[1:]:
            size *= s
        at = place["at"]
        place["at"] = at + size + (-size) % 64
        return sb_at(name, shape, dt, at)

    ident = sb("ident", [P, P])
    ones = sb("ones", [P, P])
    upper = sb("upper", [P, P])
    lower = sb("lower", [P, P])
    before = sb("before", [P, P])
    glamask = sb("glamask", [P, BLK])
    identb = sb("identb", [P, P], BF16)
    causal = sb("causal", [P, P], BF16)
    epst = sb("epst", [P, 1])
    g_mix = sb("g_mix", [P, KC])
    g_ffn = sb("g_ffn", [P, KC])
    g_fin = sb("g_fin", [P, KC])
    b_adaT = sb("b_adaT", [P, 6, KC])
    adaT = sb("adaT", [P, 6, 2, KC])
    gain1 = sb("gain1", [P, 2, KC])
    gain2 = sb("gain2", [P, 2, KC])
    g_gla = sb("g_gla", [P, 1])
    g_fox = sb("g_fox", [P, 4])
    b_gk = sb("b_gk", [P, 2])
    b_ff = sb("b_ff", [P, FH])
    b_rt = sb("b_rt", [P, E])
    w_gk2 = sb("w_gk2", [LR, 256])
    w_rt = sb("w_rt", [P, KC, E])
    w_lf = sb("w_lf", [P, KC, LR + FH])
    cT = sb("cT", [P, 2, KC])
    scT = sb("scT", [P, KC, 2])
    xT = sb("xT", [P, KC, N])
    rstdB = sb("rstdB", [P, N])
    hT = sb("hT", [P, KC, N])
    base = place["at"]
    RING = base
    NSLOT = 12
    FRONT = 6
    ring = [sb_at(f"ring{i}", [P, SLOT], F32, RING + 8192 * i) for i in range(NSLOT)]
    pair = [sb_at(f"pair{i}", [P, 2 * SLOT], F32, RING + 16384 * i) for i in range(FRONT // 2)]
    place["at"] = RING + 8192 * FRONT
    gqk = sb("gqk", [P, 4, N])
    zt = sb("zt", [P, 16, N])
    o_tok = sb_at("o_tok", [P, 3, D], F32, place["at"] - 4 * 16 * N)
    prob = [sb_at(f"prob{i}", [P, PAST + NS_], F32, place["at"] - 4 * 16 * N + 12288 + 2176 * i) for i in range(2)]
    whi = [sb_at(f"whi{i}", [P, KC, 256], F32R, place["at"] + 8192 * i) for i in range(2)]
    wlo = [sb_at("wlo0", [P, KC, 256], F32R, place["at"] + 16384)]
    toks = sb("toks", [P, 4, 3, 512])
    qA = sb("qA", [FD + 2, FH, N])
    sq1 = sb_at("sq1", [P, KC, N], F32, place["at"])
    kA = sb("kA", [FD + 2, FH, N])
    x_tok = sb_at("x_tok", [P, 3, D], F32, place["at"])
    wlo.append(sb_at("wlo1", [P, KC, 256], F32R, place["at"]))
    hhi = sb_at("hhi", [P, KC, N], F32R, place["at"] + 8192)
    hlo = sb_at("hlo", [P, KC, N], F32R, place["at"] + 8192 + 4 * KC * N)
    kS = sb("kS", [FD + 2, FH, PAST])
    cacheK = sb("cacheK", [P, 4, 512])
    probT = [sb_at(f"probT{i}", [P, 256], F32, place["at"] - 8192 + 1024 * i) for i in range(2)]
    cacheV = sb("cacheV", [P, 4, 512])
    sq = sb_at("sq", [P, KC, N], F32, place["at"])
    xn = sb_at("xn", [P, KC, N], F32, place["at"] + 9216)
    g_t = sb("g_t", [P, 2, N])
    kl_tok = sb_at("kl_tok", [P, 3, 256], F32, place["at"])
    g_a = sb("g_a", [P, 2, N])
    g_b = sb("g_b", [P, 2, N])
    junk = sb_at("junk", [P, 512], F32, place["at"])
    g_c = sb("g_c", [P, 2, N])
    sqsum1 = sb_at("sqsum1", [P, N], F32, place["at"])
    qe = sb("qe", [P, 2, N])
    ke = sb("ke", [P, 2, N])
    qb = sb("qb", [P, 2, N])
    kl = sb("kl", [P, 2, N])
    a_t = sb("a_t", [P, 2, 3, 2, BLK])
    states = sb("states", [P, 6, 2, GV])
    dec = sb("dec", [P, 2, 5])
    logf = sb("logf", [P, 3, FH])
    lf_t = sb("lf_t", [P, 3, FH])
    lf_m = sb("lf_m", [P, 3, FH])
    pastf = sb("pastf", [P, 4, FH])
    crow = sb("crow", [FH, 2, N])
    srow = sb("srow", [FH, PAST])
    glr = sb("glr", [LR, N])
    nmax = sb("nmax", [P, 24])
    rsum = sb("rsum", [P, 24])
    rinv = sb("rinv", [P, 24])
    ssq5 = sb("ssq5", [P, 3, 5])
    rs5 = sb("rs5", [P, 3, 5])
    mT = hT
    ada_row = sb("ada_row", [P, 512])
    assert place["at"] <= nc.sbuf_usable_end, (place["at"], nc.sbuf_usable_end)

    place["at"] = RING + 8192 * NSLOT
    acc = sb("acc", [P, KC, N])
    h2T = sb("h2T", [P, KC, N])
    actT = sb("actT", [P, 2, N])
    scoreT = sb_at("scoreT", [E, N], F32, place["at"])
    sil = sb("sil", [P, 2, N])
    sc = sb("sc", [P, 3, E])
    ch = sb("ch", [P, 3, E])
    top = sb("top", [P, 3 * NG, 8])
    gs = sb("gs", [P, 3, NG])
    t8 = sb("t8", [P, 3, 8])
    r_a = sb("r_a", [P, 3 * E])
    r_b = sb("r_b", [P, 3 * E])
    r_c = sb("r_c", [P, 3 * E])
    r_n = sb("r_n", [P, 3])
    restart = {w: sb(f"restart{w}", [P, 3 * w]) for w in (NG, E)}
    wrt = sb("wrt", [P, 3, E])
    posm = sb("posm", [P, 3, E + 2])
    w_hl = sb("w_hl", [P, 3, 2, E + 2], F32R)
    iota = sb("iota", [P, MAXB * CAP])
    iota_i = sb("iota_i", [P, MAXB * CAP], I32)
    mcount = sb("mcount", [1, PAIRS])
    nx = sb("nx", [1, PAIRS])
    nxc = sb("nxc", [1, PAIRS])
    table = sb("table", [1, 2 * PAIRS + E + 2], I32)
    rank_at = sb("rank_at", [E, E])
    rank_i = sb("rank_i", [E, E], I32)
    tie_i = sb("tie_i", [E, E + 1], I32)
    tie = sb("tie", [E, E + 1])
    e_col = sb("e_col", [E, 1])
    key = sb("key", [E, E + 1])
    rank = sb("rank", [E, 1])
    c_col = sb("c_col", [E, 1])
    onehot = sb("onehot", [E, E])
    h2hl = sb("h2hl", [P, 5, KC, P], F32R)
    yT = h2T
    yout = sb_at("yout", [P, 3, D], F32, place["at"] - 4 * 5 * D)
    sq2 = sb_at("sq2", [P, KC, N], F32, place["at"] - 4 * 3 * D)

    sel = sb("sel", [P, 3, 2, CAP], F32R)
    wp = sb("wp", [P, 3, 2, 2], F32R)
    comb = sb("comb", [P, N], F32R)
    ws = sb("ws", [P, 1])
    xs = sb("xs", [P, KC, P])
    xg = sb("xg", [P, KC, P])
    silg = sb("silg", [P, DE])
    hid = sb("hid", [P, DE])
    hidT = sb("hidT", [P, 2, P])
    yhi = sb("yhi", [P, D], F32R)
    ylo = sb("ylo", [P, D], F32R)
    sqsum2 = sb("sqsum2", [P, N])
    rstdT = sb("rstdT", [P, 3])
    assert place["at"] <= nc.sbuf_usable_end, (place["at"], nc.sbuf_usable_end)

    expert_w = [sb_at(f"expert_w{i}", [P, 3, SLOT], F32, RING + 3 * 8192 * i) for i in range(4)]
    psum = nc.alloc_psum_tensor("psum", [P, 8 * 512], F32)
    bank = [psum[:, 512 * i:512 * i + 512] for i in range(8)]

    crow_d = nc.dram_tensor("crow_d", [2, FH, N], F32, kind="Internal").ap()
    srow_d = nc.dram_tensor("srow_d", [FH, PAST], F32, kind="Internal").ap()

    def sem(name):
        return ctx.enter_context(nc.semaphore(name))

    s = {n: sem(n) for n in (
        "x_in c_in small_in cache_in state_in consts zeros xT_ps xT_ok sq_ok ssq_ps rstd_ok rinv_ok xn_ok sc_ok gains_in row_zeros ada_row ada_T ada_ok "
        "gain_ok hhi_act hhi_dve hT_act hT_dve hlo_ok whi_ok wlo_ok lf_zero lr_ps z_ps z_act z_dve narrow_ps glr_ok ff_ok lf_abs lf_ln logf_ok f_out crow_ps crow_ok crow_out rows_in ones_ok "
        "tok_ps tok_act tok_dve kv_out cK_ps cK_act cK_dve gate_ps gate_x gate_abs gate_ln cum_ok gexp_ok gprod_ok klT_ps klT_ok aT_ps aT_ok "
        "upd_ps state_ok st_out go_ps go_ok sc_ps max_ok exp_ok pT_ps pT_ok po_ps po_ok ssq_act rs_act on_ok mT_ps mT_act mT_dve "
        "mix_ps x1_ok d_chain a_chain w_used x2_sq h2n_ok h2_ok h2s_ok rt_ps rt_sc rtT_ps wrt_ok gu_ps sil_ok act_ok "
        "dn_ps acc_ok h2t_ps h2hi_ok h2lo_ok pos_ps rank_ok order_ps table_ok iota_ok rt_zeros sel_ok slots_ps ws_ok comb_ok xs_ps xs_ok xg_ps xg_ok pgu_ps sl_ok hid_ok hidT_ps hidT_ok yd_ps yhi_ok ylo_ok comb_ps fin_ok sqsum_ok y_act y_dve ssqT_ps rstdT_ok y_ok y_ok_dve out_done").split()}
    ring_in = [sem(f"ring_in{i}") for i in range(NSLOT)]

    wa = w_ada[0].rearrange("(p k) n -> p k n", k=KC)
    wi = w_in[0].rearrange("(p k) n -> p k n", k=KC)
    wo = w_out[0].rearrange("(j p) n -> p j n", p=P)
    GROUPS = [C_GQ, C_GV, C_GG, C_FQ, C_FK, C_FV]
    pieces = []
    for k in range(KC):
        pieces.append((wa[:, k, 0:2048], 1))
    for c in GROUPS:
        pieces.append((wi[:, :, c:c + 512], 2))
    for r in (1, 2):
        for k in range(KC):
            pieces.append((wa[:, k, 2048 * r:2048 * r + 2048], 1))
    for j in range(0, 8, 4):
        pieces.append((wo[:, j:j + 4, :], 2))
    at, slots_of, loads, owner, waits_of, turn = 0, [], [0] * NSLOT, {}, [], []
    for n, (_, w) in enumerate(pieces):
        assert w == 1 or at % 2 == 0
        sl = [(at + i) % FRONT for i in range(w)]
        at += w
        waits_of.append(max([owner[q] for q in sl if q in owner], default=-1))
        for q in sl:
            owner[q] = n
        slots_of.append(sl)
        loads[sl[0]] += 1
        turn.append(loads[sl[0]])
    FIRST_WIN, FIRST_R1, FIRST_WO = KC, KC + 6, KC + 6 + 2 * KC

    def half_group(g):
        return pair[slots_of[FIRST_WIN + g // 2][0] // 2][:, :].rearrange("p (k n) -> p k n", k=KC)[:, :, 256 * (g % 2):256 * (g % 2) + 256]

    def piece_in(eng, n):
        eng.wait_ge(ring_in[slots_of[n][0]], 16 * turn[n])

    def piece(n):
        return ring[slots_of[n][0]] if pieces[n][1] == 1 else pair[slots_of[n][0] // 2]

    SHARED = FRONT
    for q in range(3):
        loads[SHARED + q] += 1
    EARLY = 4
    SPREAD = 6
    assert (E - EARLY) % (2 * SPREAD) == 0
    FIRST_KEY = (N + 1) * E

    block = ctx.enter_context(nc.Block())
    small = [
        (g_mix[:, :], g_norm_mix[0].rearrange("(p k) -> p k", k=KC)),
        (g_ffn[:, :], g_norm_ffn[0].rearrange("(p k) -> p k", k=KC)),
        (g_fin[:, :], g_final.rearrange("(p k) -> p k", k=KC)),
        (b_adaT[:, :, :], b_ada[0].rearrange("(m p k) -> p m k", m=6, k=KC)),
        (g_gla[:, :], g_gla_out[0].rearrange("(p o) -> p o", o=1)),
        (g_fox[:, :], g_fox_out[0].rearrange("(j p) -> p j", p=P)),
        (b_gk[:, :], b_gla_gk[0].rearrange("(j p) -> p j", p=P)),
        (b_ff[:, :], b_fox_f[0].partition_broadcast(P)),
        (b_rt[:, :], b_router[0].partition_broadcast(P)),
        (w_gk2[:, :], w_gla_gk2[0]),
        (w_rt[:, :, :], w_router[0].rearrange("(p k) n -> p k n", k=KC)),
        (w_lf[:, :, 0:LR], wi[:, :, C_LR:C_LR + LR]),
        (w_lf[:, :, LR:], wi[:, :, C_FF:C_FF + FH]),
    ]
    SMALL = 16 * (len(small) - 4)
    NKEY = (128, 256, PAST + NS_)

    def score(u):
        b = 4 + 2 * (u % 2)
        return psum[:, 512 * b:512 * b + 1024]

    def divide(dve, i, link):
        n = TN[i]
        dve.wait_ge(s["po_ps"], 8 * i + 8)
        link(dve.reciprocal(rinv[0:n, 8 * i:8 * i + 8], rsum[0:n, 8 * i:8 * i + 8]))
        dve.tensor_tensor(o_tok[0:n, i, 512:1024].rearrange("t (h d) -> t h d", h=FH),
                          bank[2 + i % 2][0:n, :].rearrange("t (h d) -> t h d", h=FH),
                          rinv[0:n, 8 * i:8 * i + 8].unsqueeze(2).broadcast_to([n, FH, FD]), ALU.mult).then_inc(s["po_ok"], 1)

    def num(eng, v):
        return v if isinstance(v, int) else eng.snap(v)

    def pair_blocks(eng, b):
        b = num(eng, b)
        further = eng.value_load(table[0:1, bass.ds(b, 1)], min_val=0, max_val=MAXB - 1)
        first = eng.value_load(table[0:1, bass.ds(num(eng, b + PAIRS), 1)], min_val=0, max_val=PAIRS * MAXB - 1)
        return further, first

    def expert_at(eng, at, largest):
        return eng.value_load(table[0:1, bass.ds(num(eng, at + 2 * PAIRS), 1)], min_val=0, max_val=largest)

    def each_block(eng, b, body):
        further, first = pair_blocks(eng, b)
        with eng.If(further > 0):
            with eng.Fori(0, further) as j:
                body(eng.snap(first + j), j, False)
        body(eng.snap(first + further), further, True)

    def total_blocks(eng):
        further, first = pair_blocks(eng, PAIRS - 1)
        return eng.snap(first + further + 1)

    def update(b, c):
        w = 2 * (b // 2) % 4 + c
        return bank[2 if b == 4 else b % 2][:, GV * w:GV * w + GV]

    def inter(i, q):
        if i == 2:
            return bank[q][:, 0:256]
        return bank[6 + q][:, 256 * i:256 * i + 256]

    def y_half(y, i, q):
        return y[0:TN[i], i, :].rearrange("t (p k) -> t k p", k=KC)[:, 4 * q:4 * q + 4, :]

    def silu_gate(i):
        return toks[0:TN[i], 1, i, :]

    @block.sync
    def _(sp):
        for i, (src, tn) in enumerate(((x_prompt[0, 0:128], 128), (x_prompt[0, 128:256], 128), (x_sample[0], 32))):
            sp.dma_start(x_tok[0:tn, i, :], src).then_inc(s["x_in"], 16)
        for n, (src, w) in enumerate(pieces):
            if waits_of[n] >= 0:
                m = waits_of[n]
                if FIRST_WIN <= m < FIRST_R1:
                    sp.wait_ge(s["wlo_ok"], 2 * (m - FIRST_WIN) + 2)
                else:
                    sp.wait_ge(s["w_used"], m + 1 if m < FIRST_WIN else m + 1 - len(GROUPS))
            dst = piece(n)[:, :]
            if w == 2:
                dst = dst.rearrange("p (k n) -> p k n", n=src.shape[2])
            sp.dma_start(dst, src).then_inc(ring_in[slots_of[n][0]], 16)
        sp.wait_ge(s["mT_ps"], KC)
        sp.wait_ge(s["kv_out"], 96)
        sp.wait_ge(s["st_out"], 64)
        sp.wait_ge(s["f_out"], 32)
        for q, w, k in ((0, w_sh_gate, KC), (1, w_sh_up, KC), (2, w_sh_down, 2)):
            sp.dma_start(ring[SHARED + q][:, :], w[0].rearrange("(p k) n -> p (k n)", k=k)).then_inc(ring_in[SHARED + q], 16)

        GATE_UP, DOWN = ((0, w_exp_gate, KC), (1, w_exp_up, KC)), ((2, w_exp_down, 2),)

        def expert(u, e, parts):
            for q, w, k in parts:
                src = w[0].rearrange("e (p k) n -> e p (k n)", k=k)[bass.ds(e, 1)].rearrange("e p n -> (e p) n")
                sp.dma_start(expert_w[u][:, q, :], src).then_inc(ring_in[3 * u + q], 16)

        expert(3, 3, GATE_UP + DOWN)
        sp.wait_ge(s["mix_ps"], KC)
        for u in range(2):
            expert(u, u, GATE_UP + DOWN)
        sp.wait_ge(s["dn_ps"], KC)
        expert(2, 2, GATE_UP + DOWN)
        sp.wait_ge(s["table_ok"], 1)
        with sp.Fori(1, PAIRS // 2) as it:
            for u in range(2):
                further, first = pair_blocks(sp, it * 2 + (u - 2))
                done = sp.snap(first + further + 1)
                ab = [expert_at(sp, it * 4 + (2 * u + x), E - 1) for x in range(2)]
                sp.wait_ge(s["pgu_ps"], done)
                for x in range(2):
                    expert(2 * u + x, ab[x], GATE_UP)
                sp.wait_ge(s["yd_ps"], done)
                for x in range(2):
                    expert(2 * u + x, ab[x], DOWN)

    @block.scalar
    def _(act):
        act.dma_start(cT[:, 0, :], c_prompt[0].rearrange("(p k) -> p k", k=KC)).then_inc(s["c_in"], 16)
        act.dma_start(cT[:, 1, :], c_sample[0].rearrange("(p k) -> p k", k=KC)).then_inc(s["c_in"], 16)
        act.wait_ge(s["c_in"], 32)
        act.activation(scT[:, :, :].rearrange("p k g -> p g k"), cT[:, :, :], ACT.Silu).then_inc(s["sc_ok"], 1)
        with nc.allow_non_contiguous_dma(reason="vectors of a few hundred elements"):
            for dst, src in small[:4]:
                act.dma_start(dst, src).then_inc(s["gains_in"], 16)
        for k in range(KC):
            act.wait_ge(s["xT_ok"], k + 1)
            act.activation(sq[:, k, :], xT[:, k, :], ACT.Square).then_inc(s["sq_ok"], 1)
        act.wait_ge(s["consts"], 1)
        act.wait_ge(s["ssq_ps"], 1)
        act.activation(rstdB[:, :], bank[6][:, 0:N], ACT.Sqrt, bias=epst[:, 0:1], scale=1.0 / D).then_inc(s["rstd_ok"], 1)
        with nc.allow_non_contiguous_dma(reason="vectors of a few hundred elements"):
            for dst, src in small[4:]:
                act.dma_start(dst, src).then_inc(s["small_in"], 16)
        act.dma_start(pastf[:, :, :], cache_fox_logf[0, 0].rearrange("(j p) h -> p j h", p=P)).then_inc(s["cache_in"], 16)
        for c in range(2):
            act.dma_start(states[:, 4, c, :], state_gla[0, 0, 2 * c:2 * c + 2].rearrange("h k v -> (h k) v")).then_inc(s["state_in"], 16)

        def ada_rows(r, b):
            act.wait_ge(s["w_used"], KC * (r + 1))
            act.wait_ge(s["row_zeros"], 1)
            if r:
                act.wait_ge(s["ada_T"], r)
            for j in range(4):
                act.copy(ada_row[32 * j:32 * j + 2, :], bank[b][32 * j:32 * j + 2, :]).then_inc(s["ada_row"], 1)

        ada_rows(0, 5)

        def split_hi(g):
            piece_in(act, FIRST_WIN + g // 2)
            if g >= 2:
                act.wait_ge(s["z_ps"], 2 * g - 2)
            act.copy(whi[g % 2][:, :, :], half_group(g)).then_inc(s["whi_ok"], 1)

        split_hi(0)
        act.wait_ge(s["gain_ok"], 2)
        act.wait_ge(s["xn_ok"], 1)
        for out, done in ((hhi, "hhi_act"), (hT, "hT_act")):
            for k in range(KC):
                act.activation(out[:, k, 0:NP_], xn[:, k, 0:NP_], ACT.Identity, bias=adaT[:, 0, 0, k:k + 1],
                               scale=gain1[:, 0, k:k + 1]).then_inc(s[done], 1)
        split_hi(1)
        for c in range(1, 24, 2):
            act.wait_ge(s["z_ps"], c + 1)
            b = bank[c % 4]
            if c < 2:
                last = act.mul(gqk[:, c, :], b[:, 0:N], GK ** -0.5)
            elif c < 4:
                last = act.copy(gqk[:, c, :], b[:, 0:N])
            elif 12 <= c < 16:
                act.mul(qA[0:FD, 2 * (c - 12), :], b[0:FD, 0:N], FD ** -0.5)
                last = act.mul(qA[0:FD, 2 * (c - 12) + 1, :], b[FD:P, 0:N], FD ** -0.5)
            elif 16 <= c < 20:
                act.copy(kA[0:FD, 2 * (c - 16), :], b[0:FD, 0:N])
                act.copy(kA[0:FD, 2 * (c - 16) + 1, :], b[FD:P, 0:N])
                last = act.copy(zt[:, 8 + c - 16, :], b[:, 0:N])
            else:
                last = act.copy(zt[:, c - 4 if c < 12 else c - 8, :], b[:, 0:N])
            last.then_inc(s["z_act"], 1)
            if c // 2 + 2 < 12:
                split_hi(c // 2 + 2)
        act.dma_start(cacheK[:, :, :], cache_fox_k[0, 0].rearrange("(j p) h d -> p j (h d)", p=P)).then_inc(s["cache_in"], 16)
        act.dma_start(cacheV[:, :, :], cache_fox_v[0, 0].rearrange("(j p) h d -> p j (h d)", p=P)).then_inc(s["cache_in"], 16)
        act.wait_ge(s["lr_ps"], 1)
        act.copy(glr[:, :], bank[4][0:LR, 0:N]).then_inc(s["glr_ok"], 1)
        act.wait_ge(s["lf_abs"], 1)
        act.activation(logf[:, :, :], lf_t[:, :, :], ACT.Exp, scale=-1.0).then_inc(s["a_chain"], 1)
        act.wait_ge(s["a_chain"], 1)
        act.activation(lf_t[:, :, :], logf[:, :, :], ACT.Ln, bias=1.0).then_inc(s["lf_ln"], 1)
        act.wait_ge(s["gate_abs"], 1)
        act.activation(g_c[:, :, :], g_a[:, :, :], ACT.Exp, scale=-1.0).then_inc(s["a_chain"], 1)
        act.wait_ge(s["a_chain"], 2)
        act.activation(g_a[:, :, :], g_c[:, :, :], ACT.Ln, bias=1.0).then_inc(s["gate_ln"], 1)
        for c in range(4):
            act.wait_ge(s["cK_ps"], c + 1)
            act.copy(kS[0:FD, 2 * c + 1, :], bank[c][FD:P, :]).then_inc(s["cK_act"], 1)
        act.wait_ge(s["cum_ok"], 4)
        act.activation(qe[:, :, :], g_a[:, :, :], ACT.Exp).then_inc(s["gexp_ok"], 1)
        act.activation(ke[:, :, :], g_a[:, :, :], ACT.Exp, scale=-1.0).then_inc(s["gexp_ok"], 1)
        act.activation(qb[:, :, :], g_t[:, :, :], ACT.Exp).then_inc(s["gexp_ok"], 1)
        act.activation(kl[:, :, :], g_b[:, :, :], ACT.Exp).then_inc(s["gexp_ok"], 1)
        act.activation(dec[:, :, 0:4], g_t[:, :, BLK - 1:NP_:BLK], ACT.Exp).then_inc(s["gexp_ok"], 1)
        act.activation(dec[:, :, 4:5], g_t[:, :, N - 1:N], ACT.Exp).then_inc(s["gexp_ok"], 1)
        for i in range(3):
            act.wait_ge(s["tok_ps"], 3 + i + 1)
            act.activation(silu_gate(i), bank[4 + i][0:TN[i], :], ACT.Silu).then_inc(s["tok_act"], 1)
        ada_rows(1, 7)
        act.wait_ge(s["zeros"], 2)
        squares = [0]

        def square(i, j):
            lo, hi = (GV * j, GV * j + GV) if j < 4 else (512, 1024)
            if squares[0]:
                act.wait_ge(s["ssq_act"], squares[0])
            act.activation(junk[0:TN[i], 0:hi - lo], o_tok[0:TN[i], i, lo:hi], ACT.Square,
                           accum_out=ssq5[0:TN[i], i, j:j + 1]).then_inc(s["ssq_act"], 1)
            squares[0] += 1

        for u in range(24):
            i = u // 8
            act.wait_ge(s["max_ok"], u + 1)
            if u >= 2:
                act.wait_ge(s["pT_ps"], u - 1)
            act.activation(prob[u % 2][0:TN[i], 0:NKEY[i]], score(u)[0:TN[i], 0:NKEY[i]], ACT.Exp, bias=nmax[0:TN[i], u:u + 1],
                           accum_out=rsum[0:TN[i], u:u + 1]).then_inc(s["exp_ok"], 1)
            if u == KC:
                ada_rows(2, 3)
            if u < 12:
                square(u // 4, u % 4)
        act.wait_ge(s["po_ok"], 2)
        square(0, 4)
        square(1, 4)
        act.activation(rs5[:, :, 0:4], ssq5[:, :, 0:4], ACT.Sqrt, bias=epst[:, 0:1], scale=1.0 / GV).then_inc(s["rs_act"], 1)
        act.wait_ge(s["po_ok"], 3)
        square(2, 4)
        act.wait_ge(s["ssq_act"], 15)
        act.activation(rs5[:, :, 4:5], ssq5[:, :, 4:5], ACT.Sqrt, bias=epst[:, 0:1], scale=1.0 / 512).then_inc(s["rs_act"], 1)
        for j in range(0, 8, 2):
            act.wait_ge(s["mT_ps"], j + 1)
            act.mul(mT[:, j, :], bank[j % 4][:, 0:N], g_gla[:, 0:1] if j < 4 else g_fox[:, j - 4:j - 3]).then_inc(s["mT_act"], 1)
        for k in range(KC):
            act.wait_ge(s["x1_ok"], k + 1)
            act.activation(sq1[:, k, :], xT[:, k, :], ACT.Square).then_inc(s["x2_sq"], 1)
        act.wait_ge(s["ssq_ps"], 2)
        act.activation(rstdB[:, :], bank[6][:, 0:N], ACT.Sqrt, bias=epst[:, 0:1], scale=1.0 / D).then_inc(s["rstd_ok"], 1)
        for k in range(KC):
            act.wait_ge(s["h2n_ok"], k + 1)
            act.activation(h2T[:, k, 0:NP_], h2T[:, k, 0:NP_], ACT.Identity, bias=adaT[:, 3, 0, k:k + 1],
                           scale=gain2[:, 0, k:k + 1]).then_inc(s["h2_ok"], 1)
        act.wait_ge(s["rt_ps"], 1)
        act.activation(scoreT[:, :], bank[5][0:E, 0:N], ACT.Sigmoid).then_inc(s["rt_sc"], 1)
        for q in range(6):
            i = q // 2
            if q == 4:
                act.wait_ge(s["gu_ps"], 3)
                for j in range(2):
                    act.activation(sil[:, j, :], bank[j][:, 0:N], ACT.Silu).then_inc(s["sil_ok"], 1)
            act.wait_ge(s["h2t_ps"], q + 1)
            if q == 4:
                act.wait_ge(s["iota_ok"], 5)
            act.copy(h2hl[0:TN[i], 2 * i, 4 * (q % 2):4 * (q % 2) + 4, :], bank[4 + q % 2][0:TN[i], :].rearrange("t (k p) -> t k p", k=4)).then_inc(s["h2hi_ok"], 1)
        for k in range(KC):
            act.wait_ge(s["dn_ps"], k + 1)
            act.copy(acc[:, k, :], bank[5 + k % 2][:, 0:N]).then_inc(s["acc_ok"], 1)
        act.wait_ge(s["table_ok"], 1)

        def slots_in(n):
            for q in range(2):
                act.wait_ge(s["xs_ps"], num(act, n * 2 + (q + 1)))
                act.copy(xs[:, 4 * q:4 * q + 4, :], bank[q][:, :].rearrange("p (k n) -> p k n", k=4)).then_inc(s["xs_ok"], 1)

        def gathered(n):
            act.wait_ge(s["xg_ps"], num(act, n + 1))
            for q in range(2):
                last = act.copy(xg[:, 4 * q:4 * q + 4, :], bank[q][:, :].rearrange("p (k n) -> p k n", k=4))
            last.then_inc(s["xg_ok"], 1)

        def act_block(n):
            act.wait_ge(s["pgu_ps"], num(act, n + 1))
            act.activation(silg[:, :], bank[3][:, 0:DE], ACT.Silu).then_inc(s["sl_ok"], 1)
            slots_in(n + 1)
            act.wait_ge(s["hidT_ps"], num(act, n + 1))
            act.copy(hidT[:, :, :], bank[4][:, 0:2 * P].rearrange("p (j n) -> p j n", j=2)).then_inc(s["hidT_ok"], 1)
            gathered(n + 1)
            act.wait_ge(s["yd_ps"], num(act, n + 1))
            act.copy(yhi[:, :], psum[:, 4 * 512:6 * 512]).then_inc(s["yhi_ok"], 1)

        slots_in(0)
        gathered(0)
        with act.Fori(0, PAIRS // 2) as it:
            for u in range(2):
                each_block(act, it * 2 + u, lambda n, j, last: act_block(n))
        for k in range(KC):
            act.wait_ge(s["fin_ok"], k + 1)
            act.activation(sq2[:, k, :], acc[:, k, :], ACT.Square).then_inc(s["x2_sq"], 1)
            if k % 2 == 0:
                act.mul(yT[:, k, :], acc[:, k, :], g_fin[:, k:k + 1]).then_inc(s["y_act"], 1)
        act.wait_ge(s["ssqT_ps"], 1)
        for i in range(3):
            act.activation(rstdT[0:TN[i], i:i + 1], bank[6][0:TN[i], i:i + 1], ACT.Sqrt, bias=epst[0:TN[i], 0:1],
                           scale=1.0 / D).then_inc(s["rstdT_ok"], 1)
        for i in range(3):
            dst = y_sample[0] if i == 2 else y_prompt[0, 128 * i:128 * i + 128]
            act.wait_ge(s["rinv_ok"], i + 1)
            act.mul(y_half(yout, i, 0), bank[2 * i][0:TN[i], :].rearrange("t (k p) -> t k p", k=4),
                    rstdT[0:TN[i], i:i + 1]).then_inc(s["y_ok"], 1)
            act.wait_ge(s["y_ok"], i + 1)
            act.wait_ge(s["y_ok_dve"], i + 1)
            act.dma_start(dst, yout[0:TN[i], i, :]).then_inc(s["out_done"], 16)
        act.wait_ge(s["out_done"], 48)

    @block.gpsimd
    def _(pool):
        z = s["zeros"]
        pool.memset(ident[:, :], 0.0).then_inc(z, 1)
        pool.memset(ssq5[:, :, :], 1.0).then_inc(z, 1)
        pool.memset(identb[:, :], 0.0).then_inc(z, 1)
        pool.memset(ones[:, :], 1.0).then_inc(z, 1)
        pool.memset(causal[:, :], 0.0).then_inc(z, 1)
        pool.memset(epst[:, :], EPS).then_inc(z, 1)
        pool.wait_ge(z, 6)
        for t in (ident, identb):
            pool.affine_select(out=t[:, :], in_=t[:, :], compare_op=ALU.not_equal, fill=1.0, base=0,
                               pattern=[[-1, P]], channel_multiplier=1).then_inc(z, 1)
        pool.affine_select(out=upper[:, :], in_=ones[:, :], compare_op=ALU.is_ge, fill=0.0, base=0,
                           pattern=[[1, P]], channel_multiplier=-1).then_inc(z, 1)
        pool.affine_select(out=lower[:, :], in_=ones[:, :], compare_op=ALU.is_gt, fill=0.0, base=0,
                           pattern=[[-1, P]], channel_multiplier=1).then_inc(z, 1)
        pool.wait_ge(z, 10)
        pool.affine_select(out=glamask[0:BLK, :], in_=ones[0:BLK, 0:BLK], compare_op=ALU.is_ge, fill=0.0, base=0,
                           pattern=[[1, BLK]], channel_multiplier=-1).then_inc(z, 1)
        pool.wait_ge(z, 11)
        pool.affine_select(out=before[:, :], in_=ones[:, :], compare_op=ALU.is_gt, fill=0.0, base=0,
                           pattern=[[1, P]], channel_multiplier=-1).then_inc(z, 1)
        pool.wait_ge(z, 12)
        pool.affine_select(out=glamask[BLK:P, :], in_=ones[BLK:P, 0:BLK], compare_op=ALU.is_ge, fill=0.0, base=0,
                           pattern=[[1, BLK]], channel_multiplier=-1).then_inc(z, 1)
        pool.wait_ge(z, 13)
        pool.affine_select(out=causal[:, :], in_=causal[:, :], compare_op=ALU.is_ge, fill=NEG, base=0,
                           pattern=[[-1, P]], channel_multiplier=1).then_inc(s["consts"], 1)
        pool.wait_ge(s["consts"], 1)
        pool.memset(qA[FD:FD + 2, :, :], 1.0).then_inc(s["ones_ok"], 1)
        pool.wait_ge(s["ones_ok"], 1)
        pool.memset(kA[FD:FD + 2, :, :], 1.0).then_inc(s["ones_ok"], 1)
        pool.wait_ge(s["ones_ok"], 2)
        pool.memset(a_t[:, :, :, :, :], 0.0).then_inc(z, 1)
        pool.wait_ge(z, 14)
        pool.memset(ada_row[:, :], 0.0).then_inc(s["row_zeros"], 1)
        pool.wait_ge(s["row_zeros"], 1)
        pool.wait_ge(s["z_ps"], 24)
        pool.memset(kS[FD:FD + 2, :, :], 1.0).then_inc(s["ones_ok"], 1)
        pool.wait_ge(s["ones_ok"], 3)
        pool.wait_ge(s["logf_ok"], 1)
        pool.dma_start(f_prompt[0, 0].rearrange("(i p) h -> p i h", p=P), logf[:, 0:2, :]).then_inc(s["f_out"], 16)
        pool.dma_start(f_sample[0, 0], logf[0:NS_, 2, :]).then_inc(s["f_out"], 16)
        pool.wait_ge(s["crow_ok"], 3)
        pool.dma_start(crow_d.rearrange("a h n -> h a n"), crow[:, :, :]).then_inc(s["crow_out"], 16)
        pool.dma_start(srow_d, srow[:, :]).then_inc(s["crow_out"], 16)
        pool.wait_ge(s["crow_out"], 32)
        pool.wait_ge(s["ones_ok"], 3)
        pool.dma_start(qA[FD + 1:FD + 2, :, :], crow_d[0:1]).then_inc(s["rows_in"], 16)
        pool.dma_start(kA[FD:FD + 1, :, :], crow_d[1:2]).then_inc(s["rows_in"], 16)
        pool.dma_start(kS[FD:FD + 1, :, :], srow_d.rearrange("(o h) n -> o h n", o=1)).then_inc(s["rows_in"], 16)
        pool.wait_ge(s["state_ok"], 10)
        for c in range(2):
            pool.dma_start(st_prompt[0, 0, 2 * c:2 * c + 2].rearrange("h k v -> (h k) v"), states[:, 3, c, :]).then_inc(s["st_out"], 16)
            pool.dma_start(st_sample[0, 0, 2 * c:2 * c + 2].rearrange("h k v -> (h k) v"), states[:, 5, c, :]).then_inc(s["st_out"], 16)
        pool.wait_ge(s["tok_dve"], 9)
        for q, (kp, ks_) in enumerate(((k_prompt, k_sample), (v_prompt, v_sample))):
            for i in range(2):
                pool.dma_start(kp[0, 0, 128 * i:128 * i + 128].rearrange("t h d -> t (h d)"), toks[:, 2 + q, i, :]).then_inc(s["kv_out"], 16)
            pool.dma_start(ks_[0, 0].rearrange("t h d -> t (h d)"), toks[0:NS_, 2 + q, 2, :]).then_inc(s["kv_out"], 16)

        def sum_squares(out, src, chunks, squared, summed):
            for k in range(1, chunks):
                pool.wait_ge(s["x2_sq"], squared + k + 1)
                if k > 1:
                    pool.wait_ge(s["sqsum_ok"], summed + k - 1)
                pool.tensor_tensor(out[:, :], src[:, 0, :] if k == 1 else out[:, :], src[:, k, :], ALU.add).then_inc(s["sqsum_ok"], 1)

        sum_squares(sqsum1, sq1, KC - 1, 0, 0)
        pool.wait_ge(s["x1_ok"], KC)
        pool.wait_ge(s["kv_out"], 96)
        pool.memset(sc[:, :, :], 0.0)
        for w in (NG, E):
            last = pool.memset(restart[w][:, :], 1.0)
        last.then_inc(s["rt_zeros"], 1)
        pool.wait_ge(s["rt_zeros"], 1)
        for w in (NG, E):
            last = pool.memset(restart[w][:, ::w], 0.0)
        last.then_inc(s["rt_zeros"], 1)
        pool.wait_ge(s["rt_zeros"], 2)
        pool.iota(tie_i[:, 0:E], pattern=[[-1, E]], base=E - 1, channel_multiplier=0)
        pool.iota(tie_i[:, E:E + 1], pattern=[[0, 1]], base=E - 1, channel_multiplier=-1).then_inc(s["rt_zeros"], 1)
        pool.wait_ge(s["rt_zeros"], 3)
        pool.iota(tie_i[:, 0:EARLY], pattern=[[-FIRST_KEY, EARLY]], base=EARLY * FIRST_KEY, channel_multiplier=0)
        pool.iota(tie_i[0:EARLY, E:E + 1], pattern=[[0, 1]], base=EARLY * FIRST_KEY, channel_multiplier=-FIRST_KEY).then_inc(s["rt_zeros"], 1)
        pool.wait_ge(s["rt_zeros"], 4)
        pool.tensor_copy(tie[:, :], tie_i[:, :]).then_inc(s["rt_zeros"], 1)
        pool.wait_ge(s["rt_zeros"], 5)
        pool.iota(tie_i[:, 0:1], pattern=[[0, 1]], base=0, channel_multiplier=1).then_inc(s["rt_zeros"], 1)
        pool.wait_ge(s["rt_zeros"], 6)
        pool.tensor_copy(e_col[:, :], tie_i[:, 0:1]).then_inc(s["rt_zeros"], 1)
        pool.wait_ge(s["rt_zeros"], 7)
        pool.iota(rank_i[:, 0:EARLY], pattern=[[1, EARLY]], base=0, channel_multiplier=0)
        turns = (E - EARLY) // (2 * SPREAD)
        pool.iota(rank_i[:, EARLY:E].rearrange("p (i j x) -> p i j x", i=turns, j=SPREAD),
                  pattern=[[2, turns], [2 * turns, SPREAD], [1, 2]], base=EARLY, channel_multiplier=0).then_inc(s["rt_zeros"], 1)
        pool.wait_ge(s["rt_zeros"], 8)
        pool.tensor_copy(rank_at[:, :], rank_i[:, :]).then_inc(s["rt_zeros"], 1)
        pool.wait_ge(s["rt_zeros"], 9)
        pool.iota(iota_i[:, :], pattern=[[1, MAXB * CAP]], base=0, channel_multiplier=0).then_inc(s["iota_ok"], 1)
        pool.wait_ge(s["iota_ok"], 1)
        pool.tensor_copy(iota[:, :], iota_i[:, :]).then_inc(s["iota_ok"], 1)
        pool.wait_ge(s["iota_ok"], 2)
        pool.memset(posm[:, :, :], -1.0).then_inc(s["iota_ok"], 1)
        pool.wait_ge(s["iota_ok"], 3)
        pool.memset(w_hl[:, :, :, :].bitcast(F32), 0.0).then_inc(s["iota_ok"], 1)
        pool.wait_ge(s["iota_ok"], 4)
        pool.wait_ge(s["ssq_ps"], 2)
        pool.memset(h2hl[:, 4, :, :].bitcast(F32), 0.0).then_inc(s["iota_ok"], 1)
        pool.wait_ge(s["st_out"], 64)
        pool.wait_ge(s["f_out"], 32)

        sum_squares(sqsum2, sq2, KC, KC, KC - 2)

    @block.tensor
    def _(pe):
        mm, tr = nc.tensor.matmul, nc.tensor.transpose
        pe.wait_ge(s["consts"], 1)
        pe.wait_ge(s["x_in"], 48)
        for k in range(KC):
            if k >= 4:
                pe.wait_ge(s["xT_ok"], k - 3)
            for i in range(3):
                last = tr(bank[k % 4][:, T0[i]:T0[i] + TN[i]], x_tok[0:TN[i], i, k::KC], ident[0:TN[i], 0:TN[i]])
            last.then_inc(s["xT_ps"], 1)

        for k in range(KC):
            pe.wait_ge(s["sq_ok"], k + 1)
            last = mm(bank[6][:, 0:N], ones[:, :], sq[:, k, :], start=k == 0, stop=k == KC - 1)
        last.then_inc(s["ssq_ps"], 1)

        def ada(r, k, b):
            n = k if r == 0 else FIRST_R1 + KC * (r - 1) + k
            piece_in(pe, n)
            cols = piece(n)[:, :].rearrange("p (m q j) -> p m j q", m=2, j=KC)
            for j in range(4):
                last = mm(bank[b][32 * j:32 * j + 2, :].rearrange("g (j q) -> g j q", j=4), scT[:, k, :],
                          cols[:, j // 2, 4 * (j % 2):4 * (j % 2) + 4, :], start=k == 0, stop=k == KC - 1, tile_position=(0, 32 * j))
            last.then_inc(s["w_used"], 1)

        def ada_T(r, b):
            pe.wait_ge(s["ada_row"], 4 * r + 4)
            for j in range(4):
                last = tr(bank[b][:, P * j:P * j + P], ada_row[:, P * j:P * j + P], ident[:, :])
            last.then_inc(s["ada_T"], 1)

        pe.wait_ge(s["sc_ok"], 1)
        for k in range(KC):
            ada(0, k, 5)
        ada_T(0, 7)

        for c in range(24):
            g, q = c // 2, c % 2
            if c >= 4:
                pe.wait_ge(s["z_act" if c % 2 else "z_dve"], (c - 4) // 2 + 1)
            for w, h in ((whi, hhi), (wlo, hhi), (whi, hlo)):
                pe.wait_ge(s["whi_ok" if w is whi else "wlo_ok"], g + 1)
                for k in range(KC):
                    if c == 0 and h is hhi and w is whi:
                        pe.wait_ge(s["hhi_act"], k + 1)
                        pe.wait_ge(s["hhi_dve"], k + 1)
                    if c == 0 and h is hlo:
                        pe.wait_ge(s["hlo_ok"], k + 1)
                    last = mm(bank[c % 4][:, 0:N], w[g % 2][:, k, P * q:P * q + P], h[:, k, :],
                              start=k == 0 and w is whi and h is hhi, stop=k == KC - 1 and h is hlo)
            last.then_inc(s["z_ps"], 1)
        pe.wait_ge(s["hT_act"], KC)
        pe.wait_ge(s["hT_dve"], KC)
        pe.wait_ge(s["small_in"], SMALL)
        for k in range(KC):
            last = mm(bank[4][0:LR, 0:N], w_lf[:, k, 0:LR], hT[:, k, :], start=k == 0, stop=k == KC - 1)
        last.then_inc(s["lr_ps"], 1)
        for i in range(3):
            for k in range(KC):
                last = mm(bank[5][0:TN[i], FH * i:FH * i + FH], hT[:, k, T0[i]:T0[i] + TN[i]], w_lf[:, k, LR:],
                          start=k == 0, stop=k == KC - 1)
        last.then_inc(s["narrow_ps"], 1)
        pe.wait_ge(s["glr_ok"], 1)
        for c in range(2):
            last = mm(bank[6 + c][:, 0:N], w_gk2[:, P * c:P * c + P], glr[:, :], start=True, stop=True)
        last.then_inc(s["gate_ps"], 1)
        pe.wait_ge(s["z_act"], 12)
        pe.wait_ge(s["z_dve"], 12)
        pe.wait_ge(s["cache_in"], 48)
        for c in range(4):
            for j in range(4):
                last = tr(bank[c][:, P * j:P * j + P], cacheK[:, j, P * c:P * c + P], ident[:, :])
            last.then_inc(s["cK_ps"], 1)
        pe.wait_ge(s["logf_ok"], 1)
        pe.wait_ge(s["ff_ok"], 1)
        cb = bank[4]
        mm(cb[0:FH, 0:128], logf[:, 0, :], upper[:, :], start=True, stop=True)
        mm(cb[0:FH, 128:256], logf[:, 0, :], ones[:, :], start=True, stop=False)
        mm(cb[0:FH, 128:256], logf[:, 1, :], upper[:, :], start=False, stop=True)
        mm(cb[0:FH, 256:N], logf[0:NS_, 2, :], upper[0:NS_, 0:NS_], start=True, stop=True).then_inc(s["crow_ps"], 1)
        for j in range(4):
            for t in range(j, 4):
                last = mm(bank[5][0:FH, P * j:P * j + P], pastf[:, t, :], (lower if t == j else ones)[:, :],
                          start=t == j, stop=t == 3)
        last.then_inc(s["crow_ps"], 1)
        pe.wait_ge(s["gate_x"], 1)
        for k in range(6):
            ada(1, k, 7)
        pe.wait_ge(s["crow_ok"], 3)
        for q in range(12):
            kind, i = q // 3, q % 3
            if kind:
                pe.wait_ge(s["tok_act" if kind == 2 else "tok_dve"], i + 1 + (3 if kind == 3 else 0))
            for j in range(4):
                last = tr(bank[4 + i][0:TN[i], P * j:P * j + P], zt[:, 4 * kind + j, T0[i]:T0[i] + TN[i]], ident[:, :])
            last.then_inc(s["tok_ps"], 1)
            if q in (7, 9):
                ada(1, 6 + (q - 7) // 2, 7)
        pe.wait_ge(s["tok_dve"], 9)
        pe.wait_ge(s["tok_act"], 3)
        pe.wait_ge(s["gprod_ok"], 4)
        for i in range(3):
            for c in range(2):
                o = 256 * (i % 2) + P * c
                last = tr(bank[4 + i // 2][0:TN[i], o:o + P], kl[:, c, T0[i]:T0[i] + TN[i]], ident[:, :])
        last.then_inc(s["klT_ps"], 1)
        pe.wait_ge(s["cK_act"], 4)
        pe.wait_ge(s["cK_dve"], 4)
        ada_T(1, 3)

        def blocks():
            for b in range(5):
                i, pb, n = b // 2, 64 * (b % 2), BLK if b < 4 else NS_
                yield b, i, pb, n
        for b, i, pb, n in blocks():
            for h in range(GH):
                r, c = 64 * (h % 2), h // 2
                t0 = T0[i] + pb
                o = P * i + BLK * c
                last = mm(bank[6 + h % 2][pb:pb + n, o:o + n], ke[r:r + GK, c, t0:t0 + n], qe[r:r + GK, c, t0:t0 + n],
                          start=True, stop=True)
        last.then_inc(s["aT_ps"], 1)
        pe.wait_ge(s["klT_ok"], 1)
        for b, i, pb, n in blocks():
            for h in range(GH):
                r, c = 64 * (h % 2), h // 2
                last = mm(update(b, c)[r:r + GK, :], kl_tok[pb:pb + n, i, GK * h:GK * h + GK],
                          toks[pb:pb + n, 0, i, GV * h:GV * h + GV], start=True, stop=True)
        last.then_inc(s["upd_ps"], 1)
        pe.wait_ge(s["aT_ok"], 4)
        pe.wait_ge(s["ada_ok"], 2)
        pe.wait_ge(s["state_ok"], 10)
        for b, i, pb, n in blocks():
            for h in range(GH):
                r, c = 64 * (h % 2), h // 2
                t0 = T0[i] + pb
                mm(bank[3 + i][pb:pb + n, GV * h:GV * h + GV], a_t[pb:pb + n, h % 2, i, c, 0:n],
                   toks[pb:pb + n, 0, i, GV * h:GV * h + GV], start=True, stop=True)
                if b:
                    last = mm(inter(i, h % 2)[pb:pb + n, GV * c:GV * c + GV], qb[r:r + GK, c, t0:t0 + n],
                              states[r:r + GK, b - 1 if b < 4 else 4, c, :], start=True, stop=True)
            if b % 2 or b == 4:
                last.then_inc(s["go_ps"], 1)
        pe.wait_ge(s["rows_in"], 48)

        def scores(u):
            i, h = u // 8, u % 8
            if u < 2:
                pe.wait_ge(s["go_ok"], 3)
            else:
                pe.wait_ge(s["exp_ok"], u - 1)
            q = qA[:, h, T0[i]:T0[i] + TN[i]]
            out = score(u)[0:TN[i]]
            if i < 2:
                d = P * i
                if i:
                    mm(out[:, 0:P], q, kA[:, h, 0:P], start=True, stop=True)
                mm(out[:, d:d + P], q, kA[:, h, d:d + P], start=True, stop=False)
                last = mm(out[:, d:d + P], identb[:, :], causal[:, :], start=False, stop=True)
            else:
                mm(out[:, 0:PAST], q, kS[:, h, :], start=True, stop=True)
                mm(out[:, PAST:PAST + NS_], q, kA[:, h, NP_:N], start=True, stop=False)
                last = mm(out[:, PAST:PAST + NS_], identb[0:NS_, 0:NS_], causal[0:NS_, 0:NS_], start=False, stop=True)
            last.then_inc(s["sc_ps"], 1)

        def transposed(u):
            i, n = u // 8, TN[u // 8]
            pe.wait_ge(s["exp_ok"], u + 1)
            if u >= 2:
                pe.wait_ge(s["pT_ok"], u - 1)
            for t in range((NKEY[i] + P - 1) // P):
                w = min(P, NKEY[i] - P * t)
                last = tr(bank[u % 2][0:w, n * t:n * t + n], prob[u % 2][0:n, P * t:P * t + w], ident[0:n, 0:n])
            last.then_inc(s["pT_ps"], 1)

        def values(u):
            i, h, n = u // 8, u % 8, TN[u // 8]
            pe.wait_ge(s["pT_ok"], u + 1)
            if h == 0 and i == 1:
                pe.wait_ge(s["ada_ok"], 3)
            if h == 0 and i == 2:
                pe.wait_ge(s["po_ok"], 1)
            nt = (NKEY[i] + P - 1) // P
            for t in range(nt):
                w = min(P, NKEY[i] - P * t)
                v = cacheV[:, t, FD * h:FD * h + FD] if i == 2 and t < 4 else toks[0:w, 3, 2 if i == 2 else t, FD * h:FD * h + FD]
                last = mm(bank[2 + i % 2][0:n, FD * h:FD * h + FD], probT[u % 2][0:w, n * t:n * t + n], v, start=t == 0, stop=t == nt - 1)
            last.then_inc(s["po_ps"], 1)

        scores(0)
        for u in range(24):
            if u + 1 < 24:
                scores(u + 1)
            transposed(u)
            if u:
                values(u - 1)
            if u < KC:
                ada(2, u, 3)
            if u == KC:
                ada_T(2, 3)
        values(23)
        pe.wait_ge(s["exp_ok"], 24)
        pe.wait_ge(s["po_ok"], 3)
        for j in range(8):
            if j >= 4:
                pe.wait_ge(s["mT_dve" if j % 2 else "mT_act"], (j - 4) // 2 + 1)
            for i in range(3):
                pe.wait_ge(s["on_ok"], 3)
                last = tr(bank[j % 4][:, T0[i]:T0[i] + TN[i]], o_tok[0:TN[i], i, P * j:P * j + P], ident[0:TN[i], 0:TN[i]])
            last.then_inc(s["mT_ps"], 1)
        pe.wait_ge(s["mT_act"], 4)
        pe.wait_ge(s["mT_dve"], 4)
        piece_in(pe, FIRST_WO)
        piece_in(pe, FIRST_WO + 1)
        for k in range(KC):
            if k >= 4:
                pe.wait_ge(s["x1_ok"], k - 3)
            for j in range(8):
                w = piece(FIRST_WO + j // 4)[:, :].rearrange("p (j n) -> p j n", j=4)[:, j % 4, k::KC]
                last = mm(bank[k % 4][:, 0:N], w, mT[:, j, :], start=j == 0, stop=j == 7)
            last.then_inc(s["mix_ps"], 1)
        pe.wait_ge(s["sqsum_ok"], KC - 2)
        mm(bank[6][:, 0:N], ones[:, :], sqsum1[:, :], start=True, stop=False)
        pe.wait_ge(s["x2_sq"], KC)
        mm(bank[6][:, 0:N], ones[:, :], sq1[:, KC - 1, :], start=False, stop=True).then_inc(s["ssq_ps"], 1)
        for k in range(KC):
            pe.wait_ge(s["h2_ok"], k + 1)
            pe.wait_ge(s["h2s_ok"], k + 1)
            last = mm(bank[5][0:E, 0:N], w_rt[:, k, :], h2T[:, k, :], start=k == 0, stop=k == KC - 1)
        last.then_inc(s["rt_ps"], 1)

        def down(q0, wait_dn):
            wt = ring[q0 + 2][:, :].rearrange("p (j n) -> p j n", j=2)
            for k in range(KC):
                wait_dn(k)
                for j in range(2):
                    last = mm(bank[5 + k % 2][:, 0:N], wt[:, j, k::KC], actT[:, j, :], start=j == 0, stop=j == 1)
                last.then_inc(s["dn_ps"], 1)

        for q in range(3):
            pe.wait_ge(ring_in[SHARED + q], 16)

        def shared_gate_up(j, w):
            wt = ring[SHARED + w][:, :].rearrange("p (k n) -> p k n", k=KC)
            for k in range(KC):
                last = mm(bank[j + 2 * w][:, 0:N], wt[:, k, j::2], h2T[:, k, :], start=k == 0, stop=k == KC - 1)
            last.then_inc(s["gu_ps"], 1)

        def h2_tokens(i):
            for q in (2 * i, 2 * i + 1):
                if q >= 2:
                    pe.wait_ge(s["h2lo_ok"], q - 1)
                for k in range(4):
                    last = tr(bank[4 + q % 2][0:TN[i], P * k:P * k + P], h2T[:, 4 * (q % 2) + k, T0[i]:T0[i] + TN[i]], ident[:, :])
                last.then_inc(s["h2t_ps"], 1)

        shared_gate_up(0, 0)
        pe.wait_ge(s["rt_sc"], 1)
        for i in range(3):
            last = tr(bank[7][0:TN[i], E * i:E * i + E], scoreT[:, T0[i]:T0[i] + TN[i]], ident[0:E, 0:E])
        last.then_inc(s["rtT_ps"], 1)
        h2_tokens(0)
        shared_gate_up(0, 1)
        shared_gate_up(1, 0)
        h2_tokens(1)
        shared_gate_up(1, 1)
        h2_tokens(2)
        pe.wait_ge(s["wrt_ok"], 1)
        pb = bank[7]
        for i in range(3):
            n = TN[i]
            for j in range(i):
                mm(pb[0:n, E * i:E * i + E], ones[:, 0:n], ch[:, j, :], start=j == 0, stop=False)
            mm(pb[0:n, E * i:E * i + E], before[0:n, 0:n], ch[0:n, i, :], start=i == 0, stop=True)
        for i in range(3):
            mm(pb[0:E, 3 * E:4 * E], ones[0:TN[i], 0:E], ch[0:TN[i], i, :], start=i == 0, stop=i == 2)
        for i in range(3):
            last = mm(pb[0:E, 4 * E:4 * E + 1], ch[0:TN[i], i, :], ones[0:TN[i], 0:1], start=i == 0, stop=i == 2)
        last.then_inc(s["pos_ps"], 1)
        pe.wait_ge(s["h2lo_ok"], 6)
        pe.wait_ge(s["rank_ok"], 1)
        mm(bank[4][0:1, 0:E], e_col[:, :], onehot[:, :], start=True, stop=True)
        mm(bank[4][0:1, E:2 * E], c_col[:, :], onehot[:, :], start=True, stop=True).then_inc(s["order_ps"], 1)
        pe.wait_ge(s["act_ok"], 2)
        pe.wait_ge(s["rstd_ok"], 2)
        down(SHARED, lambda k: pe.wait_ge(s["acc_ok"], k - 1) if k >= 2 else None)
        pe.wait_ge(s["acc_ok"], KC)
        pe.wait_ge(s["iota_ok"], 5)
        pe.wait_ge(s["table_ok"], 1)

        def gather(n, q):
            pe.wait_ge(s["sel_ok"], num(pe, n + 1))
            for t in range(5):
                last = mm(bank[q][:, :], sel[:, t // 2, :, :], h2hl[:, t, 4 * q:4 * q + 4, :], start=t == 0, stop=t == 4)
            last.then_inc(s["xs_ps"], 1)

        def gather_T(n, q):
            pe.wait_ge(s["xs_ok"], num(pe, n * 2 + (q + 1)))
            for k in range(4):
                last = tr(bank[q][:, P * k:P * k + P], xs[:, 4 * q + k, :], ident[:, :])
            if q:
                last.then_inc(s["xg_ps"], 1)

        def combine(n, k):
            pe.wait_ge(s["acc_ok"], num(pe, n * KC + (KC + k - 1)))
            mm(bank[6 + k % 2][:, 0:N], yhi[:, k::KC], comb[:, :], start=True, stop=False)
            mm(bank[6 + k % 2][:, 0:N], ylo[:, k::KC], comb[:, :], start=False, stop=True).then_inc(s["comb_ps"], 1)

        def pe_block(u, n, b):
            pe.wait_ge(s["comb_ok"], num(pe, n + 1))
            for i in range(3):
                tr(bank[2][:, P * i:P * i + P], sel[:, i, :, :].bitcast(F32), ident[:, :])
            for i in range(3):
                last = mm(bank[2][:, 3 * P:3 * P + 4], sel[:, i, :, :], wp[:, i, :, :], start=i == 0, stop=i == 2)
            last.then_inc(s["slots_ps"], 1)
            for q in range(6):
                pe.wait_ge(ring_in[6 * u + q], num(pe, b * 8 + (16 + 16 * loads[6 * u + q] - 8 * u)))
            pe.wait_ge(s["xg_ok"], num(pe, n + 1))
            for k in range(KC):
                for x in ((0, 1) if k % 2 == 0 else (1, 0)):
                    last = mm(bank[3][CAP * x:CAP * x + CAP, :].rearrange("p (g n) -> p g n", g=2), xg[:, k, CAP * x:CAP * x + CAP],
                              expert_w[2 * u + x][:, 0:2, DE * k:DE * k + DE], start=k == 0, stop=k == KC - 1,
                              tile_position=(0, CAP * x))
            last.then_inc(s["pgu_ps"], 1)

            gather(n + 1, 0)
            pe.wait_ge(s["ylo_ok"], num(pe, n + 1))
            combine(n, 0)
            gather(n + 1, 1)
            combine(n, 1)
            pe.wait_ge(s["hid_ok"], num(pe, n + 1))
            for i in range(2):
                last = tr(bank[4][:, P * i:P * i + P], hid[:, i::2], ident[:, :])
            last.then_inc(s["hidT_ps"], 1)
            combine(n, 2)
            gather_T(n + 1, 0)
            combine(n, 3)
            gather_T(n + 1, 1)
            combine(n, 4)
            combine(n, 5)
            pe.wait_ge(s["hidT_ok"], num(pe, n + 1))
            for half in range(2):
                for i in range(2):
                    for x in range(2):
                        o = D * i + 512 * half
                        last = mm(bank[4 + half][CAP * x:CAP * x + CAP, :], hidT[:, i, CAP * x:CAP * x + CAP],
                                  expert_w[2 * u + x][:, 2, o:o + 512], start=i == 0, stop=i == 1, tile_position=(0, CAP * x))
                if half == 0:
                    combine(n, 6)
                    combine(n, 7)
            last.then_inc(s["yd_ps"], 1)

        for q in range(2):
            gather(0, q)
        for q in range(2):
            gather_T(0, q)
        with pe.Fori(0, PAIRS // 2) as it:
            for u in range(2):
                each_block(pe, it * 2 + u, lambda n, j, last: pe_block(u, n, it * 2 + u))
        n = total_blocks(pe)
        pe.wait_ge(s["ylo_ok"], num(pe, n + 1))

        def y_T(k):
            pe.wait_ge(s["y_dve" if k % 2 else "y_act"], k // 2 + 1)
            for i in range(3):
                tr(bank[2 * i + k // 4][0:TN[i], P * (k % 4):P * (k % 4) + P], yT[:, k, T0[i]:T0[i] + TN[i]], ident[:, :])

        pe.wait_ge(s["xg_ok"], num(pe, n + 1))
        pe.wait_ge(s["comb_ok"], num(pe, n + 1))
        LAG = 4
        for k in range(KC):
            combine(n, k)
            if k >= LAG:
                y_T(k - LAG)
        for k in range(KC - LAG, KC):
            y_T(k)
        pe.wait_ge(s["fin_ok"], KC)
        pe.wait_ge(s["sqsum_ok"], 2 * KC - 3)
        for i in range(3):
            last = mm(bank[6][0:TN[i], i:i + 1], sqsum2[:, T0[i]:T0[i] + TN[i]], ones[:, 0:1], start=True, stop=True)
        last.then_inc(s["ssqT_ps"], 1)

    @block.vector
    def _(dve):
        chain = [0]

        def link(ins):
            chain[0] += 1
            ins.then_inc(s["d_chain"], 1)
            dve.wait_ge(s["d_chain"], chain[0])

        def over_k(ap):
            return ap.unsqueeze(1).broadcast_to([P, KC, N])

        for k in range(KC):
            dve.wait_ge(s["xT_ps"], k + 1)
            dve.tensor_copy(xT[:, k, :], bank[k % 4][:, 0:N]).then_inc(s["xT_ok"], 1)
        dve.wait_ge(s["rstd_ok"], 1)
        link(dve.reciprocal(rstdB[:, :], rstdB[:, :]))
        dve.wait_ge(s["xT_ok"], KC)
        dve.tensor_tensor(xn[:, :, :], xT[:, :, :], over_k(rstdB[:, :]), ALU.mult).then_inc(s["xn_ok"], 1)

        def modulation(r, b):
            dve.wait_ge(s["ada_T"], r + 1)
            for g in range(2):
                last = dve.tensor_tensor(adaT[:, 2 * r:2 * r + 2, g, :].rearrange("p m (h j) -> p m h j", h=2),
                                         bank[b][:, :].rearrange("p (j m h x) -> p m h j x", j=4, m=2, h=2)[:, :, :, :, g],
                                         b_adaT[:, 2 * r:2 * r + 2, :].rearrange("p m (h j) -> p m h j", h=2), ALU.add)
                if g == 0:
                    link(last)
            last.then_inc(s["ada_ok"], 1)
            dve.wait_ge(s["ada_ok"], r + 1)

        dve.wait_ge(s["gains_in"], 64)
        modulation(0, 7)
        for g in range(2):
            dve.scalar_tensor_tensor(out=gain1[:, g, :], in0=adaT[:, 1, g, :], scalar=1.0, in1=g_mix[:, :],
                                     op0=ALU.add, op1=ALU.mult).then_inc(s["gain_ok"], 1)
        dve.wait_ge(s["gain_ok"], 2)
        dve.wait_ge(s["xn_ok"], 1)

        def split_lo(g):
            dve.wait_ge(s["whi_ok"], g + 1)
            dve.tensor_tensor(wlo[g % 2][:, :, :], half_group(g), whi[g % 2][:, :, :].bitcast(F32), ALU.subtract).then_inc(s["wlo_ok"], 1)

        for out, done in ((hhi, "hhi_dve"), (hT, "hT_dve")):
            for k in range(KC):
                dve.tensor_scalar(out[:, k, NP_:N], xn[:, k, NP_:N], gain1[:, 1, k:k + 1], adaT[:, 0, 1, k:k + 1],
                                  ALU.mult, ALU.add).then_inc(s[done], 1)
        split_lo(0)
        dve.wait_ge(s["hT_dve"], KC)
        for k in range(KC):
            dve.wait_ge(s["hhi_act"], k + 1)
            dve.wait_ge(s["hT_act"], k + 1)
            dve.tensor_tensor(hlo[:, k, :], hT[:, k, :], hhi[:, k, :].bitcast(F32), ALU.subtract).then_inc(s["hlo_ok"], 1)
        dve.memset(lf_t[:, :, :], 0.0).then_inc(s["lf_zero"], 1)
        split_lo(1)
        for c in range(0, 24, 2):
            dve.wait_ge(s["z_ps"], c + 1)
            b = bank[c % 4]
            if c < 2:
                last = dve.tensor_scalar(gqk[:, c, :], b[:, 0:N], GK ** -0.5, None, ALU.mult)
            elif c < 4:
                last = dve.tensor_copy(gqk[:, c, :], b[:, 0:N])
            elif 12 <= c < 16:
                dve.tensor_scalar(qA[0:FD, 2 * (c - 12), :], b[0:FD, 0:N], FD ** -0.5, None, ALU.mult)
                last = dve.tensor_scalar(qA[0:FD, 2 * (c - 12) + 1, :], b[FD:P, 0:N], FD ** -0.5, None, ALU.mult)
            elif 16 <= c < 20:
                dve.tensor_copy(kA[0:FD, 2 * (c - 16), :], b[0:FD, 0:N])
                dve.tensor_copy(kA[0:FD, 2 * (c - 16) + 1, :], b[FD:P, 0:N])
                last = dve.tensor_copy(zt[:, 8 + c - 16, :], b[:, 0:N])
            else:
                last = dve.tensor_copy(zt[:, c - 4 if c < 12 else c - 8, :], b[:, 0:N])
            last.then_inc(s["z_dve"], 1)
            if c // 2 + 2 < 12:
                split_lo(c // 2 + 2)
        dve.wait_ge(s["narrow_ps"], 1)
        dve.wait_ge(s["lf_zero"], 1)
        for i in range(3):
            last = dve.tensor_tensor(lf_t[0:TN[i], i, :], bank[5][0:TN[i], FH * i:FH * i + FH], b_ff[0:TN[i], :], ALU.add)
            if i == 2:
                last.then_inc(s["ff_ok"], 1)
            else:
                link(last)
        dve.wait_ge(s["ff_ok"], 1)
        link(dve.tensor_scalar(lf_m[:, :, :], lf_t[:, :, :], 0.0, None, ALU.min))
        dve.scalar_tensor_tensor(out=lf_t[:, :, :], in0=lf_m[:, :, :], scalar=-2.0, in1=lf_t[:, :, :], op0=ALU.mult,
                                 op1=ALU.add).then_inc(s["lf_abs"], 1)
        dve.wait_ge(s["gate_ps"], 1)
        for c in range(2):
            last = dve.tensor_scalar(g_t[:, c, :], bank[6 + c][:, 0:N], b_gk[:, c:c + 1], None, ALU.add)
            if c:
                last.then_inc(s["gate_x"], 1)
            else:
                link(last)
        dve.wait_ge(s["gate_x"], 1)
        link(dve.tensor_scalar(g_b[:, :, :], g_t[:, :, :], 0.0, None, ALU.min))
        dve.scalar_tensor_tensor(out=g_a[:, :, :], in0=g_b[:, :, :], scalar=-2.0, in1=g_t[:, :, :], op0=ALU.mult,
                                 op1=ALU.add).then_inc(s["gate_abs"], 1)
        dve.wait_ge(s["lf_ln"], 1)
        dve.tensor_tensor(logf[:, :, :], lf_m[:, :, :], lf_t[:, :, :], ALU.subtract).then_inc(s["logf_ok"], 1)
        for c in range(4):
            dve.wait_ge(s["cK_ps"], c + 1)
            dve.tensor_copy(kS[0:FD, 2 * c, :], bank[c][0:FD, :]).then_inc(s["cK_dve"], 1)
        dve.wait_ge(s["crow_ps"], 1)
        dve.tensor_copy(crow[:, 0, :], bank[4][0:FH, 0:N]).then_inc(s["crow_ok"], 1)
        dve.tensor_scalar(crow[:, 1, :], bank[4][0:FH, 0:N], -1.0, None, ALU.mult).then_inc(s["crow_ok"], 1)
        dve.wait_ge(s["crow_ps"], 2)
        dve.tensor_copy(srow[:, :], bank[5][0:FH, :]).then_inc(s["crow_ok"], 1)
        dve.wait_ge(s["gate_ln"], 1)
        link(dve.tensor_tensor(g_t[:, :, :], g_b[:, :, :], g_a[:, :, :], ALU.subtract))
        link(dve.tensor_scalar(g_b[:, :, :], g_t[:, :, :], 1.0 / 16.0, None, ALU.mult))
        for c in range(2):
            for b in range(5):
                t0, n = BLK * b, BLK if b < 4 else NS_
                last = dve.tensor_tensor_scan(g_t[:, c, t0:t0 + n], ones[:, 0:n], g_b[:, c, t0:t0 + n], 0.0, ALU.mult, ALU.add)
        link(last)

        def by_block(t, c):
            return t[:, c, 0:NP_].rearrange("p (b n) -> p b n", n=BLK)

        for c in range(2):
            def col(at):
                return g_t[:, c, at:NP_:BLK].unsqueeze(2).broadcast_to([P, 4, BLK])

            def scol(at):
                return g_t[:, c, at:at + 1].broadcast_to([P, NS_])
            dve.tensor_tensor(by_block(g_a, c), by_block(g_t, c), col(BLK // 2), ALU.subtract)
            dve.tensor_tensor(g_a[:, c, NP_:N], g_t[:, c, NP_:N], scol(NP_ + NS_ // 2), ALU.subtract).then_inc(s["cum_ok"], 1)
            dve.tensor_tensor(by_block(g_b, c), col(BLK - 1), by_block(g_t, c), ALU.subtract)
            dve.tensor_tensor(g_b[:, c, NP_:N], scol(N - 1), g_t[:, c, NP_:N], ALU.subtract).then_inc(s["cum_ok"], 1)
        for n, (t, z0) in enumerate(((qe, 0), (ke, 2), (qb, 0), (kl, 2))):
            dve.wait_ge(s["gexp_ok"], n + 1)
            dve.tensor_tensor(t[:, :, :], t[:, :, :], gqk[:, z0:z0 + 2, :], ALU.mult).then_inc(s["gprod_ok"], 1)
        for q in range(12):
            kind, i = q // 3, q % 3
            if kind != 1:
                dve.wait_ge(s["tok_ps"], q + 1)
                dve.tensor_copy(toks[0:TN[i], kind, i, :], bank[4 + i][0:TN[i], :]).then_inc(s["tok_dve"], 1)
        dve.wait_ge(s["klT_ps"], 1)
        link(dve.tensor_copy(kl_tok[:, 0:2, :], bank[4][:, :].rearrange("p (i n) -> p i n", i=2)))
        dve.tensor_copy(kl_tok[0:NS_, 2, :], bank[5][0:NS_, 0:256]).then_inc(s["klT_ok"], 1)
        dve.wait_ge(s["aT_ps"], 1)
        dve.wait_ge(s["zeros"], 14)
        mask = glamask[:, :].bitcast(I32)
        for q in range(2):
            dve.copy_predicated(a_t[:, q, 0:2, :, :].rearrange("p i c n -> p (i c) n"), mask.unsqueeze(1).broadcast_to([P, 4, BLK]),
                                bank[6 + q][:, 0:256].rearrange("p (g n) -> p g n", n=BLK)).then_inc(s["aT_ok"], 1)
            dve.copy_predicated(a_t[0:NS_, q, 2, :, 0:NS_], mask[0:NS_, 0:NS_].unsqueeze(1).broadcast_to([NS_, 2, NS_]),
                                bank[6 + q][0:NS_, 256:384].rearrange("p (g n) -> p g n", n=BLK)[:, :, 0:NS_]).then_inc(s["aT_ok"], 1)
        modulation(1, 3)
        dve.wait_ge(s["upd_ps"], 1)
        dve.wait_ge(s["gexp_ok"], 6)
        dve.wait_ge(s["state_in"], 32)
        for c in range(2):
            dve.tensor_copy(states[:, 0, c, :], update(0, c)).then_inc(s["state_ok"], 1)
            dve.scalar_tensor_tensor(out=states[:, 5, c, :], in0=states[:, 4, c, :], scalar=dec[:, c, 4:5], in1=update(4, c),
                                     op0=ALU.mult, op1=ALU.add).then_inc(s["state_ok"], 1)
        for b in range(1, 4):
            dve.wait_ge(s["state_ok"], 2 + 2 * b)
            for c in range(2):
                dve.scalar_tensor_tensor(out=states[:, b, c, :], in0=states[:, b - 1, c, :], scalar=dec[:, c, b:b + 1],
                                         in1=update(b, c), op0=ALU.mult, op1=ALU.add).then_inc(s["state_ok"], 1)
        for i in range(3):
            dve.wait_ge(s["go_ps"], max(i + 1, 2))
            link(dve.tensor_copy(o_tok[0:TN[i], i, 0:512], bank[3 + i][0:TN[i], :]))
            lo = BLK if i == 0 else 0
            for q in range(2):
                o = o_tok[lo:TN[i], i, 0:512].rearrange("t (c q v) -> t c q v", c=2, q=2)[:, :, q, :]
                last = dve.tensor_tensor(o, inter(i, q)[lo:TN[i], :].rearrange("t (c v) -> t c v", c=2), o, ALU.add)
            last.then_inc(s["go_ok"], 1)
        def maxima(u):
            i, n = u // 8, TN[u // 8]
            dve.wait_ge(s["sc_ps"], u + 1)
            dve.tensor_reduce(nmax[0:n, u:u + 1], score(u)[0:n, 0:NKEY[i]], AX, ALU.max, negate=True).then_inc(s["max_ok"], 1)

        maxima(0)
        for u in range(24):
            i, n = u // 8, TN[u // 8]
            if u + 1 < 24:
                maxima(u + 1)
            dve.wait_ge(s["pT_ps"], u + 1)
            if u >= 2:
                dve.wait_ge(s["po_ps"], u - 1)
            if i < 2:
                dve.tensor_copy(probT[u % 2][:, 0:n * (i + 1)], bank[u % 2][:, 0:n * (i + 1)]).then_inc(s["pT_ok"], 1)
            else:
                link(dve.tensor_copy(probT[u % 2][:, 0:4 * n], bank[u % 2][:, 0:4 * n]))
                dve.tensor_copy(probT[u % 2][0:NS_, 4 * n:5 * n], bank[u % 2][0:NS_, 4 * n:5 * n]).then_inc(s["pT_ok"], 1)
            if u == KC:
                modulation(2, 3)
            if u % 8 == 0 and u:
                divide(dve, i - 1, link)
        divide(dve, 2, link)
        dve.wait_ge(s["rs_act"], 1)
        link(dve.reciprocal(rs5[:, :, 0:4], rs5[:, :, 0:4]))
        for i in range(3):
            n = TN[i]
            for h in range(GH):
                o = o_tok[0:n, i, GV * h:GV * h + GV]
                dve.scalar_tensor_tensor(out=o, in0=o, scalar=rs5[0:n, i, h:h + 1], in1=toks[0:n, 1, i, GV * h:GV * h + GV],
                                         op0=ALU.mult, op1=ALU.mult)
        for g in range(2):
            dve.scalar_tensor_tensor(out=gain2[:, g, :], in0=adaT[:, 4, g, :], scalar=1.0, in1=g_ffn[:, :],
                                     op0=ALU.add, op1=ALU.mult).then_inc(s["gain_ok"], 1)
        dve.wait_ge(s["rs_act"], 2)
        link(dve.reciprocal(rs5[:, :, 4:5], rs5[:, :, 4:5]))
        for i in range(3):
            n = TN[i]
            dve.tensor_scalar(o_tok[0:n, i, 512:1024], o_tok[0:n, i, 512:1024], rs5[0:n, i, 4:5], None, ALU.mult).then_inc(s["on_ok"], 1)
        for j in range(1, 8, 2):
            dve.wait_ge(s["mT_ps"], j + 1)
            dve.tensor_scalar(mT[:, j, :], bank[j % 4][:, 0:N], g_gla[:, 0:1] if j < 4 else g_fox[:, j - 4:j - 3], None,
                              ALU.mult).then_inc(s["mT_dve"], 1)
        for k in range(KC):
            dve.wait_ge(s["mix_ps"], k + 1)
            dve.scalar_tensor_tensor(out=xT[:, k, 0:NP_], in0=bank[k % 4][:, 0:NP_], scalar=adaT[:, 2, 0, k:k + 1],
                                     in1=xT[:, k, 0:NP_], op0=ALU.mult, op1=ALU.add)
            dve.scalar_tensor_tensor(out=xT[:, k, NP_:N], in0=bank[k % 4][:, NP_:N], scalar=adaT[:, 2, 1, k:k + 1],
                                     in1=xT[:, k, NP_:N], op0=ALU.mult, op1=ALU.add).then_inc(s["x1_ok"], 1)
        dve.wait_ge(s["rstd_ok"], 2)
        link(dve.reciprocal(rstdB[:, :], rstdB[:, :]))
        dve.wait_ge(s["x1_ok"], KC)
        dve.wait_ge(s["gain_ok"], 4)
        for k in range(KC + 1):
            if k < KC:
                dve.tensor_tensor(h2T[:, k, :], xT[:, k, :], rstdB[:, :], ALU.mult).then_inc(s["h2n_ok"], 1)
            if k:
                dve.wait_ge(s["h2n_ok"], k)
                dve.tensor_scalar(h2T[:, k - 1, NP_:N], h2T[:, k - 1, NP_:N], gain2[:, 1, k - 1:k], adaT[:, 3, 1, k - 1:k],
                                  ALU.mult, ALU.add).then_inc(s["h2s_ok"], 1)

        def low_part(q):
            i, k = q // 2, 4 * (q % 2)
            if q == 4:
                dve.wait_ge(s["iota_ok"], 5)
            dve.wait_ge(s["h2hi_ok"], q + 1)
            low = h2hl[NS_:2 * NS_, 4, k:k + 4, :] if i == 2 else h2hl[:, 2 * i + 1, k:k + 4, :]
            dve.tensor_tensor(low, bank[4 + q % 2][0:TN[i], :].rearrange("t (k p) -> t k p", k=4),
                              h2hl[0:TN[i], 2 * i, k:k + 4, :].bitcast(F32), ALU.subtract).then_inc(s["h2lo_ok"], 1)

        def select(out, vals, width, k):
            thr = t8[:, :, k - 1:k].broadcast_to([P, 3, width])
            a, b, c = (t[:, 0:3 * width].rearrange("p (i e) -> p i e", i=3) for t in (r_a, r_b, r_c))
            dve.tensor_tensor(a, vals, thr, ALU.is_gt)
            link(dve.tensor_tensor(b, vals, thr, ALU.is_equal))
            dve.tensor_reduce(r_n[:, :], a, AX, ALU.add)
            link(dve.tensor_tensor_scan(r_c[:, 0:3 * width], restart[width][:, :], r_b[:, 0:3 * width], 0.0, ALU.mult, ALU.add))
            link(dve.tensor_tensor(c, c, r_n[:, :].unsqueeze(2).broadcast_to([P, 3, width]), ALU.add))
            link(dve.scalar_tensor_tensor(out=c, in0=c, scalar=float(k), in1=b, op0=ALU.is_le, op1=ALU.mult))
            link(dve.tensor_tensor(out, a, c, ALU.add))

        dve.wait_ge(s["rtT_ps"], 1)
        dve.wait_ge(s["rt_zeros"], 2)
        dve.tensor_copy(sc[:, 0:2, :], bank[7][:, 0:2 * E].rearrange("p (i e) -> p i e", i=2))
        link(dve.tensor_copy(sc[0:NS_, 2, :], bank[7][0:NS_, 2 * E:3 * E]))
        for q in range(2):
            low_part(q)
        link(dve.tensor_tensor(ch[:, :, :], sc[:, :, :], b_rt[:, :].unsqueeze(1).broadcast_to([P, 3, E]), ALU.add))
        for i in range(3):
            for g in range(NG):
                last = dve.max(top[:, NG * i + g, :], ch[:, i, 8 * g:8 * g + 8])
        link(last)
        link(dve.tensor_tensor(gs[:, :, :], top[:, :, 0].rearrange("p (i g) -> p i g", i=3), top[:, :, 1].rearrange("p (i g) -> p i g", i=3), ALU.add))
        for i in range(3):
            last = dve.max(t8[:, i, :], gs[:, i, :])
        link(last)
        select(gs[:, :, :], gs[:, :, :], NG, TOPG)
        link(dve.tensor_scalar(gs[:, :, :], gs[:, :, :], 1.0, -NEG, ALU.subtract, ALU.mult))
        grouped = ch[:, :, :].rearrange("p i (g m) -> p (i g) m", g=NG)
        link(dve.tensor_tensor(grouped, grouped, gs[:, :, :].rearrange("p i g -> p (i g)").unsqueeze(2).broadcast_to([P, 3 * NG, 8]), ALU.add))
        for i in range(3):
            last = dve.max(t8[:, i, :], ch[:, i, :])
        link(last)
        select(ch[:, :, :], ch[:, :, :], E, TOPK)
        link(dve.tensor_tensor(wrt[:, :, :], sc[:, :, :], ch[:, :, :], ALU.mult))
        link(dve.tensor_reduce(r_n[:, :], wrt[:, :, :], AX, ALU.add))
        link(dve.tensor_scalar(r_n[:, :], r_n[:, :], 1e-20, None, ALU.add))
        link(dve.reciprocal(r_n[:, :], r_n[:, :]))
        dve.scalar_tensor_tensor(out=wrt[:, :, :], in0=wrt[:, :, :], scalar=RSCALE, in1=r_n[:, :].unsqueeze(2).broadcast_to([P, 3, E]),
                                 op0=ALU.mult, op1=ALU.mult).then_inc(s["wrt_ok"], 1)
        for q in range(2, 6):
            if q == 4:
                for j in range(2):
                    dve.wait_ge(s["sil_ok"], j + 1)
                    dve.wait_ge(s["gu_ps"], 4)
                    dve.tensor_tensor(actT[:, j, :], bank[2 + j][:, 0:N], sil[:, j, :], ALU.mult).then_inc(s["act_ok"], 1)
            low_part(q)
        dve.wait_ge(s["iota_ok"], 5)
        dve.wait_ge(s["pos_ps"], 1)
        dve.wait_ge(s["rt_zeros"], 9)
        dve.scalar_tensor_tensor(out=key[:, 0:E], in0=bank[7][0:E, 3 * E:4 * E], scalar=float(E), in1=tie[:, 0:E], op0=ALU.mult, op1=ALU.add)
        link(dve.scalar_tensor_tensor(out=key[:, E:E + 1], in0=bank[7][0:E, 4 * E:4 * E + 1], scalar=float(E), in1=tie[:, E:E + 1],
                                      op0=ALU.mult, op1=ALU.add))
        dve.tensor_copy(c_col[:, :], bank[7][0:E, 4 * E:4 * E + 1])
        link(dve.tensor_scalar(onehot[:, :], key[:, 0:E], key[:, E:E + 1], 0.0, ALU.is_gt, ALU.add, accum_out=rank[:, :]))
        dve.tensor_scalar(onehot[:, :], rank_at[:, :], rank[:, :], None, ALU.is_equal).then_inc(s["rank_ok"], 1)
        halves = ((P, slice(0, 2)), (NS_, slice(2, 3)))
        for n, i in halves:
            last = dve.scalar_tensor_tensor(out=posm[0:n, i, 0:E], in0=bank[7][0:n, 0:3 * E].rearrange("p (i e) -> p i e", i=3)[:, i, :],
                                            scalar=1.0, in1=ch[0:n, i, :], op0=ALU.add, op1=ALU.mult)
            dve.tensor_copy(w_hl[0:n, i, 0, 0:E], wrt[0:n, i, :])
        link(last)
        for n, i in halves:
            last = dve.tensor_scalar(posm[0:n, i, 0:E], posm[0:n, i, 0:E], 1.0, None, ALU.subtract)
        link(last)
        for n, i in halves:
            dve.tensor_tensor(w_hl[0:n, i, 1, 0:E], wrt[0:n, i, :], w_hl[0:n, i, 0, 0:E].bitcast(F32), ALU.subtract)
        link(dve.tensor_copy(posm[NS_:2 * NS_, 2, 0:E], posm[0:NS_, 2, 0:E]))
        dve.wait_ge(s["order_ps"], 1)
        dve.tensor_copy(table[:, 2 * PAIRS:2 * PAIRS + E], bank[4][0:1, 0:E])
        dve.tensor_copy(table[:, 2 * PAIRS + E:], iota[0:1, E:E + 2])
        link(dve.tensor_reduce(mcount[:, :], bank[4][0:1, E:2 * E].rearrange("o (g m) -> o g m", m=2), AX, ALU.max))
        link(dve.tensor_scalar(nx[:, :], mcount[:, :], float(CAP), None, ALU.is_gt))
        for j in range(2, MAXB):
            link(dve.scalar_tensor_tensor(out=nx[:, :], in0=mcount[:, :], scalar=float(CAP * j), in1=nx[:, :], op0=ALU.is_gt, op1=ALU.add))
        link(dve.tensor_copy(table[:, 0:PAIRS], nx[:, :]))
        link(dve.tensor_tensor_scan(nxc[:, :], ones[0:1, 0:PAIRS], nx[:, :], 0.0, ALU.mult, ALU.add))
        link(dve.tensor_tensor(nxc[:, :], nxc[:, :], nx[:, :], ALU.subtract))
        dve.tensor_tensor(table[:, PAIRS:2 * PAIRS], nxc[:, :], iota[0:1, 0:PAIRS], ALU.add).then_inc(s["table_ok"], 1)
        dve.wait_ge(s["table_ok"], 1)

        def select_slots(b, at):
            for x in range(2):
                e = expert_at(dve, b * 2 + x, E + 1)
                dve.tensor_tensor(sel[:, :, x, :], iota[:, bass.ds(at, CAP)].unsqueeze(1).broadcast_to([P, 3, CAP]),
                                  posm[:, :, bass.ds(e, 1)].broadcast_to([P, 3, CAP]), ALU.is_equal)
                last = dve.tensor_copy(wp[:, :, :, x:x + 1], w_hl[:, :, :, bass.ds(e, 1)].bitcast(F32))
            last.then_inc(s["sel_ok"], 1)

        def add(n, k):
            dve.wait_ge(s["comb_ps"], num(dve, n * KC + (k + 1)))
            dve.wait_ge(s["acc_ok"], num(dve, n * KC + (k + 1)))
            dve.tensor_tensor(acc[:, k, :], bank[6 + k % 2][:, 0:N], acc[:, k, :], ALU.add).then_inc(s["acc_ok"], 1)

        def dve_block(n, b, j, last_of_pair):
            dve.wait_ge(s["slots_ps"], num(dve, n + 1))
            for x in range(2):
                last = dve.tensor_reduce(ws[CAP * x:CAP * x + CAP, :], bank[2][CAP * x:CAP * x + CAP, 3 * P + x:3 * P + 4:2], AX, ALU.add)
            last.then_inc(s["ws_ok"], 1)
            if last_of_pair:
                select_slots(b + 1, 0)
            else:
                select_slots(b, dve.snap((j + 1) * CAP))
            dve.wait_ge(s["sl_ok"], num(dve, n + 1))
            dve.wait_ge(s["ws_ok"], num(dve, n + 1))
            dve.scalar_tensor_tensor(out=hid[:, :], in0=bank[3][:, DE:2 * DE], scalar=ws[:, 0:1], in1=silg[:, :],
                                     op0=ALU.mult, op1=ALU.mult).then_inc(s["hid_ok"], 1)
            for k in range(KC):
                add(n, k)
            dve.tensor_copy(comb[:, :], bank[2][:, 0:N]).then_inc(s["comb_ok"], 1)
            dve.wait_ge(s["yhi_ok"], num(dve, n + 1))
            dve.tensor_tensor(ylo[:, :], psum[:, 4 * 512:6 * 512], yhi[:, :].bitcast(F32), ALU.subtract).then_inc(s["ylo_ok"], 1)

        select_slots(0, 0)
        dve.memset(comb[:, :].bitcast(F32), 0.0).then_inc(s["comb_ok"], 1)
        dve.memset(yhi[:, :].bitcast(F32), 0.0)
        dve.memset(ylo[:, :].bitcast(F32), 0.0).then_inc(s["ylo_ok"], 1)
        with dve.Fori(0, PAIRS // 2) as it:
            for u in range(2):
                each_block(dve, it * 2 + u, lambda n, j, last: dve_block(n, it * 2 + u, j, last))
        n = total_blocks(dve)

        def finish(k):
            dve.wait_ge(s["acc_ok"], num(dve, n * KC + (KC + k + 1)))
            dve.scalar_tensor_tensor(out=acc[:, k, 0:NP_], in0=acc[:, k, 0:NP_], scalar=adaT[:, 5, 0, k:k + 1],
                                     in1=xT[:, k, 0:NP_], op0=ALU.mult, op1=ALU.add)
            dve.scalar_tensor_tensor(out=acc[:, k, NP_:N], in0=acc[:, k, NP_:N], scalar=adaT[:, 5, 1, k:k + 1],
                                     in1=xT[:, k, NP_:N], op0=ALU.mult, op1=ALU.add).then_inc(s["fin_ok"], 1)

        def scale(k):
            if k % 2:
                dve.wait_ge(s["fin_ok"], k + 1)
                dve.tensor_scalar(yT[:, k, :], acc[:, k, :], g_fin[:, k:k + 1], None, ALU.mult).then_inc(s["y_dve"], 1)

        for k in range(KC):
            add(n, k)
            if k:
                finish(k - 1)
            if k >= 2:
                scale(k - 2)
        finish(KC - 1)
        scale(KC - 1)
        for i in range(3):
            dve.wait_ge(s["rstdT_ok"], i + 1)
            dve.reciprocal(rstdT[0:TN[i], i:i + 1], rstdT[0:TN[i], i:i + 1]).then_inc(s["rinv_ok"], 1)
        for i in range(3):
            dve.wait_ge(s["rinv_ok"], i + 1)
            dve.tensor_scalar(y_half(yout, i, 1), bank[2 * i + 1][0:TN[i], :].rearrange("t (k p) -> t k p", k=4),
                              rstdT[0:TN[i], i:i + 1], None, ALU.mult).then_inc(s["y_ok_dve"], 1)

    ctx.close()


_INS = ["x_prompt", "x_sample", "state_gla", "cache_fox_k", "cache_fox_v", "cache_fox_logf", "c_prompt", "c_sample",
        "w_ada", "b_ada", "g_norm_mix", "g_norm_ffn", "w_in", "w_gla_gk2", "b_gla_gk", "g_gla_out", "b_fox_f", "g_fox_out",
        "w_out", "w_router", "b_router", "w_exp_gate", "w_exp_up", "w_exp_down", "w_sh_gate", "w_sh_up", "w_sh_down", "g_final"]
_OUTS = [(1, NP_, D), (1, NS_, D), (1, 1, GH, GK, GV), (1, 1, GH, GK, GV), (1, 1, NP_, FH, FD), (1, 1, NP_, FH, FD),
         (1, 1, NP_, FH), (1, 1, NS_, FH, FD), (1, 1, NS_, FH, FD), (1, 1, NS_, FH)]


def kernel(**inputs):
    import numpy as _np
    import concourse.bacc as _bacc
    from concourse import mybir as _mybir
    from concourse.bass_utils import run_bass_kernel_spmd as _run

    nc = _bacc.Bacc("TRN2", target_bir_lowering=False, num_devices=1)
    arrays, args = {}, []
    for name in _INS:
        a = _np.ascontiguousarray(inputs[name])
        arrays[f"in_{name}"] = a
        args.append(nc.dram_tensor(f"in_{name}", a.shape, _mybir.dt.from_np(a.dtype), kind="ExternalInput").ap())
    for i, shape in enumerate(_OUTS):
        args.append(nc.dram_tensor(f"out_{i}", shape, F32, kind="ExternalOutput").ap())
    layer(nc, *args)
    r = _run(nc, [arrays], core_ids=[0])
    return tuple(r.results[0][f"out_{i}"] for i in range(len(_OUTS)))
```
